# Optimizing a Trainium2 kernel written in Bass

```python
import math, functools
import jax, jax.numpy as jnp
from jax import lax
import numpy as np

D_MODEL = 1024
BATCH = 1
SEQ = 256
DEPTH = 2
DEC_BATCH = 8
DEC_SEQ = 1
PAST_LEN = 256
PAGE_SIZE = 128

N_META = 16
N_EVEN = (DEPTH + 1) // 2
N_ODD = DEPTH // 2
D_SSM = D_MODEL // 2
SSM_GROUP = 16
N_SSM_GROUPS = D_SSM // SSM_GROUP
SSM_STATE = 64
N_HEADS = 8
HEAD_DIM = 64
D_ATT = N_HEADS * HEAD_DIM
N_IDX_HEADS = 8
IDX_DIM = 64
TOPK_MAX = 256
QBLOCK = 64
ROPE_THETA = 10000.0
POOL_WINDOWS = (2, 4, 8, 16)
POOL_GROUP_DIM = D_MODEL // len(POOL_WINDOWS)
POOL_HIST = max(POOL_WINDOWS) - 1
D_FF = 2816
N_EXPERTS = 8
TOP_K_EXPERTS = 2
D_FF_EXPERT = 3584
EPS = 1e-6
SPLITS = (D_SSM, D_SSM + D_ATT, D_SSM + 2 * D_ATT, D_SSM + 3 * D_ATT,
          D_SSM + 3 * D_ATT + N_IDX_HEADS * IDX_DIM,
          D_SSM + 3 * D_ATT + N_IDX_HEADS * IDX_DIM + IDX_DIM)
D_IN0 = SPLITS[-1] + N_IDX_HEADS

kernel_name = "hybrid_s5_dsa_pool_moe_step"

def rmsnorm(x, g):
    x32 = x.astype(jnp.float32)
    y = x32 * lax.rsqrt(jnp.mean(x32 * x32, axis=-1, keepdims=True) + EPS)
    return (y * g.astype(jnp.float32)).astype(x.dtype)

def rope(x, pos):
    half = x.shape[-1] // 2
    inv = ROPE_THETA ** (-jnp.arange(half, dtype=jnp.float32) / half)
    ang = pos[:, None] * inv[None, :]
    cos = jnp.cos(ang)[None, :, None, :]
    sin = jnp.sin(ang)[None, :, None, :]
    x32 = x.astype(jnp.float32)
    x1, x2 = x32[..., :half], x32[..., half:]
    return jnp.concatenate([x1 * cos - x2 * sin, x2 * cos + x1 * sin], axis=-1).astype(x.dtype)

def gather_rows(rows, idx):
    return jax.vmap(lambda r, i: r[i])(rows, idx)

def swiglu(h, w_gate, w_up, w_down):
    return (jax.nn.silu(h @ w_gate) * (h @ w_up)) @ w_down

def mixer_inputs(h, w_in, q_norm, k_norm, pos):
    B, L, _ = h.shape
    z = h @ w_in
    u, q, k, v, qi, ki, wi = jnp.split(z, SPLITS, axis=-1)
    q = rope(rmsnorm(q.reshape(B, L, N_HEADS, HEAD_DIM), q_norm), pos)
    k = rope(rmsnorm(k.reshape(B, L, N_HEADS, HEAD_DIM), k_norm), pos)
    v = v.reshape(B, L, N_HEADS, HEAD_DIM)
    qi = rope(qi.reshape(B, L, N_IDX_HEADS, IDX_DIM), pos)
    ki = rope(ki[:, :, None, :], pos)[:, :, 0]
    return u, q, k, v, qi, ki, wi

def index_scores(qi, ki, wi):
    dots = jnp.einsum('bqhd,bsd->bqhs', qi, ki, preferred_element_type=jnp.float32) * (IDX_DIM ** -0.5)
    w = wi.astype(jnp.float32) * (N_IDX_HEADS ** -0.5)
    return jnp.einsum('bqh,bqhs->bqs', w, jax.nn.relu(dots))

def sparse_attend(q, kg, vg, valid):
    logits = jnp.einsum('bqhd,bqkhd->bhqk', q, kg, preferred_element_type=jnp.float32) * (HEAD_DIM ** -0.5)
    logits = jnp.where(valid[:, None], logits, -jnp.inf)
    p = jax.nn.softmax(logits, axis=-1)
    out = jnp.einsum('bhqk,bqkhd->bqhd', p.astype(vg.dtype), vg, preferred_element_type=jnp.float32)
    return out.astype(q.dtype)

def dsa_prompt(q, k, v, qi, ki, wi, topk):
    B, L = q.shape[:2]
    nblk = -(-L // QBLOCK)
    Lp = nblk * QBLOCK

    def blocks(a):
        a = jnp.pad(a, [(0, 0), (0, Lp - L)] + [(0, 0)] * (a.ndim - 2))
        return a.reshape((B, nblk, QBLOCK) + a.shape[2:]).swapaxes(0, 1)

    qpos = jnp.arange(Lp, dtype=jnp.int32).reshape(nblk, QBLOCK)
    kpos = jnp.arange(L, dtype=jnp.int32)

    def one_block(args):
        qb, qib, wib, pb = args
        s = index_scores(qib, ki, wib)
        s = jnp.where(kpos[None, None, :] <= pb[None, :, None], s, -jnp.inf)
        _, idx = lax.top_k(s, topk)
        valid = idx <= pb[None, :, None]
        return sparse_attend(qb, gather_rows(k, idx), gather_rows(v, idx), valid)

    out = lax.map(one_block, (blocks(q), blocks(qi), blocks(wi), qpos))
    return out.swapaxes(0, 1).reshape(B, Lp, N_HEADS, HEAD_DIM)[:, :L]

def dsa_sample(q, k, v, qi, ki, wi, cache_k, cache_v, cache_kidx, page_table, topk):
    DB, S = q.shape[:2]
    page_size = cache_k.shape[1]
    past = page_table.shape[1] * page_size
    ki_past = cache_kidx[page_table].reshape(DB, past, IDX_DIM)
    ki_all = jnp.concatenate([ki_past.astype(ki.dtype), ki], axis=1)
    s = index_scores(qi, ki_all, wi)
    qpos = past + jnp.arange(S, dtype=jnp.int32)
    kpos = jnp.arange(past + S, dtype=jnp.int32)
    s = jnp.where(kpos[None, None, :] <= qpos[None, :, None], s, -jnp.inf)
    _, idx = lax.top_k(s, topk)
    valid = idx <= qpos[None, :, None]
    in_past = (idx < past)[..., None, None]
    jp = jnp.minimum(idx, past - 1)
    row = gather_rows(page_table, jp // page_size) * page_size + jp % page_size
    jn = jnp.clip(idx - past, 0, S - 1)
    flat_k = cache_k.reshape(-1, N_HEADS, HEAD_DIM)
    flat_v = cache_v.reshape(-1, N_HEADS, HEAD_DIM)
    kg = jnp.where(in_past, flat_k[row].astype(k.dtype), gather_rows(k, jn))
    vg = jnp.where(in_past, flat_v[row].astype(v.dtype), gather_rows(v, jn))
    return sparse_attend(q, kg, vg, valid)

def s5_mixer(u, h0_re, h0_im, lam_re, lam_im, log_dt, b_re, b_im, c_re, c_im, d_skip, w_glu):
    f32 = jnp.float32
    B, L, _ = u.shape
    ug = u.astype(f32).reshape(B, L, N_SSM_GROUPS, SSM_GROUP)
    lam = lax.complex(lam_re.astype(f32), lam_im.astype(f32))
    dt = jnp.exp(log_dt.astype(f32))[:, None]
    lam_bar = jnp.exp(lam * dt)
    b_bar = ((lam_bar - 1.0) / lam)[..., None] * lax.complex(b_re.astype(f32), b_im.astype(f32))
    bu = jnp.einsum('blgc,gpc->blgp', ug.astype(jnp.complex64), b_bar)
    a = jnp.broadcast_to(lam_bar, bu.shape)

    def combine(e1, e2):
        a1, b1 = e1
        a2, b2 = e2
        return a1 * a2, a2 * b1 + b2

    a_cum, h = lax.associative_scan(combine, (a, bu), axis=1)
    h = h + a_cum * lax.complex(h0_re.astype(f32), h0_im.astype(f32))[:, None]
    c_mat = lax.complex(c_re.astype(f32), c_im.astype(f32))
    y = jnp.real(jnp.einsum('blgp,gcp->blgc', h, c_mat)) + d_skip.astype(f32).reshape(N_SSM_GROUPS, SSM_GROUP) * ug
    y = jax.nn.gelu(y.reshape(B, L, D_SSM))
    y = y * jax.nn.sigmoid(y @ w_glu.astype(f32))
    h_last = h[:, -1]
    return y.astype(u.dtype), jnp.real(h_last), jnp.imag(h_last)

def pool_mixer(u, hist, pos0, pool_w, pool_scale):
    f32 = jnp.float32
    B, S, _ = u.shape
    n_hist = hist.shape[1]
    ext = jnp.concatenate([hist.astype(u.dtype), u], axis=1)
    T = ext.shape[1]
    ext32 = ext.astype(f32)
    c = jnp.cumsum(ext32, axis=1)
    pos = pos0 + jnp.arange(S, dtype=f32)
    pooled = []
    for g, w in enumerate(POOL_WINDOWS):
        sl = slice(g * POOL_GROUP_DIM, (g + 1) * POOL_GROUP_DIM)
        cg = c[..., sl]
        lagged = jnp.pad(cg, ((0, 0), (w, 0), (0, 0)))[:, :T]
        mean = (cg - lagged)[:, n_hist:] / jnp.minimum(float(w), pos + 1.0)[None, :, None]
        pooled.append(mean - ext32[:, n_hist:, sl])
    pooled = jnp.stack(pooled, axis=2)
    mixed = jnp.einsum('bsgc,gcd->bsgd', pooled, pool_w.astype(f32)).reshape(B, S, D_MODEL)
    return (mixed * pool_scale.astype(f32)).astype(u.dtype), ext[:, T - POOL_HIST:]

def moe(h, router_w, w_gate, w_up, w_down):
    B, S, D = h.shape
    t = h.reshape(B * S, D)
    logits = (t @ router_w).astype(jnp.float32)
    top_v, top_i = lax.top_k(logits, TOP_K_EXPERTS)
    gates = jax.nn.softmax(top_v, axis=-1)
    dense_gate = jnp.sum(jax.nn.one_hot(top_i, N_EXPERTS, dtype=jnp.float32) * gates[..., None], axis=1)
    out = jnp.zeros((B * S, D), jnp.float32)
    for e in range(N_EXPERTS):
        out = out + dense_gate[:, e:e + 1] * swiglu(t, w_gate[e], w_up[e], w_down[e]).astype(jnp.float32)
    return out.astype(h.dtype).reshape(B, S, D)

def even_layer(x, pos, h0_re, h0_im, attend, norm_mix, w_in, q_norm, k_norm, lam_re, lam_im, log_dt,
               b_re, b_im, c_re, c_im, d_skip, w_glu, w_out, norm_ffn, w_gate, w_up, w_down):
    B, L, _ = x.shape
    h = rmsnorm(x, norm_mix)
    u, q, k, v, qi, ki, wi = mixer_inputs(h, w_in, q_norm, k_norm, pos)
    y_ssm, h_re, h_im = s5_mixer(u, h0_re, h0_im, lam_re, lam_im, log_dt, b_re, b_im, c_re, c_im, d_skip, w_glu)
    y_att = attend(q, k, v, qi, ki, wi)
    x = x + jnp.concatenate([y_ssm, y_att.reshape(B, L, D_ATT)], axis=-1) @ w_out
    x = x + swiglu(rmsnorm(x, norm_ffn), w_gate, w_up, w_down)
    return x, k, v, ki, h_re, h_im

def odd_layer(x, hist, pos0, norm_mix, pool_w, pool_scale, norm_ffn, router_w, w_gate, w_up, w_down):
    y, new_hist = pool_mixer(rmsnorm(x, norm_mix), hist, pos0, pool_w, pool_scale)
    x = x + y
    x = x + moe(rmsnorm(x, norm_ffn), router_w, w_gate, w_up, w_down)
    return x, new_hist

def setup_inputs(seed: int = 0) -> dict:
    key = jax.random.key(seed)
    ks = iter(jax.random.split(key, 48))
    f32 = jnp.float32

    def nrm(shape, scale=1.0):
        return jax.random.normal(next(ks), shape, f32) * scale

    n_pages = PAST_LEN // PAGE_SIZE
    n_used = DEC_BATCH * n_pages
    n_pool = (n_used * 5) // 4
    x_prompt = nrm((BATCH, SEQ, D_MODEL))
    x_sample = nrm((DEC_BATCH, DEC_SEQ, D_MODEL))
    cache_k = nrm((N_EVEN, n_pool, PAGE_SIZE, N_HEADS, HEAD_DIM))
    cache_v = nrm((N_EVEN, n_pool, PAGE_SIZE, N_HEADS, HEAD_DIM))
    cache_kidx = nrm((N_EVEN, n_pool, PAGE_SIZE, IDX_DIM))
    page_table = jax.random.permutation(next(ks), n_pool)[:n_used].reshape(DEC_BATCH, n_pages).astype(jnp.int32)
    state_ssm_re = nrm((N_EVEN, DEC_BATCH, N_SSM_GROUPS, SSM_STATE), 0.1)
    state_ssm_im = nrm((N_EVEN, DEC_BATCH, N_SSM_GROUPS, SSM_STATE), 0.1)
    state_pool = nrm((N_ODD, DEC_BATCH, POOL_HIST, D_MODEL))
    meta_tokens = nrm((N_META, D_MODEL))
    norm_mix0 = 1.0 + nrm((N_EVEN, D_MODEL), 0.02)
    w_in0 = nrm((N_EVEN, D_MODEL, D_IN0), D_MODEL ** -0.5)
    q_norm = 1.0 + nrm((N_EVEN, HEAD_DIM), 0.02)
    k_norm = 1.0 + nrm((N_EVEN, HEAD_DIM), 0.02)
    ssm_lambda_re = -0.5 + nrm((N_EVEN, N_SSM_GROUPS, SSM_STATE), 0.01)
    ssm_lambda_im = math.pi * jnp.arange(SSM_STATE, dtype=f32) + nrm((N_EVEN, N_SSM_GROUPS, SSM_STATE), 0.01)
    ssm_log_dt = jax.random.uniform(next(ks), (N_EVEN, N_SSM_GROUPS), f32, math.log(0.001), math.log(0.1))
    ssm_b_re = nrm((N_EVEN, N_SSM_GROUPS, SSM_STATE, SSM_GROUP), (2 * SSM_GROUP) ** -0.5)
    ssm_b_im = nrm((N_EVEN, N_SSM_GROUPS, SSM_STATE, SSM_GROUP), (2 * SSM_GROUP) ** -0.5)
    ssm_c_re = nrm((N_EVEN, N_SSM_GROUPS, SSM_GROUP, SSM_STATE), SSM_STATE ** -0.5)
    ssm_c_im = nrm((N_EVEN, N_SSM_GROUPS, SSM_GROUP, SSM_STATE), SSM_STATE ** -0.5)
    ssm_d = nrm((N_EVEN, D_SSM))
    ssm_w_glu = nrm((N_EVEN, D_SSM, D_SSM), D_SSM ** -0.5)
    w_out0 = nrm((N_EVEN, D_SSM + D_ATT, D_MODEL), (D_SSM + D_ATT) ** -0.5)
    norm_ffn0 = 1.0 + nrm((N_EVEN, D_MODEL), 0.02)
    ffn_w_gate = nrm((N_EVEN, D_MODEL, D_FF), D_MODEL ** -0.5)
    ffn_w_up = nrm((N_EVEN, D_MODEL, D_FF), D_MODEL ** -0.5)
    ffn_w_down = nrm((N_EVEN, D_FF, D_MODEL), D_FF ** -0.5)
    norm_mix1 = 1.0 + nrm((N_ODD, D_MODEL), 0.02)
    pool_w = nrm((N_ODD, len(POOL_WINDOWS), POOL_GROUP_DIM, POOL_GROUP_DIM), POOL_GROUP_DIM ** -0.5)
    pool_scale = 1.0 + nrm((N_ODD, D_MODEL), 0.02)
    norm_ffn1 = 1.0 + nrm((N_ODD, D_MODEL), 0.02)
    router_w = nrm((N_ODD, D_MODEL, N_EXPERTS), D_MODEL ** -0.5)
    moe_w_gate = nrm((N_ODD, N_EXPERTS, D_MODEL, D_FF_EXPERT), D_MODEL ** -0.5)
    moe_w_up = nrm((N_ODD, N_EXPERTS, D_MODEL, D_FF_EXPERT), D_MODEL ** -0.5)
    moe_w_down = nrm((N_ODD, N_EXPERTS, D_FF_EXPERT, D_MODEL), D_FF_EXPERT ** -0.5)
    return {"x_prompt": x_prompt, "x_sample": x_sample, "cache_k": cache_k, "cache_v": cache_v,
            "cache_kidx": cache_kidx, "page_table": page_table, "state_ssm_re": state_ssm_re,
            "state_ssm_im": state_ssm_im, "state_pool": state_pool, "meta_tokens": meta_tokens,
            "norm_mix0": norm_mix0, "w_in0": w_in0, "q_norm": q_norm, "k_norm": k_norm,
            "ssm_lambda_re": ssm_lambda_re, "ssm_lambda_im": ssm_lambda_im, "ssm_log_dt": ssm_log_dt,
            "ssm_b_re": ssm_b_re, "ssm_b_im": ssm_b_im, "ssm_c_re": ssm_c_re, "ssm_c_im": ssm_c_im,
            "ssm_d": ssm_d, "ssm_w_glu": ssm_w_glu, "w_out0": w_out0, "norm_ffn0": norm_ffn0,
            "ffn_w_gate": ffn_w_gate, "ffn_w_up": ffn_w_up, "ffn_w_down": ffn_w_down,
            "norm_mix1": norm_mix1, "pool_w": pool_w, "pool_scale": pool_scale, "norm_ffn1": norm_ffn1,
            "router_w": router_w, "moe_w_gate": moe_w_gate, "moe_w_up": moe_w_up, "moe_w_down": moe_w_down}

def reference(x_prompt, x_sample, cache_k, cache_v, cache_kidx, page_table, state_ssm_re, state_ssm_im,
              state_pool, meta_tokens, norm_mix0, w_in0, q_norm, k_norm, ssm_lambda_re, ssm_lambda_im,
              ssm_log_dt, ssm_b_re, ssm_b_im, ssm_c_re, ssm_c_im, ssm_d, ssm_w_glu, w_out0, norm_ffn0,
              ffn_w_gate, ffn_w_up, ffn_w_down, norm_mix1, pool_w, pool_scale, norm_ffn1, router_w,
              moe_w_gate, moe_w_up, moe_w_down):
    f32 = jnp.float32
    B = x_prompt.shape[0]
    S = x_sample.shape[1]
    past_len = page_table.shape[1] * cache_k.shape[2]
    meta = jnp.broadcast_to(meta_tokens.astype(x_prompt.dtype)[None], (B, N_META, D_MODEL))
    x_p = jnp.concatenate([meta, x_prompt], axis=1)
    x_s = x_sample
    L = x_p.shape[1]
    pos_p = jnp.arange(L, dtype=f32)
    pos_s = past_len + jnp.arange(S, dtype=f32)
    topk_p = min(TOPK_MAX, x_prompt.shape[1] // 4)
    topk_s = min(TOPK_MAX, (past_len + S) // 4)
    zero_h = jnp.zeros((B, N_SSM_GROUPS, SSM_STATE), f32)
    no_hist = jnp.zeros((B, 0, D_MODEL), x_p.dtype)
    attend_p = functools.partial(dsa_prompt, topk=topk_p)

    k_p, v_p, ki_p, hre_p, him_p, pool_p = [], [], [], [], [], []
    k_s, v_s, ki_s, hre_s, him_s, pool_s = [], [], [], [], [], []
    for layer in range(DEPTH):
        i = layer // 2
        if layer % 2 == 0:
            params = (norm_mix0[i], w_in0[i], q_norm[i], k_norm[i], ssm_lambda_re[i], ssm_lambda_im[i],
                      ssm_log_dt[i], ssm_b_re[i], ssm_b_im[i], ssm_c_re[i], ssm_c_im[i], ssm_d[i],
                      ssm_w_glu[i], w_out0[i], norm_ffn0[i], ffn_w_gate[i], ffn_w_up[i], ffn_w_down[i])
            attend_s = functools.partial(dsa_sample, cache_k=cache_k[i], cache_v=cache_v[i],
                                         cache_kidx=cache_kidx[i], page_table=page_table, topk=topk_s)
            x_p, kk, vv, kki, hre, him = even_layer(x_p, pos_p, zero_h, zero_h, attend_p, *params)
            k_p.append(kk); v_p.append(vv); ki_p.append(kki); hre_p.append(hre); him_p.append(him)
            x_s, kk, vv, kki, hre, him = even_layer(x_s, pos_s, state_ssm_re[i], state_ssm_im[i], attend_s, *params)
            k_s.append(kk); v_s.append(vv); ki_s.append(kki); hre_s.append(hre); him_s.append(him)
        else:
            params = (norm_mix1[i], pool_w[i], pool_scale[i], norm_ffn1[i], router_w[i],
                      moe_w_gate[i], moe_w_up[i], moe_w_down[i])
            x_p, hist = odd_layer(x_p, no_hist, 0, *params)
            pool_p.append(hist)
            x_s, hist = odd_layer(x_s, state_pool[i], past_len, *params)
            pool_s.append(hist)

    y_prompt = x_p[:, N_META:]
    y_sample = x_s
    k_prompt = jnp.stack(k_p); v_prompt = jnp.stack(v_p); kidx_prompt = jnp.stack(ki_p)
    ssm_re_prompt = jnp.stack(hre_p); ssm_im_prompt = jnp.stack(him_p); pool_prompt = jnp.stack(pool_p)
    k_sample = jnp.stack(k_s); v_sample = jnp.stack(v_s); kidx_sample = jnp.stack(ki_s)
    ssm_re_sample = jnp.stack(hre_s); ssm_im_sample = jnp.stack(him_s); pool_sample = jnp.stack(pool_s)
    return (y_prompt, y_sample, k_prompt, v_prompt, kidx_prompt, ssm_re_prompt, ssm_im_prompt, pool_prompt,
            k_sample, v_sample, kidx_sample, ssm_re_sample, ssm_im_sample, pool_sample)


_drawn_inputs = setup_inputs


def setup_inputs(seed=0):
    import zlib

    import numpy as np

    out = dict(_drawn_inputs(seed))
    spreads = {}
    factors = {'q_norm': 8.0,
     'k_norm': 2.8,
     'ssm_lambda_re': 17.553,
     'norm_ffn0': 3.618,
     'norm_mix1': 2.769,
     'pool_scale': 8.0,
     'norm_ffn1': 8.0}
    for name, (base, spread) in spreads.items():
        noise = np.random.default_rng([zlib.crc32(name.encode()), seed]).standard_normal(out[name].shape)
        drawn = base * np.exp(spread * noise) if base else spread * noise
        out[name] = __import__('jax').numpy.asarray(drawn.astype(out[name].dtype))
    for name, factor in factors.items():
        out[name] = (out[name] * factor).astype(out[name].dtype)
    return out
```

```python
import math
from contextlib import ExitStack

import numpy as np
import concourse.bass as bass
from concourse import mybir

F32 = mybir.dt.float32
I32 = mybir.dt.int32
U32 = mybir.dt.uint32
ALU = mybir.AluOpType
ACT = mybir.ActivationFunctionType
AX = mybir.AxisListType

P = 128
D = 1024
C = D // P
NP_ = 272
NB = 8
T = NP_ + NB
TC = 3
TCN = [128, 128, 24]
QN = [128, 128, 16]
KN = [128, 256, 272]
H = 8
HD = 64
PAST = 256
SK = PAST + 1
NJ = 16
FF = 2816
FT = FF // P
FE = 3584
NE = 8
FC = FE // 512
EPS = 1e-6
NEG = -1e30
TAKEN = -3e38
TOPK = 64
RING = 7
SLOT = 4096
MAGIC = 12582912.0
WINDOWS = (2, 4, 8, 16)
GELU_C = math.sqrt(2.0 / math.pi)

CONST_COLS = [("ident", 128), ("ones", 128), ("tri", 128), ("iota", 128), ("cos", 96), ("sin", 96),
              ("init", 816), ("rsel", 64), ("m24", 24), ("d8", 64), ("rw", 64), ("valid", 4),
              ("ecol", 16)]
PARAM_COLS = [("g_mix0", C), ("g_ffn0", C), ("g_mix1", C), ("g_ffn1", C), ("pool_scale", C),
              ("d_skip", 4), ("lam_re", NJ), ("lam_im", NJ), ("log_dt", NJ), ("qg", HD), ("kg", HD),
              ("router", C * NE), ("h0r", NJ * NB), ("h0i", NJ * NB), ("b", 4 * 2 * 128),
              ("c", NJ * 2 * 32)]


def offsets(cols):
    at, out = 0, {}
    for name, n in cols:
        out[name] = (at, n)
        at += n
    return out, at


CONST_AT, CONST_N = offsets(CONST_COLS)
PARAM_AT, PARAM_N = offsets(PARAM_COLS)


def shape_constants():
    c = np.zeros((P, CONST_N), np.float32)

    def put(name):
        a, n = CONST_AT[name]
        return c[:, a:a + n]

    p = np.arange(P)
    put("ident")[:] = np.eye(P)
    put("ones")[:] = 1.0
    put("tri")[:] = (p[:, None] <= p[None, :])
    put("iota")[:] = p[None, :]
    inv = (np.float32(10000.0) ** (-np.arange(32, dtype=np.float32) / np.float32(32))).astype(np.float32)
    for tc in range(TC):
        t = tc * P + p
        pos = np.where(t < NP_, t, np.where(t < T, PAST, 0)).astype(np.float32)
        ang = (pos[:, None] * inv[None, :]).astype(np.float32)
        put("cos")[:, tc * 32:tc * 32 + 32] = np.cos(ang)
        put("sin")[:, tc * 32:tc * 32 + 32] = np.sin(ang)
        init = np.where(np.arange(NP_)[None, :] <= t[:, None], 0.0, NEG)
        if tc == 2:
            init[32:40] = np.where(np.arange(NP_)[None, :] < SK, 0.0, NEG)
        put("init")[:, tc * NP_:(tc + 1) * NP_] = init
        put("valid")[:, tc] = t < T
    for b in range(NB):
        put("rsel")[32 + b, b * H:(b + 1) * H] = 1.0
        put("m24")[b * H:(b + 1) * H, 16 + b] = 1.0
        put("d8")[:, b * NB + b] = 1.0
    for g, w in enumerate(WINDOWS):
        put("rw")[:, g * 16:g * 16 + w - 1] = 1.0 / np.arange(1, w, dtype=np.float32)
    put("ecol")[:] = np.tile(np.arange(NE), 2)[None, :]
    return c


MIXER_UNITS = ["u", "qi", "kw", "q", "k", "v", "glu", "wout0", "wout1"]
DENSE_UNITS = [f"ffn{i}" for i in range(FT // 2)] + [f"down{i}" for i in range(C)] + ["pool"]
UNITS = MIXER_UNITS + DENSE_UNITS
UNIT_NO = {name: n for n, name in enumerate(UNITS)}
MIXER_SLOTS = 3
MOE_UNITS = 3 * FC


def slot_of(n):
    return n % MIXER_SLOTS if n < len(MIXER_UNITS) else (n - len(MIXER_UNITS)) % RING


def slot_count(n):
    return sum(16 * (2 if UNITS[m].startswith("ffn") else 1)
               for m in range(n + 1) if slot_of(m) == slot_of(n))


def slot_before(n):
    earlier = [m for m in range(n) if slot_of(m) == slot_of(n)]
    return earlier[-1] if earlier else None


def last_fill(unit):
    if unit in ("qi", "q", "k", "v"):
        return (unit, TC - 1)
    if unit in ("u", "glu"):
        return (unit, 3)
    if unit.startswith("wout"):
        return ("wout", 4 * int(unit[4:]) + 3)
    if unit.startswith("ffn"):
        return ("up", 2 * int(unit[3:]) + 1)
    if unit.startswith("down"):
        return ("down", int(unit[4:]))
    return ("pool", C - 1) if unit == "pool" else unit


BANKS = 7


def fill_order():
    f = ["norm0"] + [("u", c) for c in range(4)]
    proj = [("qi", t) for t in range(TC)] + ["kw"] + [(n, t) for n in ("q", "k", "v") for t in range(TC)]
    j = 0
    for i, name in enumerate(proj):
        f.append(name)
        while j < NJ and j < (i + 1) * NJ / len(proj):
            f += [("bur", j), ("bui", j)]
            j += 1
    f += [("qiT", t) for t in range(TC)] + ["kiT", "wT"]
    for b in range(NB):
        f += [("skT", b), ("sdot", b)]
    f += [("dot", t, h) for t in range(TC) for h in range(H)]
    f += [("kT", t) for t in range(TC)] + [("qT", t) for t in range(TC)]
    f += [("y", c) for c in range(4)] + [("glu", c) for c in range(4)]
    for t in range(TC):
        f += [("logit", t, h) for h in range(H)]
        f += [("pT", t, i) for i in range(PT_FILLS[t])]
        f += [("att", t), ("attT", t)]
    for b in range(NB):
        f += [("cT", b, 0), ("cT", b, 1)]
    f += ["spT", "sself", "satt"]
    f += [("wout", c) for c in range(C)] + ["norm1"]
    for i in range(FT):
        f += [("gate", i), ("up", i)]
    f += [("down", c) for c in range(C)] + ["norm2", ("pnew", 0), ("pnew", 1)]
    f += [("pool", c) for c in range(C)] + ["norm3"]
    f += [("h2n", t, i) for t in range(TC) for i in range(2)]
    f += [("xn", t, i) for t in range(TC) for i in range(2)]
    f += ["router", "rank"]
    return f


def prob_blocks(t, i):
    heads = H // PT_FILLS[t]
    return [(h, kc) for h in range(heads * i, heads * (i + 1)) for kc in range(t + 1)]


PT_FILLS = [2, 4, 1]
FILLS = fill_order()
FILL_NO = {name: n for n, name in enumerate(FILLS)}
SAMPLE_BANK = 7


def bank_of(name):
    return SAMPLE_BANK if name in ("sscore", "slogit") else FILL_NO[name] % BANKS


def bank_uses(name):
    if name in ("sscore", "slogit"):
        return 1 if name == "sscore" else 2
    return FILL_NO[name] // BANKS + 1


PASS_FILLS = [[("gate", j) for j in range(0, FC, 2)], [("up", j) for j in range(0, FC, 2)],
              [("gate", j) for j in range(1, FC, 2)], [("up", j) for j in range(1, FC, 2)],
              [("gather", 1)] + [("hT", j) for j in range(FC)] + [("scatter", k) for k in (1, 3, 5)],
              [("y", 0)], [("y", 1)],
              [("gather", 0), "pickT"] + [("scatter", k) for k in (0, 2, 4)]]
PASS_BANK = {name: b for b, names in enumerate(PASS_FILLS) for name in names}
PASS_FILL_AT = {name: k for names in PASS_FILLS for k, name in enumerate(names)}
FIRST_FILL = [sum(bank_of(n) == b for n in FILLS) for b in range(BANKS)] + [2]
PASSES_EXTRA = 4
PASSES = NE + PASSES_EXTRA

PASS_UNITS = []
for _j in range(FC):
    PASS_UNITS += [("gate", _j), ("up", _j)] + ([("down", _j - 1)] if _j else [])
PASS_UNITS += [("down", FC - 1)]
PASS_UNIT_AT = {name: m for m, name in enumerate(PASS_UNITS)}


def hybrid_step(nc, a, o):
    with ExitStack() as ctx:
        sems = {}

        def sem(name):
            if name not in sems:
                sems[name] = ctx.enter_context(nc.semaphore(name))
            return sems[name]

        def sb(name, n, dt=F32):
            return ctx.enter_context(nc.sbuf_tensor(name, [P, n], dt))

        consts, params = sb("consts", CONST_N), sb("params", PARAM_N)
        xT, hT = sb("xT", C * T), sb("hT", C * T)
        ring = sb("ring", RING * SLOT)
        M2 = 14100
        low = sb("low", M2)
        small = sb("small", 1300)
        small_i = sb("small_i", 64, I32)
        bank = [ctx.enter_context(nc.psum_tensor(f"bank{b}", [P, 512], F32)) for b in range(8)]
        bank_full = [sem(f"bank{b}_full") for b in range(8)]
        bank_free = [sem(f"bank{b}_free") for b in range(8)]
        slot_full = [sem(f"slot{s}_full") for s in range(RING)]

        def const(name):
            at, n = CONST_AT[name]
            return consts[:, at:at + n]

        def param(name):
            at, n = PARAM_AT[name]
            return params[:, at:at + n]

        def carve(tensor, start):
            at = [start]

            def take(n):
                v = tensor[:, at[0]:at[0] + n]
                at[0] += n
                return v
            return take, at

        x3 = xT[:, :].rearrange("p (c t) -> p c t", c=C)
        h3 = hT[:, :].rearrange("p (c t) -> p c t", c=C)
        ycat = h3
        ident, ones, iota = const("ident"), const("ones"), const("iota")
        cos3 = const("cos").rearrange("p (t d) -> p t d", t=TC)
        sin3 = const("sin").rearrange("p (t d) -> p t d", t=TC)
        init3 = const("init").rearrange("p (t k) -> p t k", t=TC)
        b_m = param("b").rearrange("p (j r s) -> p j r s", j=4, r=2)
        c_m = param("c").rearrange("p (j r s) -> p j r s", j=NJ, r=2)

        tk, _ = carve(small, 0)
        eps, nmax, rsum, rinv, mx8 = tk(1), tk(TC * H), tk(TC * H), tk(TC * H), tk(TC * 8)
        mx = tk(TC * H)
        qss, kss = tk(TC * H), tk(TC * H)
        smx, snm, srs, sri = tk(1), tk(1), tk(1), tk(1)
        dself = tk(24)
        wT = tk(24)
        wbd = tk(64)
        hs = tk(NJ * 2 * NB).rearrange("p (j r b) -> p j r b", j=NJ, r=2)
        raw = tk(NJ * 2 * NB).rearrange("p (j r b) -> p j r b", j=NJ, r=2)
        hlast = tk(2 * NJ)
        cur = tk(6)
        rt = [tk(24) for _ in range(8)]
        f16 = [tk(NJ) for _ in range(14)]

        tk, at = carve(low, 0)
        zqi, zq = tk(TC * 512), tk(TC * 512)
        zk, zv, zkid, zwi = tk(TC * 512), tk(TC * 512), tk(TC * 128), tk(TC * 8)
        cf = tk(NJ * 64)
        csn = tk(NJ * 32)
        qT, kT, qiT = tk(4 * T), tk(4 * T), tk(4 * T)
        qbd = tk(4 * NB * 64)
        sprob = tk(SK)
        tail = tk(2 * 128 + 64)
        psT, psd = tail[:, 0:128], tail[:, 128:192]
        assert at[0] <= M2, at
        etmp = low[:, at[0] - 320 - SK - 2048 - 12 * T:at[0] - 320 - SK - 2048 - 12 * T + 4096]
        rtmp = low[:, at[0] - 320 - SK - 2048:at[0]]
        ga, gb = rtmp[:, 0:4 * T], rtmp[:, 4 * T:8 * T]
        kcT = low[:, 0:2 * 4 * SK].rearrange("p (r c k) -> p r c k", r=2, c=4)
        assert 2 * 4 * SK <= 2 * TC * 512

        m1 = MIXER_SLOTS * SLOT
        tk, at = carve(ring, m1)
        er, ei = tk(NJ * NP_), tk(NJ * NP_)
        er3, ei3 = er.rearrange("p (j t) -> p j t", j=NJ), ei.rearrange("p (j t) -> p j t", j=NJ)
        vr, vi, d1, d2, d3, d4 = [tk(NP_) for _ in range(6)]
        g4 = tk(4 * NP_).rearrange("p (r k t) -> p r k t", r=2, k=2)
        pt = [tk(NP_) for _ in range(4)]
        kin = tk(2 * 2 * 128).rearrange("p (r g d) -> p r g d", r=2, g=2)
        m1_dead = at[0]
        uT = tk(4 * T).rearrange("p (c t) -> p c t", c=4)
        sc = tk(TC * NP_).rearrange("p (t k) -> p t k", t=TC)
        relu = tk(2 * NP_).rearrange("p (r k) -> p r k", r=2)
        kiT = tk(T)
        kisT = tk(2 * SK).rearrange("p (r k) -> p r k", r=2)
        qibd = tk(NB * 8)
        assert at[0] <= RING * SLOT, at
        tk, at = carve(ring, m1)
        lg = [tk(H * KN[t]).rearrange("p (h k) -> p h k", h=H) for t in range(TC)]
        pT = [tk(1024), tk(2048), tk(384)]
        kb = tk(2 * 1024).rearrange("p (r g d) -> p r g d", r=2, g=2)
        vb = tk(2 * 1024).rearrange("p (r g d) -> p r g d", r=2, g=2)
        assert at[0] <= m1_dead, at
        def rb(b):
            return relu[:, b % 2, 0:SK]

        yn = relu.rearrange("p r k -> p (r k)")[:, 0:512]

        hff = low[:, 0:FT * T].rearrange("p (f t) -> p f t", f=FT)
        sq = low[:, FT * T:FT * T + C * T].rearrange("p (c t) -> p c t", c=C)
        std = low[:, FT * T + C * T:FT * T + C * T + T]
        rs = low[:, FT * T + C * T + T:FT * T + C * T + 2 * T]
        ffa = low[:, FT * T + C * T + 2 * T:FT * T + C * T + 6 * T].rearrange("p (r t) -> p r t", r=4)
        tk, at = carve(low, 0)
        win_a = tk(C * NP_).rearrange("p (c t) -> p c t", c=C)
        win_b = tk(C * NP_).rearrange("p (c t) -> p c t", c=C)
        assert at[0] <= FT * T
        tk, at = carve(low, FT * T + C * T + 6 * T)
        pl = tk(C * T).rearrange("p (c t) -> p c t", c=C)
        hist = tk(C * NB * 15).rearrange("p (c b r) -> p c b r", c=C, b=NB)
        assert at[0] <= M2, at
        ext = low[:, 2 * C * NP_:2 * C * NP_ + C * NB * 16].rearrange("p (c b r) -> p c b r", c=C, b=NB)
        pnew = low[:, FT * T + C * T + 2 * T:FT * T + C * T + 2 * T + D]
        assert 2 * C * NP_ + C * NB * 16 <= FT * T and D <= 4 * T
        tk, at = carve(low, 0)
        hn = tk(TC * D).rearrange("p (t d) -> p t d", t=TC)
        acc = tk(TC * D).rearrange("p (t d) -> p t d", t=TC)
        assert at[0] <= FT * T
        tk, at = carve(low, FT * T)
        xg = tk(C * P).rearrange("p (c s) -> p c s", c=C)
        pick = tk(TC * P).rearrange("p (t s) -> p t s", t=TC)
        pickT = tk(T)
        th = tk(2 * 512).rearrange("p (r k) -> p r k", r=2)
        hb = tk(2 * 512).rearrange("p (r k) -> p r k", r=2)
        hbT = tk(2 * 512).rearrange("p (r f s) -> p r f s", r=2, f=4)
        yb = tk(D)
        sel, gate, slot_v, rk = [tk(TC * NE).rearrange("p (t e) -> p t e", t=TC) for _ in range(4)]
        pslot = tk(PASSES * TC).rearrange("p (i t) -> p i t", i=PASSES)
        pgate = tk(PASSES * TC).rearrange("p (i t) -> p i t", i=PASSES)
        pexp = tk(PASSES)
        cand = tk(TC * 16).rearrange("p (t b e) -> p t b e", t=TC, b=2)
        gcand = tk(TC * 16).rearrange("p (t b e) -> p t b e", t=TC, b=2)
        over, ranko = tk(16), tk(16)
        oh = tk(4 * 16).rearrange("p (k e) -> p k e", k=4)
        prod = tk(TC * 4 * 16).rearrange("p (t k e) -> p t k e", t=TC, k=4)
        idxf = tk(TC * 8).rearrange("p (t e) -> p t e", t=TC)
        oh1, oh2 = [tk(TC * NE).rearrange("p (t e) -> p t e", t=TC) for _ in range(2)]
        lgt = tk(TC * NE).rearrange("p (t e) -> p t e", t=TC)
        m8r = tk(TC * 8).rearrange("p (t e) -> p t e", t=TC)
        g12 = tk(4 * TC).rearrange("p (k t) -> p k t", k=4)
        assert at[0] <= M2, at
        exp_i, idx_u = small_i[:, 0:PASSES + 1], small_i[:, 16:40].bitcast(U32)
        pages, expo = small_i[:, 48:64], sb("expo", NJ, I32)

        def filled(eng, name):
            eng.wait_ge(bank_full[bank_of(name)], bank_uses(name))

        def emptied(eng, name):
            eng.wait_ge(bank_free[bank_of(name)], bank_uses(name))

        def pass_filled(eng, name, i):
            b = PASS_BANK[name]
            eng.wait_ge(bank_full[b], FIRST_FILL[b] + len(PASS_FILLS[b]) * i + PASS_FILL_AT[name] + 1)

        def pass_emptied(eng, name, i):
            b = PASS_BANK[name]
            eng.wait_ge(bank_free[b], FIRST_FILL[b] + len(PASS_FILLS[b]) * i + PASS_FILL_AT[name] + 1)

        def full(name):
            return bank_full[bank_of(name)]

        def free(name):
            return bank_free[bank_of(name)]

        def ps(name):
            return bank[bank_of(name)]

        def view(slot, width):
            return ring[:, slot * SLOT:slot * SLOT + (SLOT // width) * width].rearrange(
                "p (c n) -> p c n", n=width)

        def unit(name, width):
            return view(slot_of(UNIT_NO[name]), width)


        z4 = {n: v.rearrange("p (t h d) -> p t h d", t=TC, h=H)
              for n, v in (("q", zq), ("k", zk), ("v", zv), ("qi", zqi))}
        z3 = {n: v.rearrange("p (t n) -> p t n", t=TC)
              for n, v in (("q", zq), ("k", zk), ("v", zv), ("qi", zqi), ("kid", zkid), ("wi", zwi))}
        qT3, kT3, qiT3 = [v.rearrange("p (c t) -> p c t", c=4) for v in (qT, kT, qiT)]
        qbd4 = qbd.rearrange("p (c b m) -> p c b m", c=4, b=NB)
        qib3 = qibd.rearrange("p (b h) -> p b h", b=NB)
        cf4 = cf.rearrange("p (j r s) -> p j r s", j=NJ, r=2)
        csn3 = csn.rearrange("p (j s) -> p j s", j=NJ)
        lam_r, lam_i = param("lam_re"), param("lam_im")
        dt_, rad, rate, lbr, lbi, fr_, fi_, s1, s2, s3, sn, cn, ang, cang = f16

        slot_base = [slot_count(max(n for n in range(len(UNITS)) if slot_of(n) == s)) for s in range(RING)]

        block = ctx.enter_context(nc.Block())

        @block.sync
        def _(sp):
            def to_slot(n, dst, src):
                sp.dma_start(dst, src).then_inc(slot_full[slot_of(n)], 16)

            def load_unit(n):
                name = UNITS[n]
                if slot_before(n) is not None:
                    filled(sp, last_fill(UNITS[slot_before(n)]))
                elif n >= len(MIXER_UNITS):
                    sp.wait_ge(sem("mixer_over"), 1)
                w_in = a["w_in"].rearrange("(c p) n -> p c n", p=P)
                cols = {"u": 0, "q": 512, "k": 1024, "v": 1536, "qi": 2048}
                if name in cols:
                    to_slot(n, unit(name, 512)[:, 0:C, :], w_in[:, :, cols[name]:cols[name] + 512])
                elif name == "kw":
                    to_slot(n, unit(name, 72)[:, 0:C, :], w_in[:, :, 2560:2632])
                elif name == "glu":
                    to_slot(n, unit(name, 512)[:, 0:4, :], a["w_glu"].rearrange("(c p) n -> p c n", p=P))
                elif name.startswith("wout"):
                    at = int(name[4:]) * 512
                    to_slot(n, unit(name, 512)[:, 0:C, :],
                            a["w_out"].rearrange("(c p) n -> p c n", p=P)[:, :, at:at + 512])
                elif name.startswith("ffn"):
                    at = int(name[3:]) * 256
                    for k, w in enumerate(("w_gate", "w_up")):
                        sp.dma_start(unit(name, 256)[:, k * C:(k + 1) * C, :],
                                     a[w].rearrange("(c p) n -> p c n", p=P)[:, :, at:at + 256]
                                     ).then_inc(slot_full[slot_of(n)], 16)
                elif name.startswith("down"):
                    at = int(name[4:]) * P
                    to_slot(n, unit(name, P)[:, 0:FT, :],
                            a["w_down"].rearrange("(f p) n -> p f n", p=P)[:, :, at:at + P])
                else:
                    to_slot(n, unit(name, 256)[:, 0:C, :], a["pool_w"].rearrange("(c p) n -> p c n", p=P))

            for n in range(len(MIXER_UNITS)):
                load_unit(n)
                if n == 0:
                    sp.dma_start(pages[0:1, :], a["page_table"]).then_inc(sem("pages_in"), 16)

            sp.wait_ge(sem("pages_in"), 16)
            for b in range(NB):
                if b >= 2:
                    filled(sp, ("skT", b - 2))
                for g in range(2):
                    page = sp.value_load(pages[0:1, 2 * b + g:2 * b + g + 1], min_val=0, max_val=a["n_pool"] - 1)
                    for half in range(2):
                        sp.dma_start(kin[:, b % 2, g, half * HD:half * HD + HD],
                                     a["cache_kidx"][bass.ds(page, 1), :, :].rearrange("o t d -> (o t) d")
                                     ).then_inc(sem(f"kidx_in{b % 2}"), 16)

            def load_pages(b, cache, dst, what):
                for g in range(2):
                    page = sp.value_load(pages[0:1, 2 * b + g:2 * b + g + 1], min_val=0, max_val=a["n_pool"] - 1)
                    sp.dma_start(dst[:, b % 2, g, :],
                                 a[cache][bass.ds(page, 1), :, :].rearrange("o t d -> (o t) d")
                                 ).then_inc(sem(f"{what}_in{b % 2}"), 16)

            filled(sp, ("y", 3))
            for b in range(NB):
                if b >= 2:
                    filled(sp, ("cT", b - 2, 1))
                load_pages(b, "cache_k", kb, "ck")
                if b < 2:
                    load_pages(b, "cache_v", vb, "cv")
            for b in range(2, NB):
                sp.wait_ge(sem("values_used"), b - 1)
                load_pages(b, "cache_v", vb, "cv")

            for n in range(len(MIXER_UNITS), len(UNITS)):
                load_unit(n)

            def expert_unit(e, i, m, wait_at, wait_m):
                kind, j = PASS_UNITS[m]
                s = (len(UNITS) + m - len(MIXER_UNITS)) % RING
                if kind == "down":
                    src = a["moe_down"][e, j * 512:(j + 1) * 512, :].rearrange("o (f p) n -> p (o f) n", p=P)
                    dst = view(s, 1024)
                else:
                    src = a["moe_" + kind][e, :, j * 512:(j + 1) * 512].rearrange("o (c p) n -> p (o c) n", p=P)
                    dst = view(s, 512)
                if wait_at is None:
                    filled(sp, last_fill(UNITS[len(UNITS) - RING + m]))
                else:
                    kind, j = PASS_UNITS[wait_m]
                    if (kind, j) == ("down", FC - 1):
                        pass_filled(sp, ("y", 1), wait_at)
                    elif kind == "down":
                        sp.wait_ge(sem("down_used"), wait_at * (FC - 1) + j + 1)
                    else:
                        pass_filled(sp, (kind, j), wait_at)
                sp.dma_start(dst, src).then_inc(slot_full[s], 16)

            def first_units(e, i, wait_at):
                for m in range(RING):
                    expert_unit(e, i, m, wait_at, m + 2 * RING)

            def other_units(e, i):
                for m in range(RING, 3 * RING):
                    expert_unit(e, i, m, i, m - RING)

            first_units(slice(0, 1), 0, None)
            with sp.Fori(0, NE - 1) as i:
                other_units(bass.ds(i, 1), i)
                first_units(bass.ds(i + 1, 1), i + 1, i)
            other_units(slice(NE - 1, NE), NE - 1)
            sp.wait_ge(sem("passes_ready"), 1)
            n_pass = sp.value_load(exp_i[0:1, PASSES:PASSES + 1], min_val=NE, max_val=PASSES)
            with sp.If(n_pass > NE):
                with sp.Fori(NE, n_pass) as i:
                    e = sp.value_load(exp_i[0:1, bass.ds(i, 1)], min_val=0, max_val=NE - 1)
                    first_units(bass.ds(e, 1), i, i - 1)
                    other_units(bass.ds(e, 1), i)

            for k in (2 * TC - 2, 2 * TC - 1):
                b = PASS_BANK[("scatter", k)]
                sp.wait_ge(bank_free[b], len(PASS_FILLS[b]) * n_pass + (FIRST_FILL[b] - len(PASS_FILLS[b]) + PASS_FILL_AT[("scatter", k)] + 1))
            for t in range(TC):
                sp.dma_start(o["y"][t * P:t * P + TCN[t], :], acc[0:TCN[t], t, :]).then_inc(sem("out"), 16)
            sp.wait_ge(sem("out"), 16 * TC)
            sp.wait_ge(sem("kv_out"), 16 * 2 * TC)
            sp.wait_ge(sem("ki_out"), 16 * TC)
            sp.wait_ge(sem("state_out"), 16 * 2)
            sp.wait_ge(sem("pool_out"), 16 * 2)
            sp.wait_ge(sem("pool_old_out"), 16)

        @block.gpsimd
        def _(pool):
            done = [0]

            def link(ins):
                done[0] += 1
                ins.then_inc(sem("pool_step"), 1)
                pool.wait_ge(sem("pool_step"), done[0])

            TT = nc.gpsimd.tensor_tensor
            nc.gpsimd.memset(eps, EPS)
            for v in ("q", "k", "v", "qi"):
                last = nc.gpsimd.memset(z3[v][:, 2, :], 0.0)
            nc.gpsimd.memset(qibd, 0.0).then_inc(sem("zeroed"), 1)
            filled(pool, "norm0")
            nc.gpsimd.memset(z3["kid"][:, 2, :], 0.0)
            nc.gpsimd.memset(z3["wi"][:, 2, :], 0.0).then_inc(sem("zeroed"), 1)
            pool.dma_start(o["pool_s"][:, 0:14, :], a["state_pool"][:, 1:15, :]).then_inc(sem("pool_old_out"), 16)
            for j in range(NJ):
                pool.wait_ge(sem("scanned"), j + 1)
                gr, gi = g4[:, j % 2, 0, :], g4[:, j % 2, 1, :]
                TT(pt[0], er3[:, j, :], gr, ALU.mult)
                TT(pt[1], ei3[:, j, :], gi, ALU.mult)
                TT(pt[2], er3[:, j, :], gi, ALU.mult)
                link(TT(pt[3], ei3[:, j, :], gr, ALU.mult))
                TT(er3[:, j, :], pt[0], pt[1], ALU.subtract)
                TT(ei3[:, j, :], pt[2], pt[3], ALU.add).then_inc(sem("states"), 1)
                pool.wait_ge(sem("states"), j + 1)
            pool.wait_ge(sem("kid_ready"), 1)
            for t in range(TC):
                pool.dma_start(o["kidx"][t * P:t * P + TCN[t], :], z3["kid"][0:TCN[t], t, 0:HD]).then_inc(sem("ki_out"), 16)
            pool.wait_ge(sem("qk_ready"), 2)
            for t in range(TC):
                for n in ("k", "v"):
                    if n == "v":
                        emptied(pool, ("v", t))
                    pool.dma_start(o[n][t * P:t * P + TCN[t], :], z3[n][0:TCN[t], t, :]).then_inc(sem("kv_out"), 16)
            pool.wait_ge(sem("sample_state"), 1)
            pool.dma_start(o["hs"], hs.rearrange("p j r b -> p (j r b)")).then_inc(sem("state_out"), 16)
            pool.wait_ge(sem("last_state"), 1)
            pool.dma_start(o["hl"], hlast).then_inc(sem("state_out"), 16)
            pool.wait_ge(sem("mixer_over"), 1)
            emptied(pool, "satt")
            pool.dma_start(hist.rearrange("p c b r -> p (c b r)"), a["hist"]).then_inc(sem("hist_in"), 16)

        @block.tensor
        def _(pe):
            mm = nc.tensor.matmul

            def open_fill(name):
                if bank_uses(name) > 1:
                    pe.wait_ge(bank_free[bank_of(name)], bank_uses(name) - 1)
                return ps(name)

            def unit_there(name):
                n = UNIT_NO[name]
                pe.wait_ge(slot_full[slot_of(n)], slot_count(n))

            def norm_sums(k):
                out = open_fill(f"norm{k}")
                for c in range(C):
                    pe.wait_ge(sem("squares"), C * k + c + 1)
                    last = mm(out[:, 0:T], ones, sq[:, c, :], start=(c == 0), stop=(c == C - 1))
                last.then_inc(full(f"norm{k}"), 1)

            def blocks_T(name, src, n, count, step=P):
                out = open_fill(name)
                for i in range(count):
                    last = nc.tensor.transpose(out[0:step, i * P:i * P + n], src[0:n, i * step:(i + 1) * step],
                                               ident[0:n, 0:n])
                last.then_inc(full(name), 1)

            pe.wait_ge(sem("consts_in"), 16)
            norm_sums(0)
            unit_there("u")
            w = unit("u", 512)
            for co in range(4):
                out = open_fill(("u", co))
                for c in range(C):
                    if co == 0:
                        pe.wait_ge(sem("normed"), c + 1)
                    last = mm(out[:, 0:T], w[:, c, co * P:(co + 1) * P], h3[:, c, :], start=(c == 0), stop=(c == C - 1))
                last.then_inc(full(("u", co)), 1)

            def project(name, width, t, out):
                w = unit(name, width)
                for c in range(C):
                    last = mm(out[0:TCN[t], 0:width], h3[:, c, t * P:t * P + TCN[t]], w[:, c, :],
                              start=(c == 0), stop=(c == C - 1))
                return last

            def state_inputs(j):
                emptied(pe, ("u", j // 4))
                rows = slice(32 * (j % 4), 32 * (j % 4) + 32)
                for r, name in enumerate((("bur", j), ("bui", j))):
                    out = open_fill(name)
                    mm(out[:, 0:T], b_m[rows, j // 4, r, :], uT[rows, j // 4, :],
                       start=True, stop=True).then_inc(full(name), 1)

            for name in FILLS[FILL_NO[("qi", 0)]:FILL_NO[("qiT", 0)]]:
                if name == "kw":
                    unit_there("kw")
                    out = open_fill(name)
                    for t in range(TC):
                        last = project("kw", 72, t, out[:, 72 * t:72 * t + 72])
                    last.then_inc(full(name), 1)
                elif name[0] == "bur":
                    state_inputs(name[1])
                elif name[0] != "bui":
                    unit_there(name[0])
                    project(name[0], 512, name[1], open_fill(name)).then_inc(full(name), 1)

            pe.wait_ge(sem("qi_ready"), 1)
            for t in range(TC):
                blocks_T(("qiT", t), z3["qi"][:, t, :], TCN[t], 4)
            pe.wait_ge(sem("kid_ready"), 1)
            out = open_fill("kiT")
            for t in range(TC):
                last = nc.tensor.transpose(out[:, t * P:t * P + TCN[t]], z3["kid"][0:TCN[t], t, :],
                                           ident[0:TCN[t], 0:TCN[t]])
            last.then_inc(full("kiT"), 1)
            blocks_T("wT", z3["wi"][:, 2, :], TCN[2], 1, H)

            def add_sample_scores(b):
                emptied(pe, ("sdot", b))
                last = mm(ps("sscore")[32:40, 0:SK], wbd[0:H, b * NB:(b + 1) * NB], rb(b)[0:H, :],
                          start=(b == 0), stop=(b == NB - 1))
                last.then_inc(full("sscore") if b == NB - 1 else sem("sample_scored"), 1)

            for b in range(NB):
                pe.wait_ge(sem(f"kidx_in{b % 2}"), 64 * (b // 2 + 1))
                blocks_T(("skT", b), kin[:, b % 2, :, :].rearrange("p g d -> p (g d)"), P, 2)
                if b == 0:
                    pe.wait_ge(sem("sample_index_q"), 1)
                else:
                    add_sample_scores(b - 1)
                emptied(pe, ("skT", b))
                out = open_fill(("sdot", b))
                mm(out[0:H, 0:SK], qib3[:, b, :], kisT[:, b % 2, :], start=True, stop=True).then_inc(full(("sdot", b)), 1)
            add_sample_scores(NB - 1)

            emptied(pe, "kiT")
            for t in range(TC):
                emptied(pe, ("qiT", t))
                for h in range(H):
                    half = slice(HD * (h % 2), HD * (h % 2) + HD)
                    out = open_fill(("dot", t, h))
                    mm(out[0:QN[t], 0:KN[t]], qiT3[half, h // 2, t * P:t * P + QN[t]], kiT[half, 0:KN[t]],
                       start=True, stop=True).then_inc(full(("dot", t, h)), 1)

            pe.wait_ge(sem("qk_ready"), 2)
            for t in range(TC):
                blocks_T(("kT", t), z3["k"][:, t, :], TCN[t], 4)
            for t in range(TC):
                blocks_T(("qT", t), z3["q"][:, t, :], TCN[t], 4)

            pe.wait_ge(sem("out_mats"), 1)
            pe.wait_ge(sem("sample_state"), 1)
            for jc in range(4):
                out = open_fill(("y", jc))
                pe.wait_ge(sem("states"), 4 * jc + 4)
                for q in range(4):
                    j, rows = 4 * jc + q, slice(32 * q, 32 * q + 32)
                    mm(out[rows, 0:NP_], cf4[:, j, 0, :], er3[:, j, :], start=True, stop=False)
                    mm(out[rows, 0:NP_], cf4[:, j, 1, :], ei3[:, j, :], start=False, stop=True)
                    mm(out[rows, NP_:T], c_m[:, j, 0, :], hs[:, j, 0, :], start=True, stop=False)
                    last = mm(out[rows, NP_:T], csn3[:, j, :], hs[:, j, 1, :], start=False, stop=True)
                last.then_inc(full(("y", jc)), 1)
            unit_there("glu")
            w = unit("glu", 512)
            pe.wait_ge(sem("gelu"), 1)
            for co in range(4):
                out = open_fill(("glu", co))
                for c in range(4):
                    last = mm(out[:, 0:T], w[:, c, co * P:(co + 1) * P], uT[:, c, :], start=(c == 0), stop=(c == 3))
                last.then_inc(full(("glu", co)), 1)

            for t in range(TC):
                emptied(pe, ("kT", t))
            for t in range(TC):
                nq = QN[t]
                emptied(pe, ("qT", t))
                for h in range(H):
                    half = slice(HD * (h % 2), HD * (h % 2) + HD)
                    out = open_fill(("logit", t, h))
                    mm(out[0:nq, 0:KN[t]], qT3[half, h // 2, t * P:t * P + nq], kT3[half, h // 2, 0:KN[t]],
                       start=True, stop=True).then_inc(full(("logit", t, h)), 1)
                heads = H // PT_FILLS[t]
                for i in range(PT_FILLS[t]):
                    out = open_fill(("pT", t, i))
                    pe.wait_ge(sem("probs"), H * t + heads * (i + 1))
                    for n, (h, kc) in enumerate(prob_blocks(t, i)):
                        kn = min(P, KN[t] - kc * P)
                        last = nc.tensor.transpose(out[0:kn, n * nq:(n + 1) * nq], lg[t][0:nq, h, kc * P:kc * P + kn],
                                                   ident[0:nq, 0:nq])
                    last.then_inc(full(("pT", t, i)), 1)
                out = open_fill(("att", t))
                for i in range(PT_FILLS[t]):
                    emptied(pe, ("pT", t, i))
                for h in range(H):
                    for kc in range(t + 1):
                        kn, n = min(P, KN[t] - kc * P), h * (t + 1) + kc
                        last = mm(out[0:nq, h * HD:(h + 1) * HD], pT[t][0:kn, n * nq:(n + 1) * nq],
                                  z3["v"][0:kn, kc, h * HD:(h + 1) * HD], start=(kc == 0), stop=(kc == t))
                last.then_inc(full(("att", t)), 1)
                emptied(pe, ("att", t))
                blocks_T(("attT", t), yn, nq, 4)

            pe.wait_ge(sem("sample_q"), 1)
            emptied(pe, "sscore")
            slog = ps("slogit")
            for b in range(NB):
                pe.wait_ge(sem(f"ck_in{b % 2}"), 32 * (b // 2 + 1))
                for g in range(2):
                    blocks_T(("cT", b, g), kb[:, b % 2, g, :], P, 4)
                emptied(pe, ("cT", b, 1))
                emptied(pe, ("cT", b, 0))
                for c in range(4):
                    last = mm(slog[0:64, 0:SK], qbd4[:, c, b, :], kcT[:, b % 2, c, :], start=(b == 0 and c == 0), stop=False)
                last.then_inc(sem("sample_logits"), 1)
            mm(slog[0:64, 0:SK], const("rsel")[32:40, :], sc[32:40, 2, 0:SK], start=False, stop=True).then_inc(full("slogit"), 1)
            pe.wait_ge(sem("sample_probs"), 1)
            out = open_fill("spT")
            for g in range(2):
                last = nc.tensor.transpose(out[:, g * 64:(g + 1) * 64], sprob[0:64, g * P:(g + 1) * P], ident[0:64, 0:64])
            last.then_inc(full("spT"), 1)
            out = open_fill("sself")
            nc.tensor.transpose(out[0:24, 0:64], dself[0:64, :], ident[0:64, 0:64]).then_inc(full("sself"), 1)
            emptied(pe, "spT")
            emptied(pe, "sself")
            out = open_fill("satt")
            for b in range(NB):
                pe.wait_ge(sem(f"cv_in{b % 2}"), 32 * (b // 2 + 1))
                for c in range(4):
                    cols = slice(b * H + 2 * c, b * H + 2 * c + 2)
                    for g in range(2):
                        last = mm(out[:, cols], vb[:, b % 2, g, c * P:(c + 1) * P],
                                  psT[:, g * 64 + b * H + 2 * c:g * 64 + b * H + 2 * c + 2], start=(g == 0), stop=False)
                    last = mm(out[:, cols], z3["v"][0:24, 2, c * P:(c + 1) * P], psd[0:24, cols], start=False, stop=True)
                last.then_inc(full("satt") if b == NB - 1 else sem("values_used"), 1)

            for co in range(C):
                if co % 4 == 0:
                    unit_there(f"wout{co // 4}")
                w = unit(f"wout{co // 4}", 512)
                out = open_fill(("wout", co))
                if co == 0:
                    pe.wait_ge(sem("ssm_out"), 1)
                    for t in range(TC):
                        emptied(pe, ("attT", t))
                    emptied(pe, "satt")
                for c in range(C):
                    last = mm(out[:, 0:T], w[:, c, (co % 4) * P:(co % 4) * P + P], ycat[:, c, :],
                              start=(c == 0), stop=(c == C - 1))
                    if co == 0 and c == 0:
                        last.then_inc(sem("mixer_over"), 1)
                last.then_inc(full(("wout", co)), 1)

            norm_sums(1)
            for f in range(FT):
                name = f"ffn{f // 2}"
                if f % 2 == 0:
                    unit_there(name)
                w = unit(name, 256)
                for k, kind in enumerate(("gate", "up")):
                    out = open_fill((kind, f))
                    for c in range(C):
                        if f == 0:
                            pe.wait_ge(sem("normed"), C + c + 1)
                        last = mm(out[:, 0:T], w[:, k * C + c, (f % 2) * P:(f % 2) * P + P], h3[:, c, :],
                                  start=(c == 0), stop=(c == C - 1))
                    last.then_inc(full((kind, f)), 1)
            for co in range(C):
                unit_there(f"down{co}")
                w = unit(f"down{co}", P)
                out = open_fill(("down", co))
                for f in range(FT):
                    if co == 0:
                        emptied(pe, ("up", f))
                    last = mm(out[:, 0:T], w[:, f, :], hff[:, f, :], start=(f == 0), stop=(f == FT - 1))
                last.then_inc(full(("down", co)), 1)

            norm_sums(2)
            pe.wait_ge(sem("normed"), 3 * C)
            for i in range(2):
                out = open_fill(("pnew", i))
                for q in range(4):
                    last = nc.tensor.transpose(out[0:23, q * P:(q + 1) * P], h3[:, 4 * i + q, T - 23:T], ident)
                last.then_inc(full(("pnew", i)), 1)
            unit_there("pool")
            w = unit("pool", 256)
            for co in range(C):
                g = co // 2
                out = open_fill(("pool", co))
                pe.wait_ge(sem("pooled"), g + 1)
                for c in (2 * g, 2 * g + 1):
                    last = mm(out[:, 0:T], w[:, c, (co % 2) * P:(co % 2) * P + P], pl[:, c, :],
                              start=(c == 2 * g), stop=(c == 2 * g + 1))
                last.then_inc(full(("pool", co)), 1)

            norm_sums(3)
            pe.wait_ge(sem("normed"), 4 * C)
            for kind, src in (("h2n", h3), ("xn", x3)):
                for t in range(TC):
                    for i in range(2):
                        out = open_fill((kind, t, i))
                        for q in range(4):
                            last = nc.tensor.transpose(out[0:TCN[t], q * P:(q + 1) * P],
                                                       src[:, 4 * i + q, t * P:t * P + TCN[t]], ident)
                        last.then_inc(full((kind, t, i)), 1)
            rw = param("router").rearrange("p (c e) -> p c e", c=C)
            out = open_fill("router")
            for t in range(TC):
                for c in range(C):
                    last = mm(out[0:TCN[t], t * NE:(t + 1) * NE], h3[:, c, t * P:t * P + TCN[t]], rw[:, c, :],
                              start=(c == 0), stop=(c == C - 1))
            last.then_inc(full("router"), 1)
            out = open_fill("rank")
            pe.wait_ge(sem("picked"), 1)
            for t in range(TC + 1):
                for u in range(min(t + 1, TC)):
                    last = mm(out[:, t * NE:(t + 1) * NE], const("tri") if u == t else ones, sel[:, u, :],
                              start=(u == 0), stop=(u == min(t, TC - 1)))
            last.then_inc(full("rank"), 1)

            pe.wait_ge(sem("passes_ready"), 1)
            for i in range(2):
                emptied(pe, ("xn", 2, i))
            n_pass = pe.value_load(exp_i[0:1, PASSES:PASSES + 1], min_val=NE, max_val=PASSES)
            with pe.Fori(0, n_pass) as i:
                def open_pass(name):
                    b = PASS_BANK[name]
                    pe.wait_ge(bank_free[b], FIRST_FILL[b] + len(PASS_FILLS[b]) * i + PASS_FILL_AT[name])
                    return bank[b]

                def pfull(name):
                    return bank_full[PASS_BANK[name]]

                def punit(kind, j, width):
                    m = PASS_UNIT_AT[(kind, j)]
                    s = (len(UNITS) + m - len(MIXER_UNITS)) % RING
                    pe.wait_ge(slot_full[s], slot_base[s] + 48 * i + 16 * (m // RING + 1))
                    return view(s, width)

                def down(j):
                    w = punit("down", j, 1024)
                    pass_emptied(pe, ("hT", j), i)
                    for f in range(4):
                        for half in range(2):
                            out = open_pass(("y", half)) if j == 0 and f == 0 else bank[PASS_BANK[("y", half)]]
                            last = mm(out[:, :], hbT[:, j % 2, f, :], w[:, f, half * 512:(half + 1) * 512],
                                      start=(j == 0 and f == 0), stop=(j == FC - 1 and f == 3))
                            if j == FC - 1 and f == 3:
                                last.then_inc(pfull(("y", half)), 1)
                    if j < FC - 1:
                        last.then_inc(sem("down_used"), 1)

                for half in range(2):
                    out = open_pass(("gather", half))
                    if half == 0:
                        pe.wait_ge(sem("pick_ready"), i + 1)
                    for q in range(4):
                        for t in range(TC):
                            n = TCN[t]
                            last = mm(out[:, q * P:(q + 1) * P], hn[0:n, t, (4 * half + q) * P:(4 * half + q + 1) * P],
                                      pick[0:n, t, :], start=(t == 0), stop=(t == TC - 1))
                    last.then_inc(pfull(("gather", half)), 1)
                for half in range(2):
                    pass_emptied(pe, ("gather", half), i)
                for j in range(FC):
                    for kind in ("gate", "up"):
                        w = punit(kind, j, 512)
                        out = open_pass((kind, j))
                        for c in range(C):
                            last = mm(out[:, :], xg[:, c, :], w[:, c, :], start=(c == 0), stop=(c == C - 1))
                        last.then_inc(pfull((kind, j)), 1)
                        if kind == "gate" and j > 0:
                            out = open_pass(("hT", j - 1))
                            pass_emptied(pe, ("up", j - 1), i)
                            for f in range(4):
                                last = nc.tensor.transpose(out[:, f * P:(f + 1) * P], hb[:, (j - 1) % 2, f * P:(f + 1) * P], ident)
                            last.then_inc(pfull(("hT", j - 1)), 1)
                    if j == 0:
                        out = open_pass("pickT")
                        for t in range(TC):
                            last = nc.tensor.transpose(out[:, t * P:t * P + TCN[t]], pick[0:TCN[t], t, :],
                                                       ident[0:TCN[t], 0:TCN[t]])
                        last.then_inc(pfull("pickT"), 1)
                    else:
                        down(j - 1)
                out = open_pass(("hT", FC - 1))
                pass_emptied(pe, ("up", FC - 1), i)
                for f in range(4):
                    last = nc.tensor.transpose(out[:, f * P:(f + 1) * P], hb[:, (FC - 1) % 2, f * P:(f + 1) * P], ident)
                last.then_inc(pfull(("hT", FC - 1)), 1)
                down(FC - 1)
                pass_emptied(pe, "pickT", i)
                for half in range(2):
                    pass_emptied(pe, ("y", half), i)
                for k in range(2 * TC):
                    t, half = k // 2, k % 2
                    out = open_pass(("scatter", k))
                    mm(out[0:TCN[t], :], pickT[:, t * P:t * P + TCN[t]], yb[:, half * 512:(half + 1) * 512],
                       start=True, stop=True).then_inc(pfull(("scatter", k)), 1)

        @block.scalar
        def _(act):
            A = nc.scalar.activation

            act.dma_start(xT[:, :], a["x"]).then_inc(sem("x_in"), 16)
            act.dma_start(consts[:, :], a["consts"]).then_inc(sem("consts_in"), 16)
            act.dma_start(params[:, :], a["params"]).then_inc(sem("params_in"), 16)

            def squares(k, ready):
                for c in range(C):
                    ready(c)
                    A(sq[:, c, :], x3[:, c, :], ACT.Square).then_inc(sem("squares"), 1)

            def root(k):
                filled(act, f"norm{k}")
                A(std, ps(f"norm{k}")[:, 0:T], ACT.Sqrt, bias=eps, scale=1.0 / D).then_inc(free(f"norm{k}"), 1)

            def copy_out(name, dst, src=None, n=512, inc=True, scale=1.0):
                ins = A(dst, ps(name)[:, 0:n] if src is None else src, ACT.Copy, scale=scale)
                if inc:
                    ins.then_inc(free(name), 1)

            act.wait_ge(sem("x_in"), 16)
            act.wait_ge(sem("zeroed"), 1)
            squares(0, lambda c: None)
            root(0)
            act.wait_ge(sem("angles"), 1)
            A(sn, ang, ACT.Sin)
            A(cn, cang, ACT.Sin).then_inc(sem("sincos"), 1)
            for c in range(4):
                filled(act, ("u", c))
                copy_out(("u", c), uT[:, c, :], n=T)
            for name in FILLS[FILL_NO[("qi", 0)]:FILL_NO[("qiT", 0)]]:
                if name == "kw":
                    filled(act, name)
                    act.wait_ge(sem("zeroed"), 2)
                    kw = ps(name)[:, 0:216].rearrange("p (t n) -> p t n", t=TC)
                    A(z3["kid"][:, 0:2, 0:HD], kw[:, 0:2, 0:HD], ACT.Copy)
                    A(z3["kid"][0:24, 2, 0:HD], kw[0:24, 2, 0:HD], ACT.Copy)
                    A(z3["wi"][:, 0:2, :], kw[:, 0:2, HD:HD + H], ACT.Copy, scale=H ** -0.5)
                    A(z3["wi"][0:24, 2, :], kw[0:24, 2, HD:HD + H], ACT.Copy, scale=H ** -0.5).then_inc(free(name), 1)
                elif name[0] not in ("bur", "bui"):
                    filled(act, name)
                    n = TCN[name[1]]
                    copy_out(name, z3[name[0]][0:n, name[1], :], ps(name)[0:n, :])
            for k, ss in enumerate((qss, kss)):
                act.wait_ge(sem("qk_squares"), k + 1)
                A(ss, ss, ACT.Sqrt, bias=eps, scale=1.0 / HD).then_inc(sem("qk_roots"), 1)

            def copy_T(name, dst, t, n=None):
                n = n or TCN[t]
                filled(act, name)
                copy_out(name, dst[:, 0:4, t * P:t * P + n],
                         ps(name)[:, :].rearrange("p (c t) -> p c t", c=4)[:, :, 0:n])

            for t in range(TC):
                copy_T(("qiT", t), qiT3, t)
            filled(act, "kiT")
            copy_out("kiT", kiT, n=T)
            filled(act, "wT")
            copy_out("wT", wT[0:H, :], ps("wT")[0:H, 0:24])
            emptied(act, "kiT")
            for b in range(NB):
                filled(act, ("skT", b))
                if b >= 2:
                    filled(act, ("sdot", b - 2))
                A(kisT[:, b % 2, PAST:SK], kiT[:, NP_ + b:NP_ + b + 1], ACT.Copy)
                copy_out(("skT", b), kisT[:, b % 2, 0:PAST], n=PAST)
                filled(act, ("sdot", b))
                if b >= 2:
                    act.wait_ge(sem("sample_scored"), b - 1)
                A(rb(b)[0:H, :], ps(("sdot", b))[0:H, 0:SK], ACT.Relu, scale=HD ** -0.5).then_inc(free(("sdot", b)), 1)
            filled(act, "sscore")
            for t in range(TC):
                for h in range(H):
                    n = H * t + h
                    filled(act, ("dot", t, h))
                    if n >= 2:
                        act.wait_ge(sem("scored"), n - 1)
                    A(relu[0:QN[t], n % 2, 0:KN[t]], ps(("dot", t, h))[0:QN[t], 0:KN[t]], ACT.Relu,
                      scale=HD ** -0.5).then_inc(free(("dot", t, h)), 1)
            for t in range(TC):
                copy_T(("kT", t), kT3, t)
            for t in range(TC):
                copy_T(("qT", t), qT3, t)

            act.wait_ge(sem("gelu_arg"), 1)
            A(gb, ga, ACT.Tanh, scale=GELU_C).then_inc(sem("gelu_tanh"), 1)
            for c in range(4):
                filled(act, ("glu", c))
                A(ga[:, c * T:(c + 1) * T], ps(("glu", c))[:, 0:T], ACT.Tanh, scale=0.5).then_inc(free(("glu", c)), 1)

            for t in range(TC):
                nq = QN[t]
                act.wait_ge(sem("nmax"), t + 1)
                for h in range(H):
                    A(lg[t][0:nq, h, :], lg[t][0:nq, h, :], ACT.Exp, bias=nmax[0:nq, H * t + h:H * t + h + 1],
                      scale=HD ** -0.5, accum_out=rsum[0:nq, H * t + h:H * t + h + 1]).then_inc(sem("probs"), 1)
                for i in range(PT_FILLS[t]):
                    name = ("pT", t, i)
                    filled(act, name)
                    if t < 2:
                        copy_out(name, pT[t][:, i * 512:(i + 1) * 512])
                    else:
                        src = ps(name)[:, 0:384].rearrange("p (h k q) -> p h k q", h=H, k=TC)
                        dst = pT[t].rearrange("p (h k q) -> p h k q", h=H, k=TC)
                        copy_out(name, dst[:, :, 0:2, :], src[:, :, 0:2, :], inc=False)
                        copy_out(name, dst[0:16, :, 2, :], src[0:16, :, 2, :])
                copy_T(("attT", t), ycat[:, 4:8, :], t, nq)

            for b in range(NB):
                if b >= 2:
                    act.wait_ge(sem("sample_logits"), b - 1)
                A(kcT[:, b % 2, :, PAST:SK], kT3[:, :, NP_ + b:NP_ + b + 1], ACT.Copy)
                for g in range(2):
                    name = ("cT", b, g)
                    filled(act, name)
                    copy_out(name, kcT[:, b % 2, :, g * P:(g + 1) * P],
                             ps(name)[:, :].rearrange("p (c t) -> p c t", c=4))
            act.wait_ge(sem("sample_max"), 1)
            A(sprob[0:64, :], ps("slogit")[0:64, 0:SK], ACT.Exp, bias=snm[0:64, :], scale=HD ** -0.5,
              accum_out=srs[0:64, :]).then_inc(free("slogit"), 1)
            filled(act, "spT")
            copy_out("spT", psT, n=P)
            filled(act, "sself")
            copy_out("sself", psd[0:24, :], ps("sself")[0:24, 0:64])

            act.wait_ge(sem("ki_out"), 16 * TC)
            act.wait_ge(sem("kv_out"), 16 * 2 * TC)
            squares(1, lambda c: emptied(act, ("wout", c)))
            root(1)
            for f in range(FT):
                filled(act, ("gate", f))
                if f >= 2:
                    emptied(act, ("gate", f - 2))
                A(ffa[:, f % 2, :], ps(("gate", f))[:, 0:T], ACT.Tanh, scale=0.5).then_inc(sem("ff_tanh"), 1)
            squares(2, lambda c: emptied(act, ("down", c)))
            root(2)
            for i in range(2):
                filled(act, ("pnew", i))
                copy_out(("pnew", i), pnew[0:23, i * 512:(i + 1) * 512], ps(("pnew", i))[0:23, :])
            emptied(act, ("pnew", 1))
            act.dma_start(o["pool_p"], pnew[0:15, :]).then_inc(sem("pool_out"), 16)
            act.dma_start(o["pool_s"][:, 14, :], pnew[15:23, :]).then_inc(sem("pool_out"), 16)
            squares(3, lambda c: emptied(act, ("pool", c)))
            root(3)
            act.wait_ge(sem("pool_out"), 32)
            for kind, dst in (("h2n", hn), ("xn", acc)):
                for t in range(TC):
                    for i in range(2):
                        filled(act, (kind, t, i))
                        n = TCN[t]
                        copy_out((kind, t, i), dst[0:n, t, i * 512:(i + 1) * 512], ps((kind, t, i))[0:n, :])
            act.wait_ge(sem("router_gap"), 1)
            A(g12[:, 1, :], g12[:, 0, :], ACT.Exp).then_inc(sem("router_exp"), 1)

            act.wait_ge(sem("passes_ready"), 1)
            n_pass = act.value_load(exp_i[0:1, PASSES:PASSES + 1], min_val=NE, max_val=PASSES)
            with act.Fori(0, n_pass) as i:
                def take(name, dst, src):
                    pass_filled(act, name, i)
                    A(dst, src, ACT.Copy).then_inc(bank_free[PASS_BANK[name]], 1)

                for half in range(2):
                    take(("gather", half), xg[:, 4 * half:4 * half + 4, :],
                         bank[PASS_BANK[("gather", half)]][:, :].rearrange("p (c s) -> p c s", c=4))
                for j in range(FC):
                    if j >= 2:
                        pass_emptied(act, ("up", j - 2), i)
                    pass_filled(act, ("gate", j), i)
                    A(th[:, j % 2, :], bank[PASS_BANK[("gate", j)]][:, :], ACT.Tanh, scale=0.5).then_inc(sem("gate_tanh"), 1)
                    if j == 0:
                        take("pickT", pickT, bank[PASS_BANK["pickT"]][:, 0:T])
                    else:
                        take(("hT", j - 1), hbT[:, (j - 1) % 2, :, :],
                             bank[PASS_BANK[("hT", 0)]][:, :].rearrange("p (f s) -> p f s", f=4))
                take(("hT", FC - 1), hbT[:, (FC - 1) % 2, :, :],
                     bank[PASS_BANK[("hT", 0)]][:, :].rearrange("p (f s) -> p f s", f=4))
                for half in range(2):
                    take(("y", half), yb[:, half * 512:(half + 1) * 512], bank[PASS_BANK[("y", half)]][:, :])

        @block.vector
        def _(dve):
            TT, TS, STT = nc.vector.tensor_tensor, nc.vector.tensor_scalar, nc.vector.scalar_tensor_tensor
            done = [0]

            def link(ins):
                done[0] += 1
                ins.then_inc(sem("dve_step"), 1)
                dve.wait_ge(sem("dve_step"), done[0])

            def norm(k, g):
                emptied(dve, f"norm{k}")
                link(nc.vector.reciprocal(rs, std))
                for c in range(C):
                    STT(h3[:, c, :], x3[:, c, :], g[:, c:c + 1], rs, ALU.mult, ALU.mult).then_inc(sem("normed"), 1)

            def whole_exp(dst, x, t0, t1, t2):
                link(TS(t0, x, 1.4426950408889634, MAGIC, ALU.mult, ALU.add))
                link(TS(t0, t0, -MAGIC, -126.0, ALU.add, ALU.max))
                link(TS(t0, t0, 127.0, None, ALU.min))
                link(STT(t1, t0, -0.693359375, x, ALU.mult, ALU.add))
                link(STT(t1, t0, 2.12194440e-4, t1, ALU.mult, ALU.add))
                link(TS(t2, t1, 1.0 / 5040, None, ALU.mult))
                for c in (720, 120, 24, 6, 2, 1):
                    link(STT(t2, t2, 1.0 / c, t1, ALU.add, ALU.mult))
                link(TS(t0, t0, 127.0, 8388608.0, ALU.add, ALU.mult))
                link(nc.vector.tensor_copy(expo[:, :], t0))
                link(STT(dst, t2, 1.0, expo[:, :].bitcast(F32), ALU.add, ALU.mult))

            def wide(v, n):
                return v.unsqueeze(2).to_broadcast([P, NJ, n])

            dve.wait_ge(sem("x_in"), 16)
            dve.wait_ge(sem("params_in"), 16)
            norm(0, param("g_mix0"))

            whole_exp(dt_, param("log_dt"), s1, s2, s3)
            link(TT(rad, lam_r, dt_, ALU.mult))
            whole_exp(rate, rad, s1, s2, s3)
            link(TT(s1, lam_i, dt_, ALU.mult))
            link(TS(s2, s1, 1.0 / (2 * math.pi), MAGIC, ALU.mult, ALU.add))
            link(TS(s2, s2, -MAGIC, None, ALU.add))
            link(STT(s1, s2, -6.28125, s1, ALU.mult, ALU.add))
            link(STT(s1, s2, -0.0019353071795864769, s1, ALU.mult, ALU.add))
            lim = 3.1415925
            link(TS(ang, s1, lim, -lim, ALU.min, ALU.max))
            link(TS(s2, s1, math.pi / 2, None, ALU.add))
            link(TS(s3, s2, math.pi, -2 * math.pi, ALU.is_gt, ALU.mult))
            link(TT(s2, s2, s3, ALU.add))
            TS(cang, s2, lim, -lim, ALU.min, ALU.max).then_inc(sem("angles"), 1)
            dve.wait_ge(sem("sincos"), 1)
            link(TT(s1, sn, sn, ALU.mult))
            link(TT(s2, cn, cn, ALU.mult))
            link(TT(s1, s1, s2, ALU.add))
            link(TS(s1, s1, -0.5, 1.5, ALU.mult, ALU.add))
            TT(er3[:, :, 0], cn, s1, ALU.mult)
            TT(ei3[:, :, 0], sn, s1, ALU.mult)
            link(TT(cn, cn, s1, ALU.mult))
            link(TT(sn, sn, s1, ALU.mult))
            m = 1
            while m < NP_:
                n = min(m, NP_ - m)
                step = NJ if n <= 64 else NJ // 2
                for j in range(0, NJ, step):
                    js = slice(j, j + step)
                    tmp = [etmp[:, k * 1024:k * 1024 + step * n].rearrange("p (j t) -> p j t", j=step) for k in range(4)]
                    pr, pi = [e[:, js, m - 1:m].to_broadcast([P, step, n]) for e in (er3, ei3)]
                    TT(tmp[0], er3[:, js, 0:n], pr, ALU.mult)
                    TT(tmp[1], ei3[:, js, 0:n], pi, ALU.mult)
                    TT(tmp[2], er3[:, js, 0:n], pi, ALU.mult)
                    link(TT(tmp[3], ei3[:, js, 0:n], pr, ALU.mult))
                    TT(er3[:, js, m:m + n], tmp[0], tmp[1], ALU.subtract)
                    link(TT(ei3[:, js, m:m + n], tmp[2], tmp[3], ALU.add))
                m += n
            link(TT(lbr, rate, cn, ALU.mult))
            link(TT(lbi, rate, sn, ALU.mult))
            link(TT(s1, lam_r, lam_r, ALU.mult))
            link(TT(s2, lam_i, lam_i, ALU.mult))
            link(TT(s1, s1, s2, ALU.add))
            link(nc.vector.reciprocal(s1, s1))
            link(TS(s2, lbr, -1.0, None, ALU.add))
            link(TT(fr_, s2, lam_r, ALU.mult))
            link(TT(s3, lbi, lam_i, ALU.mult))
            link(TT(fr_, fr_, s3, ALU.add))
            link(TT(fr_, fr_, s1, ALU.mult))
            link(TT(fi_, lbi, lam_r, ALU.mult))
            link(TT(s3, s2, lam_i, ALU.mult))
            link(TT(fi_, fi_, s3, ALU.subtract))
            link(TT(fi_, fi_, s1, ALU.mult))
            w1, w2 = [rtmp[:, k * 512:(k + 1) * 512].rearrange("p (j s) -> p j s", j=NJ) for k in range(2)]
            TT(w1, c_m[:, :, 0, :], wide(fr_, 32), ALU.mult)
            link(TT(w2, c_m[:, :, 1, :], wide(fi_, 32), ALU.mult))
            link(TT(cf4[:, :, 0, :], w1, w2, ALU.subtract))
            TT(w1, c_m[:, :, 0, :], wide(fi_, 32), ALU.mult)
            link(TT(w2, c_m[:, :, 1, :], wide(fr_, 32), ALU.mult))
            STT(cf4[:, :, 1, :], w1, -1.0, w2, ALU.mult, ALU.subtract)
            TS(csn3, c_m[:, :, 1, :], -1.0, None, ALU.mult).then_inc(sem("out_mats"), 1)

            for j in range(NJ):
                filled(dve, ("bur", j))
                br, bi = ps(("bur", j)), ps(("bui", j))
                TT(d1, er3[:, j, :], br[:, 0:NP_], ALU.mult)
                TT(d4, ei3[:, j, :], br[:, 0:NP_], ALU.mult)
                nc.vector.tensor_copy(raw[:, j, 0, :], br[:, NP_:T]).then_inc(free(("bur", j)), 1)
                filled(dve, ("bui", j))
                TT(d2, ei3[:, j, :], bi[:, 0:NP_], ALU.mult)
                TT(d3, er3[:, j, :], bi[:, 0:NP_], ALU.mult)
                nc.vector.tensor_copy(raw[:, j, 1, :], bi[:, NP_:T]).then_inc(free(("bui", j)), 1)
                emptied(dve, ("bui", j))
                TT(vr, d1, d2, ALU.add)
                link(TT(vi, d3, d4, ALU.subtract))
                if j >= 2:
                    dve.wait_ge(sem("states"), j - 1)
                r_row = rate[:, j:j + 1].to_broadcast([P, NP_])
                nc.vector.tensor_tensor_scan(g4[:, j % 2, 0, :], r_row, vr, 0.0, ALU.mult, ALU.add)
                nc.vector.tensor_tensor_scan(g4[:, j % 2, 1, :], r_row, vi, 0.0, ALU.mult, ALU.add).then_inc(sem("scanned"), 1)
                dve.wait_ge(sem("scanned"), j + 1)

            t8 = [rtmp[:, k * 128:(k + 1) * 128].rearrange("p (j b) -> p j b", j=NJ) for k in range(4)]
            h0r, h0i = [param(n).rearrange("p (j b) -> p j b", j=NJ) for n in ("h0r", "h0i")]
            for out, terms in ((0, ((lbr, h0r, None), (lbi, h0i, ALU.subtract), (fr_, raw[:, :, 0, :], ALU.add),
                                    (fi_, raw[:, :, 1, :], ALU.subtract))),
                               (1, ((lbr, h0i, None), (lbi, h0r, ALU.add), (fr_, raw[:, :, 1, :], ALU.add),
                                    (fi_, raw[:, :, 0, :], ALU.add)))):
                for n, (f, v, op) in enumerate(terms):
                    link(TT(t8[0] if n == 0 else t8[1], v, wide(f, NB), ALU.mult))
                    if n:
                        dst = hs[:, :, out, :] if n == 3 else t8[0]
                        if n == 3 and out == 1:
                            TT(dst, t8[0], t8[1], op).then_inc(sem("sample_state"), 1)
                        else:
                            link(TT(dst, t8[0], t8[1], op))

            dve.wait_ge(sem("sample_state"), 1)

            def rope(v, heads):
                n = TC * heads * 32
                t1, t2, t3 = [rtmp[:, k * n:(k + 1) * n].rearrange("p (t h d) -> p t h d", t=TC, h=heads) for k in range(3)]
                cs, sn_ = [w.unsqueeze(2).to_broadcast([P, TC, heads, 32]) for w in (cos3, sin3)]
                lo, hi = v[:, :, :, 0:32], v[:, :, :, 32:64]
                TT(t1, lo, cs, ALU.mult)
                TT(t2, hi, sn_, ALU.mult)
                TT(t3, lo, sn_, ALU.mult)
                link(TT(hi, hi, cs, ALU.mult))
                TT(lo, t1, t2, ALU.subtract)
                return TT(hi, hi, t3, ALU.add)

            for t in range(TC):
                emptied(dve, ("qi", t))
            rope(z4["qi"], H).then_inc(sem("qi_ready"), 1)
            dve.wait_ge(sem("qi_ready"), 1)
            emptied(dve, "kw")
            kid4 = z3["kid"][:, :, 0:HD].unsqueeze(2)
            link(rope(kid4, 1))
            nc.vector.tensor_copy(z3["kid"][:, :, HD:2 * HD], z3["kid"][:, :, 0:HD]).then_inc(sem("kid_ready"), 1)
            sq4 = rtmp[:, 0:TC * 512].rearrange("p (t h d) -> p t h d", t=TC, h=H)
            dve.wait_ge(sem("kid_ready"), 1)
            for n, ss in (("q", qss), ("k", kss)):
                for t in range(TC):
                    emptied(dve, (n, t))
                link(TT(sq4, z4[n], z4[n], ALU.mult))
                nc.vector.tensor_reduce(ss.rearrange("p (t h) -> p t h", t=TC), sq4, AX.X, ALU.add).then_inc(sem("qk_squares"), 1)
                dve.wait_ge(sem("qk_squares"), 1 if n == "q" else 2)
            for k, (n, ss, g) in enumerate((("q", qss, "qg"), ("k", kss, "kg"))):
                dve.wait_ge(sem("qk_roots"), k + 1)
                link(nc.vector.reciprocal(ss, ss))
                rs4 = ss.rearrange("p (t h) -> p t h", t=TC).unsqueeze(3).to_broadcast([P, TC, H, HD])
                link(TT(z4[n], z4[n], rs4, ALU.mult))
                g4_ = param(g).unsqueeze(1).to_broadcast([P, TC * H, HD])
                zz = z4[n].rearrange("p t h d -> p (t h) d")
                link(TT(zz, zz, g4_, ALU.mult))
                rope(z4[n], H).then_inc(sem("qk_ready"), 1)
                dve.wait_ge(sem("qk_ready"), k + 1)

            for t in range(TC):
                emptied(dve, ("qiT", t))
            emptied(dve, "wT")
            dve.wait_ge(sem("zeroed"), 1)
            for hh in range(2):
                half = slice(HD * hh, HD * hh + HD)
                nc.vector.tensor_copy(qib3[half, :, hh::2], qiT3[half, :, NP_:T].rearrange("p c b -> p b c"))
            TT(wbd[0:H, :].rearrange("p (b m) -> p b m", b=NB), const("d8")[0:H, :].rearrange("p (b m) -> p b m", b=NB),
               wT[0:H, 16:24].unsqueeze(1).to_broadcast([H, NB, NB]), ALU.mult).then_inc(sem("sample_index_q"), 1)
            link(nc.vector.tensor_copy(sc[0:40, 2, :], init3[0:40, 2, :]))
            for t in range(TC):
                nq, nk = QN[t], KN[t]
                for h in range(H):
                    n = H * t + h
                    emptied(dve, ("dot", t, h))
                    base = init3 if h == 0 else sc
                    STT(sc[0:nq, t, 0:nk], relu[0:nq, n % 2, 0:nk], z3["wi"][0:nq, t, h:h + 1], base[0:nq, t, 0:nk],
                        ALU.mult, ALU.add).then_inc(sem("scored"), 1)
                    dve.wait_ge(sem("scored"), n + 1)
            filled(dve, "sscore")
            TT(sc[32:40, 2, 0:SK], ps("sscore")[32:40, 0:SK], init3[32:40, 2, 0:SK], ALU.add).then_inc(free("sscore"), 1)
            emptied(dve, "sscore")
            m8 = mx8.rearrange("p (t k) -> p t k", t=TC)
            for r in range(TOPK // 8):
                for t in range(TC):
                    rows, nk = (40 if t == 2 else P), KN[t]
                    last = nc.vector.max(m8[0:rows, t, :], sc[0:rows, t, 0:nk])
                link(last)
                for t in range(TC):
                    rows, nk = (40 if t == 2 else P), KN[t]
                    last = nc.vector.match_replace(sc[0:rows, t, 0:nk], m8[0:rows, t, :], sc[0:rows, t, 0:nk], TAKEN)
                link(last)
            for t in range(TC):
                rows, nk = (40 if t == 2 else P), KN[t]
                link(TS(sc[0:rows, t, 0:nk], sc[0:rows, t, 0:nk], TAKEN, -NEG, ALU.is_equal, ALU.mult))
                link(STT(sc[0:rows, t, 0:nk], sc[0:rows, t, 0:nk], NEG, init3[0:rows, t, 0:nk], ALU.add, ALU.add))

            for c in range(4):
                filled(dve, ("y", c))
                STT(uT[:, c, :], uT[:, c, :], param("d_skip")[:, c:c + 1], ps(("y", c))[:, 0:T], ALU.mult,
                    ALU.add).then_inc(free(("y", c)), 1)
            emptied(dve, ("y", 3))
            yv = uT.rearrange("p c t -> p (c t)")
            link(TT(ga, yv, yv, ALU.mult))
            link(TS(ga, ga, 0.044715, 1.0, ALU.mult, ALU.add))
            TT(ga, ga, yv, ALU.mult).then_inc(sem("gelu_arg"), 1)
            hr_, hi_ = er3[:, :, NP_ - 1], ei3[:, :, NP_ - 1]
            TT(s1, fr_, hr_, ALU.mult)
            TT(s2, fi_, hi_, ALU.mult)
            TT(s3, fr_, hi_, ALU.mult)
            link(TT(ang, fi_, hr_, ALU.mult))
            TT(hlast[:, 0:NJ], s1, s2, ALU.subtract)
            TT(hlast[:, NJ:2 * NJ], s3, ang, ALU.add).then_inc(sem("last_state"), 1)
            dve.wait_ge(sem("gelu_tanh"), 1)
            link(STT(gb, gb, 1.0, yv, ALU.add, ALU.mult))
            TS(yv, gb, 0.5, None, ALU.mult).then_inc(sem("gelu"), 1)
            dve.wait_ge(sem("gelu"), 1)
            for c in range(4):
                emptied(dve, ("glu", c))
            link(TS(ga, ga, 0.5, 0.5, ALU.mult, ALU.add))
            TT(ycat[:, 0:4, :].rearrange("p c t -> p (c t)"), ga, yv, ALU.mult).then_inc(sem("ssm_out"), 1)
            dve.wait_ge(sem("ssm_out"), 1)
            link(nc.vector.memset(qbd, 0.0))
            emptied(dve, ("qT", 2))
            for hh in range(2):
                half = slice(HD * hh, HD * hh + HD)
                for c in range(4):
                    at = c * NB * 64 + 2 * c + hh
                    last = nc.vector.tensor_copy(qbd[half, at:at + 72 * (NB - 1) + 1:72], qT3[half, c, NP_:T])
            last.then_inc(sem("sample_q"), 1)

            for t in range(TC):
                nq, nk = QN[t], KN[t]
                for h in range(H):
                    filled(dve, ("logit", t, h))
                    nc.vector.tensor_tensor_reduce(
                        out=lg[t][0:nq, h, :], in0=ps(("logit", t, h))[0:nq, 0:nk], in1=sc[0:nq, t, 0:nk], scale=1.0,
                        scalar=-3e38, op0=ALU.add, op1=ALU.max,
                        accum_out=mx[0:nq, H * t + h:H * t + h + 1]).then_inc(free(("logit", t, h)), 1)
                emptied(dve, ("logit", t, H - 1))
                cols = slice(H * t, H * t + H)
                TS(nmax[0:nq, cols], mx[0:nq, cols], -(HD ** -0.5), None, ALU.mult).then_inc(sem("nmax"), 1)
                dve.wait_ge(sem("probs"), H * (t + 1))
                link(nc.vector.reciprocal(rinv[0:nq, cols], rsum[0:nq, cols]))
                filled(dve, ("att", t))
                TT(yn[0:nq, :].rearrange("p (h d) -> p h d", h=H), ps(("att", t))[0:nq, :].rearrange("p (h d) -> p h d", h=H),
                   rinv[0:nq, cols].unsqueeze(2).to_broadcast([nq, H, HD]), ALU.mult).then_inc(free(("att", t)), 1)

            filled(dve, "slogit")
            link(nc.vector.tensor_reduce(smx[0:64, :], ps("slogit")[0:64, 0:SK], AX.X, ALU.max))
            TS(snm[0:64, :], smx[0:64, :], -(HD ** -0.5), None, ALU.mult).then_inc(sem("sample_max"), 1)
            emptied(dve, "slogit")
            link(nc.vector.reciprocal(sri[0:64, :], srs[0:64, :]))
            link(TS(sprob[0:64, :], sprob[0:64, :], sri[0:64, :], None, ALU.mult))
            TS(dself[0:64, :], const("m24")[0:64, :], sprob[0:64, PAST:SK], None, ALU.mult).then_inc(sem("sample_probs"), 1)
            filled(dve, "satt")
            sv = ps("satt")[:, 0:64].rearrange("p (b c w) -> p c b w", b=NB, c=4)
            nc.vector.tensor_copy(ycat[0:HD, 4:8, NP_:T], sv[0:HD, :, :, 0])
            nc.vector.tensor_copy(ycat[HD:P, 4:8, NP_:T], sv[HD:P, :, :, 1]).then_inc(free("satt"), 1)

            def add_residual(name, c):
                filled(dve, (name, c))
                TT(x3[:, c, :], x3[:, c, :], ps((name, c))[:, 0:T], ALU.add).then_inc(free((name, c)), 1)

            for c in range(C):
                add_residual("wout", c)
            norm(1, param("g_ffn0"))
            dve.wait_ge(sem("kv_out"), 16 * 2 * TC)
            for f in range(FT):
                dve.wait_ge(sem("ff_tanh"), f + 1)
                STT(ffa[:, 2 + f % 2, :], ffa[:, f % 2, :], 1.0, ps(("gate", f))[:, 0:T], ALU.add,
                    ALU.mult).then_inc(free(("gate", f)), 1)
                filled(dve, ("up", f))
                emptied(dve, ("gate", f))
                STT(hff[:, f, :], ffa[:, 2 + f % 2, :], 0.5, ps(("up", f))[:, 0:T], ALU.mult,
                    ALU.mult).then_inc(free(("up", f)), 1)
            for c in range(C):
                add_residual("down", c)

            norm(2, param("g_mix1"))
            dve.wait_ge(sem("normed"), 3 * C)
            nc.vector.tensor_copy(win_a[:, :, 0:1], h3[:, :, 0:1])
            link(TT(win_a[:, :, 1:NP_], h3[:, :, 1:NP_], h3[:, :, 0:NP_ - 1], ALU.add))
            nc.vector.tensor_copy(win_b[:, 2:8, 0:2], win_a[:, 2:8, 0:2])
            link(TT(win_b[:, 2:8, 2:NP_], win_a[:, 2:8, 2:NP_], win_a[:, 2:8, 0:NP_ - 2], ALU.add))
            nc.vector.tensor_copy(win_a[:, 4:8, 0:4], win_b[:, 4:8, 0:4])
            link(TT(win_a[:, 4:8, 4:NP_], win_b[:, 4:8, 4:NP_], win_b[:, 4:8, 0:NP_ - 4], ALU.add))
            nc.vector.tensor_copy(win_b[:, 6:8, 0:8], win_a[:, 6:8, 0:8])
            link(TT(win_b[:, 6:8, 8:NP_], win_a[:, 6:8, 8:NP_], win_a[:, 6:8, 0:NP_ - 8], ALU.add))
            dve.wait_ge(sem("hist_in"), 16)
            nc.vector.tensor_copy(ext[:, :, :, 0:15], hist)
            link(nc.vector.tensor_copy(ext[:, :, :, 15:16], h3[:, :, NP_:T].unsqueeze(3)))
            for g, w in enumerate(WINDOWS):
                cs = slice(2 * g, 2 * g + 2)
                win = (win_a, win_b)[g % 2]
                link(STT(pl[:, cs, 0:NP_], win[:, cs, :], 1.0 / w, h3[:, cs, 0:NP_], ALU.mult, ALU.subtract))
                few = const("rw")[:, g * 16:g * 16 + w - 1].unsqueeze(1).to_broadcast([P, 2, w - 1])
                link(TT(pl[:, cs, 0:w - 1], win[:, cs, 0:w - 1], few, ALU.mult))
                link(TT(pl[:, cs, 0:w - 1], pl[:, cs, 0:w - 1], h3[:, cs, 0:w - 1], ALU.subtract))
                link(nc.vector.tensor_reduce(pl[:, cs, NP_:T], ext[:, cs, :, 16 - w:16], AX.X, ALU.add))
                STT(pl[:, cs, NP_:T], pl[:, cs, NP_:T], 1.0 / w, h3[:, cs, NP_:T], ALU.mult,
                    ALU.subtract).then_inc(sem("pooled"), 1)
            for c in range(C):
                filled(dve, ("pool", c))
                STT(x3[:, c, :], ps(("pool", c))[:, 0:T], param("pool_scale")[:, c:c + 1], x3[:, c, :], ALU.mult,
                    ALU.add).then_inc(free(("pool", c)), 1)
            norm(3, param("g_ffn1"))

            link(nc.vector.memset(lgt, 0.0))
            filled(dve, "router")
            rl = ps("router")[:, 0:TC * NE].rearrange("p (t e) -> p t e", t=TC)
            nc.vector.tensor_copy(lgt[:, 0:2, :], rl[:, 0:2, :])
            nc.vector.tensor_copy(lgt[0:24, 2, :], rl[0:24, 2, :]).then_inc(free("router"), 1)
            emptied(dve, "router")
            iu = idx_u.rearrange("p (t e) -> p t e", t=TC)
            for t in range(TC):
                last = nc.vector.max(m8r[:, t, :], lgt[:, t, :])
            link(last)
            for t in range(TC):
                last = nc.vector.max_index(iu[:, t, :], m8r[:, t, :], lgt[:, t, :])
            link(last)
            TT(g12[:, 0, :], m8r[:, :, 1], m8r[:, :, 0], ALU.subtract).then_inc(sem("router_gap"), 1)
            link(nc.vector.tensor_copy(idxf, iu))
            e8 = iota[:, 0:NE].unsqueeze(1).to_broadcast([P, TC, NE])
            TT(oh1, e8, idxf[:, :, 0:1].to_broadcast([P, TC, NE]), ALU.is_equal)
            link(TT(oh2, e8, idxf[:, :, 1:2].to_broadcast([P, TC, NE]), ALU.is_equal))
            link(TT(sel, oh1, oh2, ALU.add))
            TT(sel, sel, const("valid")[:, 0:TC].unsqueeze(2).to_broadcast([P, TC, NE]), ALU.mult).then_inc(sem("picked"), 1)
            dve.wait_ge(sem("picked"), 1)
            dve.wait_ge(sem("router_exp"), 1)
            link(TS(g12[:, 2, :], g12[:, 1, :], 1.0, None, ALU.add))
            link(nc.vector.reciprocal(g12[:, 2, :], g12[:, 2, :]))
            link(TT(g12[:, 3, :], g12[:, 1, :], g12[:, 2, :], ALU.mult))
            link(TT(oh1, oh1, g12[:, 2, :].unsqueeze(2).to_broadcast([P, TC, NE]), ALU.mult))
            link(TT(oh2, oh2, g12[:, 3, :].unsqueeze(2).to_broadcast([P, TC, NE]), ALU.mult))
            link(TT(gate, oh1, oh2, ALU.add))
            filled(dve, "rank")
            rp = ps("rank")[:, 0:4 * NE].rearrange("p (t e) -> p t e", t=4)
            link(TT(slot_v, sel, rp[:, 0:TC, :], ALU.mult))
            link(TS(slot_v, slot_v, -1.0, None, ALU.add))
            ov2 = over.rearrange("p (b e) -> p b e", b=2)
            for b in range(2):
                link(TS(ov2[:, b, :], rp[:, TC, :], 128.0 * (b + 1), None, ALU.is_gt))
            nc.vector.tensor_tensor_scan(ranko, ones[:, 0:16], over, 0.0, ALU.mult, ALU.add).then_inc(free("rank"), 1)
            emptied(dve, "rank")
            for k in range(4):
                link(STT(oh[:, k, :], ranko, float(k + 1), over, ALU.is_equal, ALU.mult))
            for b in range(2):
                link(TS(cand[:, :, b, :], slot_v, -128.0 * (b + 1), None, ALU.add))
                link(nc.vector.tensor_copy(gcand[:, :, b, :], gate))
            ohb = oh.unsqueeze(1).to_broadcast([P, TC, 4, 16])
            for dst, src, first in ((pslot, cand, slot_v), (pgate, gcand, gate)):
                for t in range(TC):
                    sv_ = src[:, t, :, :].rearrange("p b e -> p (b e)").unsqueeze(1).to_broadcast([P, 4, 16])
                    link(TT(prod[:, t, :, :], sv_, oh, ALU.mult))
                link(nc.vector.tensor_reduce(dst[:, NE:PASSES, :].rearrange("p i t -> p t i"), prod, AX.X, ALU.add))
                link(nc.vector.tensor_copy(dst[:, 0:NE, :].rearrange("p e t -> p t e"), first))
            link(TT(prod[:, 0, :, :], const("ecol").unsqueeze(1).to_broadcast([P, 4, 16]), oh, ALU.mult))
            link(nc.vector.tensor_copy(pexp[:, 0:NE], iota[:, 0:NE]))
            link(nc.vector.tensor_reduce(pexp[:, NE:PASSES], prod[:, 0, :, :], AX.X, ALU.add))
            link(nc.vector.tensor_copy(exp_i[:, 0:PASSES], pexp))
            link(TS(over[:, 0:1], ranko[:, 15:16], float(NE), None, ALU.add))
            nc.vector.tensor_copy(exp_i[:, PASSES:PASSES + 1], over[:, 0:1]).then_inc(sem("passes_ready"), 1)
            for i in range(2):
                emptied(dve, ("xn", 2, i))

            dve.wait_ge(sem("passes_ready"), 1)
            n_pass = dve.value_load(exp_i[0:1, PASSES:PASSES + 1], min_val=NE, max_val=PASSES)
            with dve.Fori(0, n_pass) as i:
                nc.vector.tensor_copy(cur[:, 0:TC].unsqueeze(1), pslot[:, bass.ds(i, 1), :])
                nc.vector.tensor_copy(cur[:, TC:2 * TC].unsqueeze(1), pgate[:, bass.ds(i, 1), :]).then_inc(sem("pass_cols"), 1)
                dve.wait_ge(sem("pass_cols"), i + 1)
                for t in range(TC):
                    last = TS(pick[:, t, :], iota, cur[:, t:t + 1], None, ALU.is_equal)
                last.then_inc(sem("pick_ready"), 1)
                for j in range(FC):
                    dve.wait_ge(sem("gate_tanh"), FC * i + j + 1)
                    STT(th[:, j % 2, :], th[:, j % 2, :], 1.0, bank[PASS_BANK[("gate", j)]][:, :], ALU.add,
                        ALU.mult).then_inc(bank_free[PASS_BANK[("gate", j)]], 1)
                    pass_emptied(dve, ("gate", j), i)
                    pass_filled(dve, ("up", j), i)
                    if j >= 2:
                        pass_filled(dve, ("hT", j - 2), i)
                    STT(hb[:, j % 2, :], th[:, j % 2, :], 0.5, bank[PASS_BANK[("up", j)]][:, :], ALU.mult,
                        ALU.mult).then_inc(bank_free[PASS_BANK[("up", j)]], 1)
                for k in range(2 * TC):
                    t, half = k // 2, k % 2
                    n, b = TCN[t], PASS_BANK[("scatter", k)]
                    pass_filled(dve, ("scatter", k), i)
                    dst = acc[0:n, t, half * 512:(half + 1) * 512]
                    STT(dst, bank[b][0:n, :], cur[0:n, TC + t:TC + t + 1], dst, ALU.mult, ALU.add).then_inc(bank_free[b], 1)
                for k in (2 * TC - 2, 2 * TC - 1):
                    pass_emptied(dve, ("scatter", k), i)


def pack_inputs(i):
    f = np.float32

    def per_channel(v):
        return v.reshape(-1, P).T

    x = np.concatenate([i["meta_tokens"], i["x_prompt"][0], i["x_sample"][:, 0]], axis=0)
    p = np.zeros((P, PARAM_N), f)

    def put(name, v):
        at, n = PARAM_AT[name]
        p[:, at:at + n] = v.reshape(-1, n)

    for name, key in (("g_mix0", "norm_mix0"), ("g_ffn0", "norm_ffn0"), ("g_mix1", "norm_mix1"),
                      ("g_ffn1", "norm_ffn1"), ("pool_scale", "pool_scale"), ("d_skip", "ssm_d")):
        put(name, per_channel(i[key][0]))
    put("lam_re", per_channel(i["ssm_lambda_re"][0].reshape(-1)))
    put("lam_im", per_channel(i["ssm_lambda_im"][0].reshape(-1)))
    put("log_dt", per_channel(np.repeat(i["ssm_log_dt"][0], 64)))
    put("qg", i["q_norm"])
    put("kg", i["k_norm"])
    put("router", i["router_w"][0].reshape(C, P, NE).transpose(1, 0, 2))
    for name, key in (("h0r", "state_ssm_re"), ("h0i", "state_ssm_im")):
        put(name, i[key][0].reshape(NB, NJ, P).transpose(2, 1, 0))
    b = np.zeros((4, 2, 16, 4, 2, 2, 64), f)
    c = np.zeros((2, 64, NJ, 2, 2, 16), f)
    for r, (kb_, kc_) in enumerate((("ssm_b_re", "ssm_c_re"), ("ssm_b_im", "ssm_c_im"))):
        bv = i[kb_][0].reshape(4, 4, 2, 64, 16)
        cv = i[kc_][0].reshape(NJ, 2, 16, 64)
        for g in range(2):
            b[:, g, :, :, r, g, :] = bv[:, :, g].transpose(1, 3, 0, 2)
            c[g, :, :, r, g, :] = cv[:, g].transpose(2, 0, 1)
    put("b", b.reshape(P, -1))
    put("c", c.reshape(P, -1))
    return {
        "x": x.T.reshape(C, P, T).transpose(1, 0, 2).reshape(P, C * T),
        "consts": shape_constants(), "params": p,
        "w_in": i["w_in0"][0], "w_glu": i["ssm_w_glu"][0], "w_out": i["w_out0"][0],
        "w_gate": i["ffn_w_gate"][0], "w_up": i["ffn_w_up"][0], "w_down": i["ffn_w_down"][0],
        "pool_w": i["pool_w"][0].reshape(D, 256), "moe_gate": i["moe_w_gate"][0],
        "moe_up": i["moe_w_up"][0], "moe_down": i["moe_w_down"][0],
        "page_table": i["page_table"].reshape(1, 2 * NB),
        "cache_k": i["cache_k"][0].reshape(-1, P, H * HD), "cache_v": i["cache_v"][0].reshape(-1, P, H * HD),
        "cache_kidx": i["cache_kidx"][0], "state_pool": i["state_pool"][0],
        "hist": i["state_pool"][0].reshape(NB, 15, C, P).transpose(3, 2, 0, 1).reshape(P, -1),
    }


OUTS = {"y": (T, D), "k": (T, 512), "v": (T, 512), "kidx": (T, HD), "hs": (P, NJ * 2 * NB), "hl": (P, 2 * NJ),
        "pool_p": (15, D), "pool_s": (NB, 15, D)}


def kernel(**inputs):
    import concourse.bacc as bacc
    from concourse.bass_utils import run_bass_kernel_spmd

    nc = bacc.Bacc("TRN2", target_bir_lowering=False, num_devices=1)
    arrays = {k: np.ascontiguousarray(v) for k, v in pack_inputs({k: np.asarray(v) for k, v in inputs.items()}).items()}
    a = {k: nc.dram_tensor("in_" + k, v.shape, mybir.dt.from_np(v.dtype), kind="ExternalInput").ap()
         for k, v in arrays.items()}
    a["n_pool"] = arrays["cache_k"].shape[0]
    o = {k: nc.dram_tensor("out_" + k, shape, F32, kind="ExternalOutput").ap() for k, shape in OUTS.items()}
    hybrid_step(nc, a, o)
    r = run_bass_kernel_spmd(nc, [{"in_" + k: v for k, v in arrays.items()}], core_ids=[0]).results[0]
    g = {k: r["out_" + k] for k in OUTS}
    k_, v_ = [g[n].reshape(T, H, HD) for n in ("k", "v")]
    hs = g["hs"].reshape(P, NJ, 2, NB).transpose(2, 3, 1, 0).reshape(2, 1, NB, 32, 64)
    hl = g["hl"].reshape(P, 2, NJ).transpose(1, 2, 0).reshape(2, 1, 1, 32, 64)
    return (g["y"][16:NP_][None], g["y"][NP_:][:, None], k_[None, None, :NP_], v_[None, None, :NP_],
            g["kidx"][None, None, :NP_], hl[0], hl[1], g["pool_p"][None, None],
            k_[NP_:][None, :, None], v_[NP_:][None, :, None], g["kidx"][NP_:][None, :, None],
            hs[0], hs[1], g["pool_s"][None])
```

```python
import math
from contextlib import ExitStack

import numpy as np
import concourse.bass as bass
from concourse import mybir

F32 = mybir.dt.float32
I32 = mybir.dt.int32
U32 = mybir.dt.uint32
F32R = mybir.dt.float32r
ALU = mybir.AluOpType
ACT = mybir.ActivationFunctionType
AX = mybir.AxisListType

P = 128
D = 1024
C = D // P
NP_ = 272
NB = 8
T = NP_ + NB
TC = 3
TCN = [128, 128, 24]
QN = [128, 128, 16]
KN = [128, 256, 272]
H = 8
HD = 64
PAST = 256
SK = PAST + 1
NJ = 16
FF = 2816
FT = FF // P
FE = 3584
NE = 8
FC = FE // 512
EPS = 1e-6
NEG = -1e30
TAKEN = -3e38
TOPK = 64
SLOT = 4096
SLOTS = 3
RING = 7
MAGIC = 12582912.0
WINDOWS = (2, 4, 8, 16)
INDEX_AT = 15
NORM_AT = 32
GELU_C = math.sqrt(2.0 / math.pi)

CONST_COLS = [("ident", 128), ("ones", 128), ("tri", 128), ("iota", 128), ("cos", 96), ("sin", 96),
              ("init", 816), ("rsel", 64), ("m24", 24), ("d8", 64), ("rw", 64), ("valid", 4),
              ("ecol", 16)]
PARAM_COLS = [("g_mix0", C), ("g_ffn0", C), ("g_mix1", C), ("g_ffn1", C), ("pool_scale", C),
              ("d_skip", 4), ("lam_re", NJ), ("lam_im", NJ), ("log_dt", NJ), ("qg", HD), ("kg", HD),
              ("router", C * NE), ("h0r", NJ * NB), ("h0i", NJ * NB), ("b", 4 * 2 * 128),
              ("c", NJ * 2 * 32)]


def offsets(cols):
    at, out = 0, {}
    for name, n in cols:
        out[name] = (at, n)
        at += n
    return out, at


CONST_AT, CONST_N = offsets(CONST_COLS)
PARAM_AT, PARAM_N = offsets(PARAM_COLS)


def shape_constants():
    c = np.zeros((P, CONST_N), np.float32)

    def put(name):
        a, n = CONST_AT[name]
        return c[:, a:a + n]

    p = np.arange(P)
    put("ident")[:] = np.eye(P)
    put("ones")[:] = 1.0
    put("tri")[:] = (p[:, None] <= p[None, :])
    put("iota")[:] = p[None, :]
    inv = (np.float32(10000.0) ** (-np.arange(32, dtype=np.float32) / np.float32(32))).astype(np.float32)
    for tc in range(TC):
        t = tc * P + p
        pos = np.where(t < NP_, t, np.where(t < T, PAST, 0)).astype(np.float32)
        ang = (pos[:, None] * inv[None, :]).astype(np.float32)
        put("cos")[:, tc * 32:tc * 32 + 32] = np.cos(ang)
        put("sin")[:, tc * 32:tc * 32 + 32] = np.sin(ang)
        init = np.where(np.arange(NP_)[None, :] <= t[:, None], 0.0, NEG)
        if tc == 2:
            init[32:40] = np.where(np.arange(NP_)[None, :] < SK, 0.0, NEG)
        put("init")[:, tc * NP_:(tc + 1) * NP_] = init
        put("valid")[:, tc] = t < T
    for b in range(NB):
        put("rsel")[32 + b, b * H:(b + 1) * H] = 1.0
        put("m24")[b * H:(b + 1) * H, 16 + b] = 1.0
        put("d8")[:, b * NB + b] = 1.0
    for g, w in enumerate(WINDOWS):
        put("rw")[:, g * 16:g * 16 + w - 1] = 1.0 / np.arange(1, w, dtype=np.float32)
    put("ecol")[:] = np.tile(np.arange(NE), 2)[None, :]
    return c


MIXER_UNITS = ["u", "qi", "kw", "q", "k", "v", "glu", "wout0", "wout1"]
DENSE_UNITS = [f"ffn{i}" for i in range(FT // 2)] + [f"down{i}" for i in range(C)] + ["pool"]
UNITS = MIXER_UNITS + DENSE_UNITS
UNIT_NO = {name: n for n, name in enumerate(UNITS)}


def slot_of(n):
    return SLOTS if UNITS[n] == "pool" else n % SLOTS


def slot_count(n):
    return sum(16 * (2 if UNITS[m].startswith("ffn") else 1)
               for m in range(n + 1) if slot_of(m) == slot_of(n))


def slot_before(n):
    earlier = [m for m in range(n) if slot_of(m) == slot_of(n)]
    return earlier[-1] if earlier else None


def last_fill(unit):
    if unit in ("qi", "q", "k", "v"):
        return (unit, TC - 1)
    if unit in ("u", "glu"):
        return (unit, 3)
    if unit.startswith("wout"):
        return ("wout", 4 * int(unit[4:]) + 3)
    if unit.startswith("ffn"):
        return ("up", 2 * int(unit[3:]) + 1)
    if unit.startswith("down"):
        return ("down", int(unit[4:]))
    return ("pool", C - 1) if unit == "pool" else unit


BANKS = 7


def fill_order():
    f = ["norm0"] + [("u", c) for c in range(4)]
    proj = [("qi", t) for t in range(TC)] + ["kw"] + [(n, t) for n in ("q", "k", "v") for t in range(TC)]
    j = 0
    for i, name in enumerate(proj):
        f.append(name)
        while j < NJ and j < (i + 1) * NJ / len(proj):
            f += [("bur", j), ("bui", j)]
            j += 1
    f += [("qiT", t) for t in range(TC)] + ["kiT", "wT"]
    for b in range(NB):
        f += [("skT", b), ("sdot", b)]
    f += [("dot", t, h) for t in range(TC) for h in range(H)]
    f += [("kT", t) for t in range(TC)] + [("qT", t) for t in range(TC)]
    f += [("y", c) for c in range(4)] + [("glu", c) for c in range(4)]
    for t in range(TC):
        f += [("logit", t, h) for h in range(H)]
        f += [("pT", t, i) for i in range(PT_FILLS[t])]
        f += [("att", t), ("attT", t)]
    for b in range(NB):
        f += [("cT", b, 0), ("cT", b, 1)]
    f += ["spT", "sself", "satt"]
    f += [("wout", c) for c in range(C)] + ["norm1"]
    for i in range(FT):
        f += [("gate", i), ("up", i)]
    f += [("down", c) for c in range(C)] + ["norm2", ("pnew", 0), ("pnew", 1)]
    f += [("pool", c) for c in range(C)] + ["norm3"]
    f += [("h2n", t, i) for t in range(TC) for i in range(2)]
    f += [("xn", t, i) for t in range(TC) for i in range(2)]
    f += ["router", "rank"]
    return f


def prob_blocks(t, i):
    heads = H // PT_FILLS[t]
    return [(h, kc) for h in range(heads * i, heads * (i + 1)) for kc in range(t + 1)]


PT_FILLS = [2, 4, 1]
FILLS = fill_order()
FILL_NO = {name: n for n, name in enumerate(FILLS)}
SAMPLE_BANK = 7


def bank_of(name):
    return SAMPLE_BANK if name in ("sscore", "slogit") else FILL_NO[name] % BANKS


def bank_uses(name):
    if name in ("sscore", "slogit"):
        return 1 if name == "sscore" else 2
    return FILL_NO[name] // BANKS + 1


PASS_FILLS = [[("gate", j) for j in range(0, FC, 2)], [("up", j) for j in range(0, FC, 2)],
              [("gate", j) for j in range(1, FC, 2)], [("up", j) for j in range(1, FC, 2)],
              [("gather", 1)] + [("hT", j) for j in range(FC)] + [("scatter", k) for k in (1, 3, 5)],
              [("y", 0)], [("y", 1)],
              [("gather", 0), "pickT"] + [("scatter", k) for k in (0, 2, 4)]]
PASS_BANK = {name: b for b, names in enumerate(PASS_FILLS) for name in names}
PASS_FILL_AT = {name: k for names in PASS_FILLS for k, name in enumerate(names)}
FIRST_FILL = [sum(bank_of(n) == b for n in FILLS) for b in range(BANKS)] + [2]
PASSES_EXTRA = 4
PASSES = NE + PASSES_EXTRA

BLOCK = 1024
PLACES = 7
AHEAD = 5
FF_PLACES = 4
FF_AHEAD = 3
FF_BLOCKS = 2 * FT
PASS_UNITS = []
for _j in range(FC):
    PASS_UNITS += [("gate", _j), ("up", _j)] + ([("down", _j - 1)] if _j else [])
PASS_UNITS += [("down", FC - 1)]
PASS_BLOCKS = [(kind, j, q) for kind, j in PASS_UNITS for q in range(4)]
NBLK = len(PASS_BLOCKS)
PASS_BLOCK_AT = {b: n for n, b in enumerate(PASS_BLOCKS)}
PASS_HALVES = NBLK // 2
RAW_USES = PASS_HALVES // PLACES


def hybrid_step(nc, a, o):
    with ExitStack() as ctx:
        sems = {}

        def sem(name):
            if name not in sems:
                sems[name] = ctx.enter_context(nc.semaphore(name))
            return sems[name]

        def sb(name, n, dt=F32):
            return ctx.enter_context(nc.sbuf_tensor(name, [P, n], dt))

        consts = sb("consts", CONST_N)
        M2 = 14100
        low = sb("low", M2)
        small = sb("small", 1300)
        small_i = sb("small_i", 64, I32)
        expo = sb("expo", NJ, I32)
        with ExitStack() as early:
            params, xT, hT, ring = [early.enter_context(nc.sbuf_tensor(name, [P, n], F32)) for name, n in (
                ("params", PARAM_N), ("xT", C * T), ("hT", C * T), ("ring", RING * SLOT))]
        xgr = sb("xgr", 2 * C * P, F32R)
        hbr = sb("hbr", 2 * 2 * 512, F32R)
        sb("under_hT", PARAM_N + 2 * C * T - 2 * C * P - 2 * 2 * 512)
        raw_w = sb("raw_w", PLACES * 2 * BLOCK)
        split = sb("split", PLACES * 2 * BLOCK, F32R)
        bank = [ctx.enter_context(nc.psum_tensor(f"bank{b}", [P, 512], F32)) for b in range(8)]
        bank_full = [sem(f"bank{b}_full") for b in range(8)]
        bank_free = [sem(f"bank{b}_free") for b in range(8)]
        slot_full = [sem(f"slot{s}_full") for s in range(SLOTS + 1)]

        def const(name):
            at, n = CONST_AT[name]
            return consts[:, at:at + n]

        def param(name):
            at, n = PARAM_AT[name]
            return params[:, at:at + n]

        def carve(tensor, start):
            at = [start]

            def take(n):
                v = tensor[:, at[0]:at[0] + n]
                at[0] += n
                return v
            return take, at

        x3 = xT[:, :].rearrange("p (c t) -> p c t", c=C)
        h3 = hT[:, :].rearrange("p (c t) -> p c t", c=C)
        ycat = h3
        ident, ones, iota = const("ident"), const("ones"), const("iota")
        cos3 = const("cos").rearrange("p (t d) -> p t d", t=TC)
        sin3 = const("sin").rearrange("p (t d) -> p t d", t=TC)
        init3 = const("init").rearrange("p (t k) -> p t k", t=TC)
        b_m = param("b").rearrange("p (j r s) -> p j r s", j=4, r=2)
        c_m = param("c").rearrange("p (j r s) -> p j r s", j=NJ, r=2)

        tk, _ = carve(small, 0)
        eps, nmax, rsum, rinv, mx8 = tk(1), tk(TC * H), tk(TC * H), tk(TC * H), tk(TC * 8)
        mx = tk(TC * H)
        qss, kss = tk(TC * H), tk(TC * H)
        smx, snm, srs, sri = tk(1), tk(1), tk(1), tk(1)
        dself = tk(24)
        wT = tk(24)
        wbd = tk(64)
        hs = tk(NJ * 2 * NB).rearrange("p (j r b) -> p j r b", j=NJ, r=2)
        raw = tk(NJ * 2 * NB).rearrange("p (j r b) -> p j r b", j=NJ, r=2)
        hlast = tk(2 * NJ)
        cur = tk(6)
        rt = [tk(24) for _ in range(8)]
        f16 = [tk(NJ) for _ in range(14)]

        tk, at = carve(low, 0)
        zqi, zq = tk(TC * 512), tk(TC * 512)
        zk, zv, zkid, zwi = tk(TC * 512), tk(TC * 512), tk(TC * 128), tk(TC * 8)
        cf = tk(NJ * 64)
        csn = tk(NJ * 32)
        qT, kT, qiT = tk(4 * T), tk(4 * T), tk(4 * T)
        qbd = tk(4 * NB * 64)
        sprob = tk(SK)
        tail = tk(2 * 128 + 64)
        psT, psd = tail[:, 0:128], tail[:, 128:192]
        assert at[0] <= M2, at
        etmp = low[:, at[0] - 320 - SK - 2048 - 12 * T:at[0] - 320 - SK - 2048 - 12 * T + 4096]
        rtmp = low[:, at[0] - 320 - SK - 2048:at[0]]
        ga, gb = rtmp[:, 0:4 * T], rtmp[:, 4 * T:8 * T]
        kcT = low[:, 0:2 * 4 * SK].rearrange("p (r c k) -> p r c k", r=2, c=4)
        assert 2 * 4 * SK <= 2 * TC * 512

        m1 = SLOTS * SLOT
        tk, at = carve(ring, m1)
        er, ei = tk(NJ * NP_), tk(NJ * NP_)
        er3, ei3 = er.rearrange("p (j t) -> p j t", j=NJ), ei.rearrange("p (j t) -> p j t", j=NJ)
        vr, vi, d1, d2, d3, d4 = [tk(NP_) for _ in range(6)]
        g4 = tk(4 * NP_).rearrange("p (r k t) -> p r k t", r=2, k=2)
        pt = [tk(NP_) for _ in range(4)]
        kin = tk(2 * 2 * 128).rearrange("p (r g d) -> p r g d", r=2, g=2)
        m1_dead = at[0]
        uT = tk(4 * T).rearrange("p (c t) -> p c t", c=4)
        sc = tk(TC * NP_).rearrange("p (t k) -> p t k", t=TC)
        relu = tk(2 * NP_).rearrange("p (r k) -> p r k", r=2)
        kiT = tk(T)
        kisT = tk(2 * SK).rearrange("p (r k) -> p r k", r=2)
        qibd = tk(NB * 8)
        assert at[0] <= RING * SLOT, at
        tk, at = carve(ring, m1)
        lg = [tk(H * KN[t]).rearrange("p (h k) -> p h k", h=H) for t in range(TC)]
        pT = [tk(1024), tk(2048), tk(384)]
        kb = tk(2 * 1024).rearrange("p (r g d) -> p r g d", r=2, g=2)
        vb = tk(2 * 1024).rearrange("p (r g d) -> p r g d", r=2, g=2)
        assert at[0] <= m1_dead, at
        def rb(b):
            return relu[:, b % 2, 0:SK]

        yn = relu.rearrange("p r k -> p (r k)")[:, 0:512]

        hff = low[:, 0:FT * T].rearrange("p (f t) -> p f t", f=FT)
        sq = low[:, FT * T:FT * T + C * T].rearrange("p (c t) -> p c t", c=C)
        std = low[:, FT * T + C * T:FT * T + C * T + T]
        rs = low[:, FT * T + C * T + T:FT * T + C * T + 2 * T]
        ffa = low[:, FT * T + C * T + 2 * T:FT * T + C * T + 6 * T].rearrange("p (r t) -> p r t", r=4)
        tk, at = carve(low, 0)
        win_a = tk(C * NP_).rearrange("p (c t) -> p c t", c=C)
        win_b = tk(C * NP_).rearrange("p (c t) -> p c t", c=C)
        assert at[0] <= FT * T
        tk, at = carve(low, FT * T + C * T + 6 * T)
        pl = tk(C * T).rearrange("p (c t) -> p c t", c=C)
        hist = tk(C * NB * 15).rearrange("p (c b r) -> p c b r", c=C, b=NB)
        assert at[0] <= M2, at
        ext = low[:, 2 * C * NP_:2 * C * NP_ + C * NB * 16].rearrange("p (c b r) -> p c b r", c=C, b=NB)
        pnew = low[:, FT * T + C * T + 2 * T:FT * T + C * T + 2 * T + D]
        assert 2 * C * NP_ + C * NB * 16 <= FT * T and D <= 4 * T
        tk, at = carve(low, 0)
        hn = tk(TC * D).rearrange("p (t d) -> p t d", t=TC)
        acc = tk(TC * D).rearrange("p (t d) -> p t d", t=TC)
        assert at[0] <= FT * T
        tk, at = carve(low, FT * T)
        xg4 = xgr[:, :].rearrange("p (h c s) -> p h c s", h=2, c=C)
        hb5 = hbr[:, :].rearrange("p (r h f s) -> p r h f s", r=2, h=2, f=4)
        place = split[:, :].rearrange("p (s h n) -> p s h n", s=PLACES, h=2)
        xs = split[:, FF_PLACES * 2 * BLOCK:FF_PLACES * 2 * BLOCK + 2 * C * T].rearrange(
            "p (h c t) -> p h c t", h=2, c=C)
        assert FF_PLACES * 2 * BLOCK + 2 * C * T <= PLACES * 2 * BLOCK
        pick = tk(TC * P).rearrange("p (t s) -> p t s", t=TC)
        pickT = tk(T)
        th = tk(2 * 512).rearrange("p (r k) -> p r k", r=2)
        hb = tk(2 * 512).rearrange("p (r k) -> p r k", r=2)
        yb = tk(D)
        sel, gate, slot_v, rk = [tk(TC * NE).rearrange("p (t e) -> p t e", t=TC) for _ in range(4)]
        pslot = tk(PASSES * TC).rearrange("p (i t) -> p i t", i=PASSES)
        pgate = tk(PASSES * TC).rearrange("p (i t) -> p i t", i=PASSES)
        pexp = tk(PASSES)
        cand = tk(TC * 16).rearrange("p (t b e) -> p t b e", t=TC, b=2)
        gcand = tk(TC * 16).rearrange("p (t b e) -> p t b e", t=TC, b=2)
        over, ranko = tk(16), tk(16)
        oh = tk(4 * 16).rearrange("p (k e) -> p k e", k=4)
        prod = tk(TC * 4 * 16).rearrange("p (t k e) -> p t k e", t=TC, k=4)
        idxf = tk(TC * 8).rearrange("p (t e) -> p t e", t=TC)
        oh1, oh2 = [tk(TC * NE).rearrange("p (t e) -> p t e", t=TC) for _ in range(2)]
        lgt = tk(TC * NE).rearrange("p (t e) -> p t e", t=TC)
        m8r = tk(TC * 8).rearrange("p (t e) -> p t e", t=TC)
        g12 = tk(4 * TC).rearrange("p (k t) -> p k t", k=4)
        assert at[0] <= M2, at
        exp_i, idx_u = small_i[:, 0:PASSES + 1], small_i[:, 16:40].bitcast(U32)
        pages = small_i[:, 48:64]

        def filled(eng, name):
            eng.wait_ge(bank_full[bank_of(name)], bank_uses(name))

        def emptied(eng, name):
            eng.wait_ge(bank_free[bank_of(name)], bank_uses(name))

        def pass_filled(eng, name, i):
            b = PASS_BANK[name]
            eng.wait_ge(bank_full[b], FIRST_FILL[b] + len(PASS_FILLS[b]) * i + PASS_FILL_AT[name] + 1)

        def pass_emptied(eng, name, i):
            b = PASS_BANK[name]
            eng.wait_ge(bank_free[b], FIRST_FILL[b] + len(PASS_FILLS[b]) * i + PASS_FILL_AT[name] + 1)

        def full(name):
            return bank_full[bank_of(name)]

        def free(name):
            return bank_free[bank_of(name)]

        def ps(name):
            return bank[bank_of(name)]

        def view(slot, width):
            return ring[:, slot * SLOT:slot * SLOT + (SLOT // width) * width].rearrange(
                "p (c n) -> p c n", n=width)

        def unit(name, width):
            return view(slot_of(UNIT_NO[name]), width)


        z4 = {n: v.rearrange("p (t h d) -> p t h d", t=TC, h=H)
              for n, v in (("q", zq), ("k", zk), ("v", zv), ("qi", zqi))}
        z3 = {n: v.rearrange("p (t n) -> p t n", t=TC)
              for n, v in (("q", zq), ("k", zk), ("v", zv), ("qi", zqi), ("kid", zkid), ("wi", zwi))}
        qT3, kT3, qiT3 = [v.rearrange("p (c t) -> p c t", c=4) for v in (qT, kT, qiT)]
        qbd4 = qbd.rearrange("p (c b m) -> p c b m", c=4, b=NB)
        qib3 = qibd.rearrange("p (b h) -> p b h", b=NB)
        cf4 = cf.rearrange("p (j r s) -> p j r s", j=NJ, r=2)
        csn3 = csn.rearrange("p (j s) -> p j s", j=NJ)
        lam_r, lam_i = param("lam_re"), param("lam_im")
        dt_, rad, rate, lbr, lbi, fr_, fi_, s1, s2, s3, sn, cn, ang, cang = f16


        block = ctx.enter_context(nc.Block())

        @block.sync
        def _(sp):
            def to_slot(n, dst, src):
                sp.dma_start(dst, src).then_inc(slot_full[slot_of(n)], 16)

            def load_unit(n):
                name = UNITS[n]
                if slot_before(n) is not None:
                    filled(sp, last_fill(UNITS[slot_before(n)]))
                elif n >= len(MIXER_UNITS):
                    sp.wait_ge(sem("mixer_over"), 1)
                w_in = a["w_in"].rearrange("(c p) n -> p c n", p=P)
                cols = {"u": 0, "q": 512, "k": 1024, "v": 1536, "qi": 2048}
                if name in cols:
                    to_slot(n, unit(name, 512)[:, 0:C, :], w_in[:, :, cols[name]:cols[name] + 512])
                elif name == "kw":
                    to_slot(n, unit(name, 72)[:, 0:C, :], w_in[:, :, 2560:2632])
                elif name == "glu":
                    to_slot(n, unit(name, 512)[:, 0:4, :], a["w_glu"].rearrange("(c p) n -> p c n", p=P))
                elif name.startswith("wout"):
                    at = int(name[4:]) * 512
                    to_slot(n, unit(name, 512)[:, 0:C, :],
                            a["w_out"].rearrange("(c p) n -> p c n", p=P)[:, :, at:at + 512])
                elif name.startswith("ffn"):
                    at = int(name[3:]) * 256
                    for k, w in enumerate(("w_gate", "w_up")):
                        sp.dma_start(unit(name, 256)[:, k * C:(k + 1) * C, :],
                                     a[w].rearrange("(c p) n -> p c n", p=P)[:, :, at:at + 256]
                                     ).then_inc(slot_full[slot_of(n)], 16)
                elif name.startswith("down"):
                    at = int(name[4:]) * P
                    to_slot(n, unit(name, P)[:, 0:FT, :],
                            a["w_down"].rearrange("(f p) n -> p f n", p=P)[:, :, at:at + P])
                else:
                    to_slot(n, unit(name, 256)[:, 0:C, :], a["pool_w"].rearrange("(c p) n -> p c n", p=P))

            for n in range(len(MIXER_UNITS)):
                load_unit(n)
                if n == 0:
                    sp.dma_start(pages[0:1, :], a["page_table"]).then_inc(sem("pages_in"), 16)
                    sp.wait_ge(sem("x_in"), 16)
                    sp.wait_ge(sem("consts_in"), 16)

            sp.wait_ge(sem("pages_in"), 16)
            for b in range(NB):
                if b >= 2:
                    filled(sp, ("skT", b - 2))
                for g in range(2):
                    page = sp.value_load(pages[0:1, 2 * b + g:2 * b + g + 1], min_val=0, max_val=a["n_pool"] - 1)
                    for half in range(2):
                        sp.dma_start(kin[:, b % 2, g, half * HD:half * HD + HD],
                                     a["cache_kidx"][bass.ds(page, 1), :, :].rearrange("o t d -> (o t) d")
                                     ).then_inc(sem(f"kidx_in{b % 2}"), 16)

            def load_pages(b, cache, dst, what):
                for g in range(2):
                    page = sp.value_load(pages[0:1, 2 * b + g:2 * b + g + 1], min_val=0, max_val=a["n_pool"] - 1)
                    sp.dma_start(dst[:, b % 2, g, :],
                                 a[cache][bass.ds(page, 1), :, :].rearrange("o t d -> (o t) d")
                                 ).then_inc(sem(f"{what}_in{b % 2}"), 16)

            filled(sp, ("y", 3))
            for b in range(NB):
                if b >= 2:
                    filled(sp, ("cT", b - 2, 1))
                load_pages(b, "cache_k", kb, "ck")
                if b < 2:
                    load_pages(b, "cache_v", vb, "cv")
            for b in range(2, NB):
                sp.wait_ge(sem("values_used"), b - 1)
                load_pages(b, "cache_v", vb, "cv")

            for n in range(len(MIXER_UNITS), len(UNITS)):
                load_unit(n)

            def expert_half(e, after, h):
                kind, j = PASS_UNITS[h // 2]
                k, s = h % 2, h % PLACES
                if kind == "down":
                    f = 4 * j + 2 * k
                    src = a["moe_down"].rearrange("e (f p) n -> p (e f) n", p=P)[:, bass.ds(e * (FE // P) + f, 2), :]
                else:
                    src = a["moe_" + kind][bass.ds(e, 1), k * 512:(k + 1) * 512, j * 512:(j + 1) * 512].rearrange(
                        "o (c p) n -> p (o c) n", p=P)
                dst = raw_w[:, s * 2 * BLOCK:(s + 1) * 2 * BLOCK].rearrange(
                    "p (c n) -> p c n", n=BLOCK if kind == "down" else 512)
                if after is not None:
                    sp.wait_ge(sem("low_ready"), after[0] + (after[1] + 2 * (h - PLACES) + 2))
                sp.dma_start(dst, src).then_inc(sem(f"raw{s}_full"), 16)

            def first_halves(e, after):
                for h in range(PLACES):
                    expert_half(e, after, h)

            def other_halves(e, after):
                for h in range(PLACES, PASS_HALVES):
                    expert_half(e, after, h)

            last_unit = {slot_of(n): name for n, name in enumerate(UNITS)}
            for h in range(PLACES):
                if h % 2 == 0:
                    filled(sp, last_fill(last_unit[h // 2]))
                expert_half(0, None, h)
            with sp.Fori(0, NE - 1) as i:
                other_halves(i, (NBLK * i, 0))
                first_halves(i + 1, (NBLK * i, NBLK))
            other_halves(NE - 1, (NBLK * (NE - 1), 0))
            sp.wait_ge(sem("passes_ready"), 1)
            n_pass = sp.value_load(exp_i[0:1, PASSES:PASSES + 1], min_val=NE, max_val=PASSES)
            with sp.If(n_pass > NE):
                with sp.Fori(NE, n_pass) as i:
                    e = sp.value_load(exp_i[0:1, bass.ds(i, 1)], min_val=0, max_val=NE - 1)
                    first_halves(e, (NBLK * i, 0))
                    other_halves(e, (NBLK * i, 0))

            for k in (2 * TC - 2, 2 * TC - 1):
                b = PASS_BANK[("scatter", k)]
                sp.wait_ge(bank_free[b], len(PASS_FILLS[b]) * n_pass + (FIRST_FILL[b] - len(PASS_FILLS[b]) + PASS_FILL_AT[("scatter", k)] + 1))
            for t in range(TC):
                sp.dma_start(o["y"][t * P:t * P + TCN[t], :], acc[0:TCN[t], t, :]).then_inc(sem("out"), 16)
            sp.wait_ge(sem("out"), 16 * TC)
            sp.wait_ge(sem("kv_out"), 16 * 2 * TC)
            sp.wait_ge(sem("ki_out"), 16 * TC)
            sp.wait_ge(sem("state_out"), 16 * 2)
            sp.wait_ge(sem("pool_out"), 16 * 2)
            sp.wait_ge(sem("pool_old_out"), 16)

        @block.gpsimd
        def _(pool):
            done = [0]

            def link(ins):
                done[0] += 1
                ins.then_inc(sem("pool_step"), 1)
                pool.wait_ge(sem("pool_step"), done[0])

            TT = nc.gpsimd.tensor_tensor
            nc.gpsimd.memset(eps, EPS)
            for v in ("q", "k", "v", "qi"):
                last = nc.gpsimd.memset(z3[v][:, 2, :], 0.0)
            nc.gpsimd.memset(qibd, 0.0).then_inc(sem("zeroed"), 1)
            filled(pool, "norm0")
            nc.gpsimd.memset(z3["kid"][:, 2, :], 0.0)
            nc.gpsimd.memset(z3["wi"][:, 2, :], 0.0).then_inc(sem("zeroed"), 1)
            pool.dma_start(o["pool_s"][:, 0:14, :], a["state_pool"][:, 1:15, :]).then_inc(sem("pool_old_out"), 16)
            for j in range(NJ):
                pool.wait_ge(sem("scanned"), j + 1)
                gr, gi = g4[:, j % 2, 0, :], g4[:, j % 2, 1, :]
                TT(pt[0], er3[:, j, :], gr, ALU.mult)
                TT(pt[1], ei3[:, j, :], gi, ALU.mult)
                TT(pt[2], er3[:, j, :], gi, ALU.mult)
                link(TT(pt[3], ei3[:, j, :], gr, ALU.mult))
                TT(er3[:, j, :], pt[0], pt[1], ALU.subtract)
                TT(ei3[:, j, :], pt[2], pt[3], ALU.add).then_inc(sem("states"), 1)
                pool.wait_ge(sem("states"), j + 1)
            pool.wait_ge(sem("kid_ready"), 1)
            for t in range(TC):
                pool.dma_start(o["kidx"][t * P:t * P + TCN[t], :], z3["kid"][0:TCN[t], t, 0:HD]).then_inc(sem("ki_out"), 16)
            pool.wait_ge(sem("qk_ready"), 2)
            for t in range(TC):
                for n in ("k", "v"):
                    if n == "v":
                        emptied(pool, ("v", t))
                    pool.dma_start(o[n][t * P:t * P + TCN[t], :], z3[n][0:TCN[t], t, :]).then_inc(sem("kv_out"), 16)
            pool.wait_ge(sem("sample_state"), 1)
            pool.dma_start(o["hs"], hs.rearrange("p j r b -> p (j r b)")).then_inc(sem("state_out"), 16)
            pool.wait_ge(sem("last_state"), 1)
            pool.dma_start(o["hl"], hlast).then_inc(sem("state_out"), 16)
            pool.wait_ge(sem("mixer_over"), 1)
            emptied(pool, "satt")
            pool.dma_start(hist.rearrange("p c b r -> p (c b r)"), a["hist"]).then_inc(sem("hist_in"), 16)

        @block.tensor
        def _(pe):
            mm = nc.tensor.matmul

            def open_fill(name):
                if bank_uses(name) > 1:
                    pe.wait_ge(bank_free[bank_of(name)], bank_uses(name) - 1)
                return ps(name)

            def unit_there(name):
                n = UNIT_NO[name]
                pe.wait_ge(slot_full[slot_of(n)], slot_count(n))

            def norm_sums(k):
                out = open_fill(f"norm{k}")
                for c in range(C):
                    pe.wait_ge(sem("squares"), C * k + c + 1)
                    last = mm(out[:, 0:T], ones, sq[:, c, :], start=(c == 0), stop=(c == C - 1))
                    if k == 3 and c == 0:
                        last.then_inc(sem("blocks_begun"), PLACES)
                last.then_inc(full(f"norm{k}"), 1)

            def blocks_T(name, src, n, count, step=P):
                out = open_fill(name)
                for i in range(count):
                    last = nc.tensor.transpose(out[0:step, i * P:i * P + n], src[0:n, i * step:(i + 1) * step],
                                               ident[0:n, 0:n])
                last.then_inc(full(name), 1)

            pe.wait_ge(sem("consts_in"), 16)
            norm_sums(0)
            unit_there("u")
            w = unit("u", 512)
            for co in range(4):
                out = open_fill(("u", co))
                for c in range(C):
                    if co == 0:
                        pe.wait_ge(sem("normed"), c + 1)
                    last = mm(out[:, 0:T], w[:, c, co * P:(co + 1) * P], h3[:, c, :], start=(c == 0), stop=(c == C - 1))
                last.then_inc(full(("u", co)), 1)

            def project(name, width, t, out):
                w = unit(name, width)
                for c in range(C):
                    last = mm(out[0:TCN[t], 0:width], h3[:, c, t * P:t * P + TCN[t]], w[:, c, :],
                              start=(c == 0), stop=(c == C - 1))
                return last

            def state_inputs(j):
                emptied(pe, ("u", j // 4))
                if j == 0:
                    pe.wait_ge(sem("mats_in"), 16)
                rows = slice(32 * (j % 4), 32 * (j % 4) + 32)
                for r, name in enumerate((("bur", j), ("bui", j))):
                    out = open_fill(name)
                    mm(out[:, 0:T], b_m[rows, j // 4, r, :], uT[rows, j // 4, :],
                       start=True, stop=True).then_inc(full(name), 1)

            for name in FILLS[FILL_NO[("qi", 0)]:FILL_NO[("qiT", 0)]]:
                if name == "kw":
                    unit_there("kw")
                    out = open_fill(name)
                    for t in range(TC):
                        last = project("kw", 72, t, out[:, 72 * t:72 * t + 72])
                    last.then_inc(full(name), 1)
                elif name[0] == "bur":
                    state_inputs(name[1])
                elif name[0] != "bui":
                    unit_there(name[0])
                    project(name[0], 512, name[1], open_fill(name)).then_inc(full(name), 1)

            pe.wait_ge(sem("qi_ready"), 1)
            for t in range(TC):
                blocks_T(("qiT", t), z3["qi"][:, t, :], TCN[t], 4)
            pe.wait_ge(sem("kid_ready"), 1)
            out = open_fill("kiT")
            for t in range(TC):
                last = nc.tensor.transpose(out[:, t * P:t * P + TCN[t]], z3["kid"][0:TCN[t], t, :],
                                           ident[0:TCN[t], 0:TCN[t]])
            last.then_inc(full("kiT"), 1)
            blocks_T("wT", z3["wi"][:, 2, :], TCN[2], 1, H)

            def add_sample_scores(b):
                emptied(pe, ("sdot", b))
                last = mm(ps("sscore")[32:40, 0:SK], wbd[0:H, b * NB:(b + 1) * NB], rb(b)[0:H, :],
                          start=(b == 0), stop=(b == NB - 1))
                last.then_inc(full("sscore") if b == NB - 1 else sem("sample_scored"), 1)

            for b in range(NB):
                pe.wait_ge(sem(f"kidx_in{b % 2}"), 64 * (b // 2 + 1))
                blocks_T(("skT", b), kin[:, b % 2, :, :].rearrange("p g d -> p (g d)"), P, 2)
                if b == 0:
                    pe.wait_ge(sem("sample_index_q"), 1)
                else:
                    add_sample_scores(b - 1)
                emptied(pe, ("skT", b))
                out = open_fill(("sdot", b))
                mm(out[0:H, 0:SK], qib3[:, b, :], kisT[:, b % 2, :], start=True, stop=True).then_inc(full(("sdot", b)), 1)
            add_sample_scores(NB - 1)

            emptied(pe, "kiT")
            for t in range(TC):
                emptied(pe, ("qiT", t))
                for h in range(H):
                    half = slice(HD * (h % 2), HD * (h % 2) + HD)
                    out = open_fill(("dot", t, h))
                    mm(out[0:QN[t], 0:KN[t]], qiT3[half, h // 2, t * P:t * P + QN[t]], kiT[half, 0:KN[t]],
                       start=True, stop=True).then_inc(full(("dot", t, h)), 1)

            pe.wait_ge(sem("qk_ready"), 2)
            for t in range(TC):
                blocks_T(("kT", t), z3["k"][:, t, :], TCN[t], 4)
            for t in range(TC):
                blocks_T(("qT", t), z3["q"][:, t, :], TCN[t], 4)

            pe.wait_ge(sem("out_mats"), 1)
            pe.wait_ge(sem("sample_state"), 1)
            for jc in range(4):
                out = open_fill(("y", jc))
                pe.wait_ge(sem("states"), 4 * jc + 4)
                for q in range(4):
                    j, rows = 4 * jc + q, slice(32 * q, 32 * q + 32)
                    mm(out[rows, 0:NP_], cf4[:, j, 0, :], er3[:, j, :], start=True, stop=False)
                    mm(out[rows, 0:NP_], cf4[:, j, 1, :], ei3[:, j, :], start=False, stop=True)
                    mm(out[rows, NP_:T], c_m[:, j, 0, :], hs[:, j, 0, :], start=True, stop=False)
                    last = mm(out[rows, NP_:T], csn3[:, j, :], hs[:, j, 1, :], start=False, stop=True)
                last.then_inc(full(("y", jc)), 1)
            unit_there("glu")
            w = unit("glu", 512)
            pe.wait_ge(sem("gelu"), 1)
            for co in range(4):
                out = open_fill(("glu", co))
                for c in range(4):
                    last = mm(out[:, 0:T], w[:, c, co * P:(co + 1) * P], uT[:, c, :], start=(c == 0), stop=(c == 3))
                last.then_inc(full(("glu", co)), 1)

            for t in range(TC):
                emptied(pe, ("kT", t))
            for t in range(TC):
                nq = QN[t]
                emptied(pe, ("qT", t))
                for h in range(H):
                    half = slice(HD * (h % 2), HD * (h % 2) + HD)
                    out = open_fill(("logit", t, h))
                    mm(out[0:nq, 0:KN[t]], qT3[half, h // 2, t * P:t * P + nq], kT3[half, h // 2, 0:KN[t]],
                       start=True, stop=True).then_inc(full(("logit", t, h)), 1)
                heads = H // PT_FILLS[t]
                for i in range(PT_FILLS[t]):
                    out = open_fill(("pT", t, i))
                    pe.wait_ge(sem("probs"), H * t + heads * (i + 1))
                    for n, (h, kc) in enumerate(prob_blocks(t, i)):
                        kn = min(P, KN[t] - kc * P)
                        last = nc.tensor.transpose(out[0:kn, n * nq:(n + 1) * nq], lg[t][0:nq, h, kc * P:kc * P + kn],
                                                   ident[0:nq, 0:nq])
                    last.then_inc(full(("pT", t, i)), 1)
                out = open_fill(("att", t))
                for i in range(PT_FILLS[t]):
                    emptied(pe, ("pT", t, i))
                for h in range(H):
                    for kc in range(t + 1):
                        kn, n = min(P, KN[t] - kc * P), h * (t + 1) + kc
                        last = mm(out[0:nq, h * HD:(h + 1) * HD], pT[t][0:kn, n * nq:(n + 1) * nq],
                                  z3["v"][0:kn, kc, h * HD:(h + 1) * HD], start=(kc == 0), stop=(kc == t))
                last.then_inc(full(("att", t)), 1)
                emptied(pe, ("att", t))
                blocks_T(("attT", t), yn, nq, 4)

            pe.wait_ge(sem("sample_q"), 1)
            emptied(pe, "sscore")
            slog = ps("slogit")
            for b in range(NB):
                pe.wait_ge(sem(f"ck_in{b % 2}"), 32 * (b // 2 + 1))
                for g in range(2):
                    blocks_T(("cT", b, g), kb[:, b % 2, g, :], P, 4)
                emptied(pe, ("cT", b, 1))
                emptied(pe, ("cT", b, 0))
                for c in range(4):
                    last = mm(slog[0:64, 0:SK], qbd4[:, c, b, :], kcT[:, b % 2, c, :], start=(b == 0 and c == 0), stop=False)
                last.then_inc(sem("sample_logits"), 1)
            mm(slog[0:64, 0:SK], const("rsel")[32:40, :], sc[32:40, 2, 0:SK], start=False, stop=True).then_inc(full("slogit"), 1)
            pe.wait_ge(sem("sample_probs"), 1)
            out = open_fill("spT")
            for g in range(2):
                last = nc.tensor.transpose(out[:, g * 64:(g + 1) * 64], sprob[0:64, g * P:(g + 1) * P], ident[0:64, 0:64])
            last.then_inc(full("spT"), 1)
            out = open_fill("sself")
            nc.tensor.transpose(out[0:24, 0:64], dself[0:64, :], ident[0:64, 0:64]).then_inc(full("sself"), 1)
            emptied(pe, "spT")
            emptied(pe, "sself")
            out = open_fill("satt")
            for b in range(NB):
                pe.wait_ge(sem(f"cv_in{b % 2}"), 32 * (b // 2 + 1))
                for c in range(4):
                    cols = slice(b * H + 2 * c, b * H + 2 * c + 2)
                    for g in range(2):
                        last = mm(out[:, cols], vb[:, b % 2, g, c * P:(c + 1) * P],
                                  psT[:, g * 64 + b * H + 2 * c:g * 64 + b * H + 2 * c + 2], start=(g == 0), stop=False)
                    last = mm(out[:, cols], z3["v"][0:24, 2, c * P:(c + 1) * P], psd[0:24, cols], start=False, stop=True)
                last.then_inc(full("satt") if b == NB - 1 else sem("values_used"), 1)

            for co in range(C):
                if co % 4 == 0:
                    unit_there(f"wout{co // 4}")
                w = unit(f"wout{co // 4}", 512)
                out = open_fill(("wout", co))
                if co == 0:
                    pe.wait_ge(sem("ssm_out"), 1)
                    for t in range(TC):
                        emptied(pe, ("attT", t))
                    emptied(pe, "satt")
                for c in range(C):
                    last = mm(out[:, 0:T], w[:, c, (co % 4) * P:(co % 4) * P + P], ycat[:, c, :],
                              start=(c == 0), stop=(c == C - 1))
                    if co == 0 and c == 0:
                        last.then_inc(sem("mixer_over"), 1)
                last.then_inc(full(("wout", co)), 1)

            norm_sums(1)
            for f in range(FT):
                for k, kind in enumerate(("gate", "up")):
                    out = open_fill((kind, f))
                    n = 2 * f + k
                    pe.wait_ge(sem("ff_low_ready"), n + 1)
                    w = [place[:, n % FF_PLACES, half, :].rearrange("p (c m) -> p c m", c=C) for half in range(2)]
                    for c in range(C):
                        if n == 0:
                            pe.wait_ge(sem("xs_low"), c + 1)
                        first = mm(out[:, 0:T], w[0][:, c, :], xs[:, 0, c, :], start=(c == 0), stop=False)
                        if c == 0:
                            first.then_inc(sem("ff_begun"), 1)
                        mm(out[:, 0:T], w[0][:, c, :], xs[:, 1, c, :], start=False, stop=False)
                        last = mm(out[:, 0:T], w[1][:, c, :], xs[:, 0, c, :], start=False, stop=(c == C - 1))
                    last.then_inc(full((kind, f)), 1)
            for co in range(C):
                unit_there(f"down{co}")
                w = unit(f"down{co}", P)
                out = open_fill(("down", co))
                for f in range(FT):
                    if co == 0:
                        emptied(pe, ("up", f))
                    last = mm(out[:, 0:T], w[:, f, :], hff[:, f, :], start=(f == 0), stop=(f == FT - 1))
                last.then_inc(full(("down", co)), 1)

            norm_sums(2)
            pe.wait_ge(sem("normed"), 3 * C)
            for i in range(2):
                out = open_fill(("pnew", i))
                for q in range(4):
                    last = nc.tensor.transpose(out[0:23, q * P:(q + 1) * P], h3[:, 4 * i + q, T - 23:T], ident)
                last.then_inc(full(("pnew", i)), 1)
            unit_there("pool")
            w = unit("pool", 256)
            for co in range(C):
                g = co // 2
                out = open_fill(("pool", co))
                pe.wait_ge(sem("pooled"), g + 1)
                for c in (2 * g, 2 * g + 1):
                    last = mm(out[:, 0:T], w[:, c, (co % 2) * P:(co % 2) * P + P], pl[:, c, :],
                              start=(c == 2 * g), stop=(c == 2 * g + 1))
                last.then_inc(full(("pool", co)), 1)

            norm_sums(3)
            pe.wait_ge(sem("normed"), 4 * C)
            for kind, src in (("h2n", h3), ("xn", x3)):
                for t in range(TC):
                    for i in range(2):
                        out = open_fill((kind, t, i))
                        for q in range(4):
                            last = nc.tensor.transpose(out[0:TCN[t], q * P:(q + 1) * P],
                                                       src[:, 4 * i + q, t * P:t * P + TCN[t]], ident)
                        last.then_inc(full((kind, t, i)), 1)
            rw = param("router").rearrange("p (c e) -> p c e", c=C)
            out = open_fill("router")
            for t in range(TC):
                for c in range(C):
                    last = mm(out[0:TCN[t], t * NE:(t + 1) * NE], h3[:, c, t * P:t * P + TCN[t]], rw[:, c, :],
                              start=(c == 0), stop=(c == C - 1))
            last.then_inc(full("router"), 1)
            out = open_fill("rank")
            pe.wait_ge(sem("picked"), 1)
            for t in range(TC + 1):
                for u in range(min(t + 1, TC)):
                    last = mm(out[:, t * NE:(t + 1) * NE], const("tri") if u == t else ones, sel[:, u, :],
                              start=(u == 0), stop=(u == min(t, TC - 1)))
            last.then_inc(full("rank"), 1)

            pe.wait_ge(sem("passes_ready"), 1)
            for i in range(2):
                emptied(pe, ("xn", 2, i))
            n_pass = pe.value_load(exp_i[0:1, PASSES:PASSES + 1], min_val=NE, max_val=PASSES)
            with pe.Fori(0, n_pass) as i:
                def open_pass(name):
                    b = PASS_BANK[name]
                    pe.wait_ge(bank_free[b], FIRST_FILL[b] + len(PASS_FILLS[b]) * i + PASS_FILL_AT[name])
                    return bank[b]

                def pfull(name):
                    return bank_full[PASS_BANK[name]]

                def split_mm(outs, n, xs):
                    pe.wait_ge(sem("low_ready"), NBLK * i + n + 1)
                    s = n % PLACES
                    begun = False
                    for hi, lo, out, cols, start, stop in xs:
                        first = mm(out, hi, place[:, s, 0, cols], start=start, stop=False)
                        if not begun:
                            first.then_inc(sem("blocks_begun"), 1)
                            begun = True
                        mm(out, lo, place[:, s, 0, cols], start=False, stop=False)
                        last = mm(out, hi, place[:, s, 1, cols], start=False, stop=stop)
                        if stop:
                            last.then_inc(outs, 1) if not isinstance(outs, dict) else last.then_inc(outs[cols.start], 1)

                def down_block(j, f):
                    n = PASS_BLOCK_AT[("down", j, f)]
                    if j == 0 and f == 0:
                        for half in range(2):
                            open_pass(("y", half))
                    ys = [bank[PASS_BANK[("y", half)]] for half in range(2)]
                    split_mm({0: pfull(("y", 0)), 512: pfull(("y", 1))}, n,
                             [(hb5[:, j % 2, 0, f, :], hb5[:, j % 2, 1, f, :], ys[half][:, :],
                               slice(512 * half, 512 * half + 512), j == 0 and f == 0, j == FC - 1 and f == 3)
                              for half in range(2)])

                def hidden_T(j):
                    out = open_pass(("hT", j))
                    pass_emptied(pe, ("up", j), i)
                    for f in range(4):
                        last = nc.tensor.transpose(out[:, f * P:(f + 1) * P], hb[:, j % 2, f * P:(f + 1) * P], ident)
                    last.then_inc(pfull(("hT", j)), 1)

                for half in range(2):
                    out = open_pass(("gather", half))
                    if half == 0:
                        pe.wait_ge(sem("pick_ready"), i + 1)
                    for q in range(4):
                        for t in range(TC):
                            n = TCN[t]
                            last = mm(out[:, q * P:(q + 1) * P], hn[0:n, t, (4 * half + q) * P:(4 * half + q + 1) * P],
                                      pick[0:n, t, :], start=(t == 0), stop=(t == TC - 1))
                    last.then_inc(pfull(("gather", half)), 1)
                for half in range(2):
                    pass_emptied(pe, ("gather", half), i)
                for kind, j in PASS_UNITS:
                    if kind == "down":
                        pass_emptied(pe, ("hT", j), i)
                    else:
                        out = open_pass((kind, j))
                    for q in range(4):
                        if kind == "down":
                            down_block(j, q)
                        else:
                            split_mm(pfull((kind, j)), PASS_BLOCK_AT[(kind, j, q)],
                                     [(xg4[:, 0, c, :], xg4[:, 1, c, :], out[:, :], slice(512 * (c % 2), 512 * (c % 2) + 512),
                                       c == 0, c == C - 1) for c in (2 * q, 2 * q + 1)])
                        if (kind, j, q) == ("down", FC - 2, 1):
                            hidden_T(FC - 1)
                    if kind == "gate" and j == 0:
                        out = open_pass("pickT")
                        for t in range(TC):
                            last = nc.tensor.transpose(out[:, t * P:t * P + TCN[t]], pick[0:TCN[t], t, :],
                                                       ident[0:TCN[t], 0:TCN[t]])
                        last.then_inc(pfull("pickT"), 1)
                    elif kind == "gate":
                        hidden_T(j - 1)
                pass_emptied(pe, "pickT", i)
                for half in range(2):
                    pass_emptied(pe, ("y", half), i)
                for k in range(2 * TC):
                    t, half = k // 2, k % 2
                    out = open_pass(("scatter", k))
                    mm(out[0:TCN[t], :], pickT[:, t * P:t * P + TCN[t]], yb[:, half * 512:(half + 1) * 512],
                       start=True, stop=True).then_inc(pfull(("scatter", k)), 1)

        @block.scalar
        def _(act):
            A = nc.scalar.activation

            first = PARAM_AT["h0r"][0]
            act.dma_start(params[:, 0:first], a["params"][:, 0:first]).then_inc(sem("params_in"), 16)
            act.dma_start(xT[:, :], a["x"]).then_inc(sem("x_in"), 16)
            act.dma_start(consts[:, :], a["consts"]).then_inc(sem("consts_in"), 16)
            act.dma_start(params[:, first:], a["params"][:, first:]).then_inc(sem("mats_in"), 16)

            def squares(k, ready):
                for c in range(C):
                    ready(c)
                    A(sq[:, c, :], x3[:, c, :], ACT.Square).then_inc(sem("squares"), 1)

            def root(k):
                filled(act, f"norm{k}")
                A(std, ps(f"norm{k}")[:, 0:T], ACT.Sqrt, bias=eps, scale=1.0 / D).then_inc(free(f"norm{k}"), 1)

            def copy_out(name, dst, src=None, n=512, inc=True, scale=1.0):
                ins = A(dst, ps(name)[:, 0:n] if src is None else src, ACT.Copy, scale=scale)
                if inc:
                    ins.then_inc(free(name), 1)

            act.wait_ge(sem("x_in"), 16)
            act.wait_ge(sem("zeroed"), 1)
            squares(0, lambda c: None)
            act.wait_ge(sem("angles"), 1)
            A(sn, ang, ACT.Sin)
            A(cn, cang, ACT.Sin).then_inc(sem("sincos"), 1)
            root(0)
            for c in range(4):
                filled(act, ("u", c))
                copy_out(("u", c), uT[:, c, :], n=T)
            for name in FILLS[FILL_NO[("qi", 0)]:FILL_NO[("qiT", 0)]]:
                if name == "kw":
                    filled(act, name)
                    act.wait_ge(sem("zeroed"), 2)
                    kw = ps(name)[:, 0:216].rearrange("p (t n) -> p t n", t=TC)
                    A(z3["kid"][:, 0:2, 0:HD], kw[:, 0:2, 0:HD], ACT.Copy)
                    A(z3["kid"][0:24, 2, 0:HD], kw[0:24, 2, 0:HD], ACT.Copy)
                    A(z3["wi"][:, 0:2, :], kw[:, 0:2, HD:HD + H], ACT.Copy, scale=H ** -0.5)
                    A(z3["wi"][0:24, 2, :], kw[0:24, 2, HD:HD + H], ACT.Copy, scale=H ** -0.5).then_inc(free(name), 1)
                elif name[0] not in ("bur", "bui"):
                    filled(act, name)
                    n = TCN[name[1]]
                    copy_out(name, z3[name[0]][0:n, name[1], :], ps(name)[0:n, :])
            def copy_T(name, dst, t, n=None):
                n = n or TCN[t]
                filled(act, name)
                copy_out(name, dst[:, 0:4, t * P:t * P + n],
                         ps(name)[:, :].rearrange("p (c t) -> p c t", c=4)[:, :, 0:n])

            for t in range(TC):
                copy_T(("qiT", t), qiT3, t)
            filled(act, "kiT")
            copy_out("kiT", kiT, n=T)
            filled(act, "wT")
            copy_out("wT", wT[0:H, :], ps("wT")[0:H, 0:24])
            for k, ss in enumerate((qss, kss)):
                act.wait_ge(sem("qk_squares"), k + 1)
                A(ss, ss, ACT.Sqrt, bias=eps, scale=1.0 / HD).then_inc(sem("qk_roots"), 1)
            emptied(act, "kiT")
            for b in range(NB):
                filled(act, ("skT", b))
                if b >= 2:
                    filled(act, ("sdot", b - 2))
                A(kisT[:, b % 2, PAST:SK], kiT[:, NP_ + b:NP_ + b + 1], ACT.Copy)
                copy_out(("skT", b), kisT[:, b % 2, 0:PAST], n=PAST)
                filled(act, ("sdot", b))
                if b >= 2:
                    act.wait_ge(sem("sample_scored"), b - 1)
                A(rb(b)[0:H, :], ps(("sdot", b))[0:H, 0:SK], ACT.Relu, scale=HD ** -0.5).then_inc(free(("sdot", b)), 1)
            filled(act, "sscore")
            for t in range(TC):
                for h in range(H):
                    n = H * t + h
                    filled(act, ("dot", t, h))
                    if n >= 2:
                        act.wait_ge(sem("scored"), n - 1)
                    A(relu[0:QN[t], n % 2, 0:KN[t]], ps(("dot", t, h))[0:QN[t], 0:KN[t]], ACT.Relu,
                      scale=HD ** -0.5).then_inc(free(("dot", t, h)), 1)
            for t in range(TC):
                copy_T(("kT", t), kT3, t)
            for t in range(TC):
                copy_T(("qT", t), qT3, t)

            act.wait_ge(sem("gelu_arg"), 1)
            A(gb, ga, ACT.Tanh, scale=GELU_C).then_inc(sem("gelu_tanh"), 1)
            for c in range(4):
                filled(act, ("glu", c))
                A(ga[:, c * T:(c + 1) * T], ps(("glu", c))[:, 0:T], ACT.Tanh, scale=0.5).then_inc(free(("glu", c)), 1)

            for t in range(TC):
                nq = QN[t]
                act.wait_ge(sem("nmax"), t + 1)
                for h in range(H):
                    A(lg[t][0:nq, h, :], lg[t][0:nq, h, :], ACT.Exp, bias=nmax[0:nq, H * t + h:H * t + h + 1],
                      scale=HD ** -0.5, accum_out=rsum[0:nq, H * t + h:H * t + h + 1]).then_inc(sem("probs"), 1)
                for i in range(PT_FILLS[t]):
                    name = ("pT", t, i)
                    filled(act, name)
                    if t < 2:
                        copy_out(name, pT[t][:, i * 512:(i + 1) * 512])
                    else:
                        src = ps(name)[:, 0:384].rearrange("p (h k q) -> p h k q", h=H, k=TC)
                        dst = pT[t].rearrange("p (h k q) -> p h k q", h=H, k=TC)
                        copy_out(name, dst[:, :, 0:2, :], src[:, :, 0:2, :], inc=False)
                        copy_out(name, dst[0:16, :, 2, :], src[0:16, :, 2, :])
                copy_T(("attT", t), ycat[:, 4:8, :], t, nq)

            for b in range(NB):
                if b >= 2:
                    act.wait_ge(sem("sample_logits"), b - 1)
                A(kcT[:, b % 2, :, PAST:SK], kT3[:, :, NP_ + b:NP_ + b + 1], ACT.Copy)
                for g in range(2):
                    name = ("cT", b, g)
                    filled(act, name)
                    copy_out(name, kcT[:, b % 2, :, g * P:(g + 1) * P],
                             ps(name)[:, :].rearrange("p (c t) -> p c t", c=4))
            act.wait_ge(sem("sample_max"), 1)
            A(sprob[0:64, :], ps("slogit")[0:64, 0:SK], ACT.Exp, bias=snm[0:64, :], scale=HD ** -0.5,
              accum_out=srs[0:64, :]).then_inc(free("slogit"), 1)
            filled(act, "spT")
            copy_out("spT", psT, n=P)
            filled(act, "sself")
            copy_out("sself", psd[0:24, :], ps("sself")[0:24, 0:64])

            act.wait_ge(sem("ki_out"), 16 * TC)
            act.wait_ge(sem("kv_out"), 16 * 2 * TC)
            def ff_high(n):
                f, k = n // 2, n % 2
                name = f"ffn{f // 2}"
                if n % 4 == 0:
                    act.wait_ge(slot_full[slot_of(UNIT_NO[name])], slot_count(UNIT_NO[name]))
                if n < FF_PLACES:
                    act.wait_ge(sem("mixer_over"), 1)
                else:
                    act.wait_ge(sem("ff_begun"), n - FF_PLACES + 2)
                A(place[:, n % FF_PLACES, 0, :].rearrange("p (c m) -> p c m", c=C),
                  unit(name, 256)[:, k * C:(k + 1) * C, (f % 2) * P:(f % 2) * P + P], ACT.Copy
                  ).then_inc(sem("ff_high_ready"), 1)

            for n in range(FF_AHEAD):
                ff_high(n)
            squares(1, lambda c: emptied(act, ("wout", c)))
            root(1)
            for c in range(C):
                act.wait_ge(sem("normed"), C + c + 1)
                A(xs[:, 0, c, :], h3[:, c, :], ACT.Copy).then_inc(sem("xs_high"), 1)
            for f in range(FT):
                for n in (2 * f + FF_AHEAD, 2 * f + FF_AHEAD + 1):
                    if n < FF_BLOCKS:
                        ff_high(n)
                filled(act, ("gate", f))
                if f >= 2:
                    emptied(act, ("up", f - 2))
                A(ffa[:, f % 2, :], ps(("gate", f))[:, 0:T], ACT.Silu).then_inc(free(("gate", f)), 1)
            squares(2, lambda c: emptied(act, ("down", c)))
            root(2)
            for i in range(2):
                filled(act, ("pnew", i))
                copy_out(("pnew", i), pnew[0:23, i * 512:(i + 1) * 512], ps(("pnew", i))[0:23, :])
            emptied(act, ("pnew", 1))
            act.dma_start(o["pool_p"], pnew[0:15, :]).then_inc(sem("pool_out"), 16)
            act.dma_start(o["pool_s"][:, 14, :], pnew[15:23, :]).then_inc(sem("pool_out"), 16)
            squares(3, lambda c: emptied(act, ("pool", c)))
            root(3)
            act.wait_ge(sem("pool_out"), 32)
            for kind, dst in (("h2n", hn), ("xn", acc)):
                for t in range(TC):
                    for i in range(2):
                        filled(act, (kind, t, i))
                        n = TCN[t]
                        copy_out((kind, t, i), dst[0:n, t, i * 512:(i + 1) * 512], ps((kind, t, i))[0:n, :])
            act.wait_ge(sem("router_gap"), 1)
            A(g12[:, 1, :], g12[:, 0, :], ACT.Exp).then_inc(sem("router_exp"), 1)

            act.wait_ge(sem("passes_ready"), 1)
            n_pass = act.value_load(exp_i[0:1, PASSES:PASSES + 1], min_val=NE, max_val=PASSES)
            with act.Fori(0, n_pass) as i:
                def take(name, dst, src):
                    pass_filled(act, name, i)
                    A(dst, src, ACT.Copy).then_inc(bank_free[PASS_BANK[name]], 1)

                def high_part(n):
                    s, h = n % PLACES, n // 2
                    if n % 2 == 0:
                        act.wait_ge(sem(f"raw{h % PLACES}_full"), 16 * RAW_USES * i + 16 * (h // PLACES + 1))
                    act.wait_ge(sem("blocks_begun"), NBLK * i + n + 2)
                    at = (h % PLACES) * 2 * BLOCK + (n % 2) * BLOCK
                    A(place[:, s, 0, :], raw_w[:, at:at + BLOCK], ACT.Copy).then_inc(sem("high_ready"), 1)

                def high_copy(name, dst, src):
                    pass_filled(act, name, i)
                    A(dst, src, ACT.Copy).then_inc(sem("high_copied"), 1)

                def hidden_high(j):
                    high_copy(("hT", j), hb5[:, j % 2, 0, :, :],
                              bank[PASS_BANK[("hT", 0)]][:, :].rearrange("p (f s) -> p f s", f=4))

                for n in range(AHEAD):
                    high_part(n)
                for half in range(2):
                    high_copy(("gather", half), xg4[:, 0, 4 * half:4 * half + 4, :],
                              bank[PASS_BANK[("gather", half)]][:, :].rearrange("p (c s) -> p c s", c=4))
                for n, (kind, j, q) in enumerate(PASS_BLOCKS):
                    if n + AHEAD < NBLK:
                        high_part(n + AHEAD)
                    if kind == "gate" and q == 3:
                        if j >= 2:
                            pass_emptied(act, ("up", j - 2), i)
                        pass_filled(act, ("gate", j), i)
                        b = PASS_BANK[("gate", j)]
                        A(th[:, j % 2, :], bank[b][:, :], ACT.Silu).then_inc(bank_free[b], 1)
                        if j == 0:
                            take("pickT", pickT, bank[PASS_BANK["pickT"]][:, 0:T])
                        else:
                            hidden_high(j - 1)
                    if (kind, j, q) == ("down", FC - 2, 2):
                        hidden_high(FC - 1)
                for half in range(2):
                    take(("y", half), yb[:, half * 512:(half + 1) * 512], bank[PASS_BANK[("y", half)]][:, :])

        @block.vector
        def _(dve):
            TT, TS, STT = nc.vector.tensor_tensor, nc.vector.tensor_scalar, nc.vector.scalar_tensor_tensor
            done = [0]

            def link(ins):
                done[0] += 1
                ins.then_inc(sem("dve_step"), 1)
                dve.wait_ge(sem("dve_step"), done[0])

            def norm(k, g):
                emptied(dve, f"norm{k}")
                link(nc.vector.reciprocal(rs, std))
                for c in range(C):
                    STT(h3[:, c, :], x3[:, c, :], g[:, c:c + 1], rs, ALU.mult, ALU.mult).then_inc(sem("normed"), 1)

            def whole_exp(dst, x, t0, t1, t2):
                link(TS(t0, x, 1.4426950408889634, MAGIC, ALU.mult, ALU.add))
                link(TS(t0, t0, -MAGIC, -126.0, ALU.add, ALU.max))
                link(TS(t0, t0, 127.0, None, ALU.min))
                link(STT(t1, t0, -0.693359375, x, ALU.mult, ALU.add))
                link(STT(t1, t0, 2.12194440e-4, t1, ALU.mult, ALU.add))
                link(TS(t2, t1, 1.0 / 5040, None, ALU.mult))
                for c in (720, 120, 24, 6, 2, 1):
                    link(STT(t2, t2, 1.0 / c, t1, ALU.add, ALU.mult))
                link(TS(t0, t0, 127.0, 8388608.0, ALU.add, ALU.mult))
                link(nc.vector.tensor_copy(expo[:, :], t0))
                link(STT(dst, t2, 1.0, expo[:, :].bitcast(F32), ALU.add, ALU.mult))

            def wide(v, n):
                return v.unsqueeze(2).to_broadcast([P, NJ, n])

            dve.wait_ge(sem("params_in"), 16)
            whole_exp(dt_, param("log_dt"), s1, s2, s3)
            link(TT(rad, lam_r, dt_, ALU.mult))
            whole_exp(rate, rad, s1, s2, s3)
            link(TT(s1, lam_i, dt_, ALU.mult))
            link(TS(s2, s1, 1.0 / (2 * math.pi), MAGIC, ALU.mult, ALU.add))
            link(TS(s2, s2, -MAGIC, None, ALU.add))
            link(STT(s1, s2, -6.28125, s1, ALU.mult, ALU.add))
            link(STT(s1, s2, -0.0019353071795864769, s1, ALU.mult, ALU.add))
            lim = 3.1415925
            link(TS(ang, s1, lim, -lim, ALU.min, ALU.max))
            link(TS(s2, s1, math.pi / 2, None, ALU.add))
            link(TS(s3, s2, math.pi, -2 * math.pi, ALU.is_gt, ALU.mult))
            link(TT(s2, s2, s3, ALU.add))
            TS(cang, s2, lim, -lim, ALU.min, ALU.max).then_inc(sem("angles"), 1)
            dve.wait_ge(sem("sincos"), 1)
            link(TT(s1, sn, sn, ALU.mult))
            link(TT(s2, cn, cn, ALU.mult))
            link(TT(s1, s1, s2, ALU.add))
            link(TS(s1, s1, -0.5, 1.5, ALU.mult, ALU.add))
            TT(er3[:, :, 0], cn, s1, ALU.mult)
            TT(ei3[:, :, 0], sn, s1, ALU.mult)
            link(TT(cn, cn, s1, ALU.mult))
            link(TT(sn, sn, s1, ALU.mult))
            m = 1
            while m < NP_:
                if m == NORM_AT:
                    dve.wait_ge(sem("x_in"), 16)
                    norm(0, param("g_mix0"))
                n = min(m, NP_ - m)
                step = NJ if n <= 64 else NJ // 2
                for j in range(0, NJ, step):
                    js = slice(j, j + step)
                    tmp = [(etmp[:, k * 1024:k * 1024 + step * n] if m >= NORM_AT
                            else g4[:, k // 2, k % 2, 0:step * n]).rearrange("p (j t) -> p j t", j=step)
                           for k in range(4)]
                    pr, pi = [e[:, js, m - 1:m].to_broadcast([P, step, n]) for e in (er3, ei3)]
                    TT(tmp[0], er3[:, js, 0:n], pr, ALU.mult)
                    TT(tmp[1], ei3[:, js, 0:n], pi, ALU.mult)
                    TT(tmp[2], er3[:, js, 0:n], pi, ALU.mult)
                    link(TT(tmp[3], ei3[:, js, 0:n], pr, ALU.mult))
                    TT(er3[:, js, m:m + n], tmp[0], tmp[1], ALU.subtract)
                    link(TT(ei3[:, js, m:m + n], tmp[2], tmp[3], ALU.add))
                m += n
            link(TT(lbr, rate, cn, ALU.mult))
            link(TT(lbi, rate, sn, ALU.mult))
            link(TT(s1, lam_r, lam_r, ALU.mult))
            link(TT(s2, lam_i, lam_i, ALU.mult))
            link(TT(s1, s1, s2, ALU.add))
            link(nc.vector.reciprocal(s1, s1))
            link(TS(s2, lbr, -1.0, None, ALU.add))
            link(TT(fr_, s2, lam_r, ALU.mult))
            link(TT(s3, lbi, lam_i, ALU.mult))
            link(TT(fr_, fr_, s3, ALU.add))
            link(TT(fr_, fr_, s1, ALU.mult))
            link(TT(fi_, lbi, lam_r, ALU.mult))
            link(TT(s3, s2, lam_i, ALU.mult))
            link(TT(fi_, fi_, s3, ALU.subtract))
            link(TT(fi_, fi_, s1, ALU.mult))
            dve.wait_ge(sem("mats_in"), 16)
            w1, w2 = [rtmp[:, k * 512:(k + 1) * 512].rearrange("p (j s) -> p j s", j=NJ) for k in range(2)]
            TT(w1, c_m[:, :, 0, :], wide(fr_, 32), ALU.mult)
            link(TT(w2, c_m[:, :, 1, :], wide(fi_, 32), ALU.mult))
            link(TT(cf4[:, :, 0, :], w1, w2, ALU.subtract))
            TT(w1, c_m[:, :, 0, :], wide(fi_, 32), ALU.mult)
            link(TT(w2, c_m[:, :, 1, :], wide(fr_, 32), ALU.mult))
            STT(cf4[:, :, 1, :], w1, -1.0, w2, ALU.mult, ALU.subtract)
            TS(csn3, c_m[:, :, 1, :], -1.0, None, ALU.mult).then_inc(sem("out_mats"), 1)

            def rope(v, heads):
                n = TC * heads * 32
                t1, t2, t3 = [rtmp[:, k * n:(k + 1) * n].rearrange("p (t h d) -> p t h d", t=TC, h=heads) for k in range(3)]
                cs, sn_ = [w.unsqueeze(2).to_broadcast([P, TC, heads, 32]) for w in (cos3, sin3)]
                lo, hi = v[:, :, :, 0:32], v[:, :, :, 32:64]
                TT(t1, lo, cs, ALU.mult)
                TT(t2, hi, sn_, ALU.mult)
                TT(t3, lo, sn_, ALU.mult)
                link(TT(hi, hi, cs, ALU.mult))
                TT(lo, t1, t2, ALU.subtract)
                return TT(hi, hi, t3, ALU.add)

            def rotate_index():
                for t in range(TC):
                    emptied(dve, ("qi", t))
                rope(z4["qi"], H).then_inc(sem("qi_ready"), 1)
                dve.wait_ge(sem("qi_ready"), 1)
                emptied(dve, "kw")
                kid4 = z3["kid"][:, :, 0:HD].unsqueeze(2)
                link(rope(kid4, 1))
                nc.vector.tensor_copy(z3["kid"][:, :, HD:2 * HD], z3["kid"][:, :, 0:HD]).then_inc(sem("kid_ready"), 1)

            for j in range(NJ):
                if j == INDEX_AT:
                    rotate_index()
                filled(dve, ("bur", j))
                br, bi = ps(("bur", j)), ps(("bui", j))
                TT(d1, er3[:, j, :], br[:, 0:NP_], ALU.mult)
                TT(d4, ei3[:, j, :], br[:, 0:NP_], ALU.mult)
                nc.vector.tensor_copy(raw[:, j, 0, :], br[:, NP_:T]).then_inc(free(("bur", j)), 1)
                filled(dve, ("bui", j))
                TT(d2, ei3[:, j, :], bi[:, 0:NP_], ALU.mult)
                TT(d3, er3[:, j, :], bi[:, 0:NP_], ALU.mult)
                nc.vector.tensor_copy(raw[:, j, 1, :], bi[:, NP_:T]).then_inc(free(("bui", j)), 1)
                emptied(dve, ("bui", j))
                TT(vr, d1, d2, ALU.add)
                link(TT(vi, d3, d4, ALU.subtract))
                if j >= 2:
                    dve.wait_ge(sem("states"), j - 1)
                r_row = rate[:, j:j + 1].to_broadcast([P, NP_])
                nc.vector.tensor_tensor_scan(g4[:, j % 2, 0, :], r_row, vr, 0.0, ALU.mult, ALU.add)
                nc.vector.tensor_tensor_scan(g4[:, j % 2, 1, :], r_row, vi, 0.0, ALU.mult, ALU.add).then_inc(sem("scanned"), 1)
                dve.wait_ge(sem("scanned"), j + 1)

            t8 = [rtmp[:, k * 128:(k + 1) * 128].rearrange("p (j b) -> p j b", j=NJ) for k in range(4)]
            h0r, h0i = [param(n).rearrange("p (j b) -> p j b", j=NJ) for n in ("h0r", "h0i")]
            for out, terms in ((0, ((lbr, h0r, None), (lbi, h0i, ALU.subtract), (fr_, raw[:, :, 0, :], ALU.add),
                                    (fi_, raw[:, :, 1, :], ALU.subtract))),
                               (1, ((lbr, h0i, None), (lbi, h0r, ALU.add), (fr_, raw[:, :, 1, :], ALU.add),
                                    (fi_, raw[:, :, 0, :], ALU.add)))):
                for n, (f, v, op) in enumerate(terms):
                    link(TT(t8[0] if n == 0 else t8[1], v, wide(f, NB), ALU.mult))
                    if n:
                        dst = hs[:, :, out, :] if n == 3 else t8[0]
                        if n == 3 and out == 1:
                            TT(dst, t8[0], t8[1], op).then_inc(sem("sample_state"), 1)
                        else:
                            link(TT(dst, t8[0], t8[1], op))

            dve.wait_ge(sem("sample_state"), 1)

            sq4 = rtmp[:, 0:TC * 512].rearrange("p (t h d) -> p t h d", t=TC, h=H)
            dve.wait_ge(sem("kid_ready"), 1)
            for n, ss in (("q", qss), ("k", kss)):
                for t in range(TC):
                    emptied(dve, (n, t))
                link(TT(sq4, z4[n], z4[n], ALU.mult))
                nc.vector.tensor_reduce(ss.rearrange("p (t h) -> p t h", t=TC), sq4, AX.X, ALU.add).then_inc(sem("qk_squares"), 1)
                dve.wait_ge(sem("qk_squares"), 1 if n == "q" else 2)
            for k, (n, ss, g) in enumerate((("q", qss, "qg"), ("k", kss, "kg"))):
                dve.wait_ge(sem("qk_roots"), k + 1)
                link(nc.vector.reciprocal(ss, ss))
                rs4 = ss.rearrange("p (t h) -> p t h", t=TC).unsqueeze(3).to_broadcast([P, TC, H, HD])
                link(TT(z4[n], z4[n], rs4, ALU.mult))
                g4_ = param(g).unsqueeze(1).to_broadcast([P, TC * H, HD])
                zz = z4[n].rearrange("p t h d -> p (t h) d")
                link(TT(zz, zz, g4_, ALU.mult))
                rope(z4[n], H).then_inc(sem("qk_ready"), 1)
                dve.wait_ge(sem("qk_ready"), k + 1)

            for t in range(TC):
                emptied(dve, ("qiT", t))
            emptied(dve, "wT")
            dve.wait_ge(sem("zeroed"), 1)
            for hh in range(2):
                half = slice(HD * hh, HD * hh + HD)
                nc.vector.tensor_copy(qib3[half, :, hh::2], qiT3[half, :, NP_:T].rearrange("p c b -> p b c"))
            TT(wbd[0:H, :].rearrange("p (b m) -> p b m", b=NB), const("d8")[0:H, :].rearrange("p (b m) -> p b m", b=NB),
               wT[0:H, 16:24].unsqueeze(1).to_broadcast([H, NB, NB]), ALU.mult).then_inc(sem("sample_index_q"), 1)
            link(nc.vector.tensor_copy(sc[0:40, 2, :], init3[0:40, 2, :]))
            for t in range(TC):
                nq, nk = QN[t], KN[t]
                for h in range(H):
                    n = H * t + h
                    emptied(dve, ("dot", t, h))
                    base = init3 if h == 0 else sc
                    STT(sc[0:nq, t, 0:nk], relu[0:nq, n % 2, 0:nk], z3["wi"][0:nq, t, h:h + 1], base[0:nq, t, 0:nk],
                        ALU.mult, ALU.add).then_inc(sem("scored"), 1)
                    dve.wait_ge(sem("scored"), n + 1)
            filled(dve, "sscore")
            TT(sc[32:40, 2, 0:SK], ps("sscore")[32:40, 0:SK], init3[32:40, 2, 0:SK], ALU.add).then_inc(free("sscore"), 1)
            emptied(dve, "sscore")
            m8 = mx8.rearrange("p (t k) -> p t k", t=TC)
            for r in range(TOPK // 8):
                for t in range(TC):
                    rows, nk = (40 if t == 2 else P), KN[t]
                    last = nc.vector.max(m8[0:rows, t, :], sc[0:rows, t, 0:nk])
                link(last)
                for t in range(TC):
                    rows, nk = (40 if t == 2 else P), KN[t]
                    last = nc.vector.match_replace(sc[0:rows, t, 0:nk], m8[0:rows, t, :], sc[0:rows, t, 0:nk], TAKEN)
                link(last)
            for t in range(TC):
                rows, nk = (40 if t == 2 else P), KN[t]
                link(TS(sc[0:rows, t, 0:nk], sc[0:rows, t, 0:nk], TAKEN, -NEG, ALU.is_equal, ALU.mult))
                link(STT(sc[0:rows, t, 0:nk], sc[0:rows, t, 0:nk], NEG, init3[0:rows, t, 0:nk], ALU.add, ALU.add))

            for c in range(4):
                filled(dve, ("y", c))
                STT(uT[:, c, :], uT[:, c, :], param("d_skip")[:, c:c + 1], ps(("y", c))[:, 0:T], ALU.mult,
                    ALU.add).then_inc(free(("y", c)), 1)
            emptied(dve, ("y", 3))
            yv = uT.rearrange("p c t -> p (c t)")
            link(TT(ga, yv, yv, ALU.mult))
            link(TS(ga, ga, 0.044715, 1.0, ALU.mult, ALU.add))
            TT(ga, ga, yv, ALU.mult).then_inc(sem("gelu_arg"), 1)
            hr_, hi_ = er3[:, :, NP_ - 1], ei3[:, :, NP_ - 1]
            TT(s1, fr_, hr_, ALU.mult)
            TT(s2, fi_, hi_, ALU.mult)
            TT(s3, fr_, hi_, ALU.mult)
            link(TT(ang, fi_, hr_, ALU.mult))
            TT(hlast[:, 0:NJ], s1, s2, ALU.subtract)
            TT(hlast[:, NJ:2 * NJ], s3, ang, ALU.add).then_inc(sem("last_state"), 1)
            dve.wait_ge(sem("gelu_tanh"), 1)
            link(STT(gb, gb, 1.0, yv, ALU.add, ALU.mult))
            TS(yv, gb, 0.5, None, ALU.mult).then_inc(sem("gelu"), 1)
            dve.wait_ge(sem("gelu"), 1)
            for c in range(4):
                emptied(dve, ("glu", c))
            link(TS(ga, ga, 0.5, 0.5, ALU.mult, ALU.add))
            TT(ycat[:, 0:4, :].rearrange("p c t -> p (c t)"), ga, yv, ALU.mult).then_inc(sem("ssm_out"), 1)
            dve.wait_ge(sem("ssm_out"), 1)
            link(nc.vector.memset(qbd, 0.0))
            emptied(dve, ("qT", 2))
            for hh in range(2):
                half = slice(HD * hh, HD * hh + HD)
                for c in range(4):
                    at = c * NB * 64 + 2 * c + hh
                    last = nc.vector.tensor_copy(qbd[half, at:at + 72 * (NB - 1) + 1:72], qT3[half, c, NP_:T])
            last.then_inc(sem("sample_q"), 1)

            for t in range(TC):
                nq, nk = QN[t], KN[t]
                for h in range(H):
                    filled(dve, ("logit", t, h))
                    nc.vector.tensor_tensor_reduce(
                        out=lg[t][0:nq, h, :], in0=ps(("logit", t, h))[0:nq, 0:nk], in1=sc[0:nq, t, 0:nk], scale=1.0,
                        scalar=-3e38, op0=ALU.add, op1=ALU.max,
                        accum_out=mx[0:nq, H * t + h:H * t + h + 1]).then_inc(free(("logit", t, h)), 1)
                emptied(dve, ("logit", t, H - 1))
                cols = slice(H * t, H * t + H)
                TS(nmax[0:nq, cols], mx[0:nq, cols], -(HD ** -0.5), None, ALU.mult).then_inc(sem("nmax"), 1)
                dve.wait_ge(sem("probs"), H * (t + 1))
                link(nc.vector.reciprocal(rinv[0:nq, cols], rsum[0:nq, cols]))
                filled(dve, ("att", t))
                TT(yn[0:nq, :].rearrange("p (h d) -> p h d", h=H), ps(("att", t))[0:nq, :].rearrange("p (h d) -> p h d", h=H),
                   rinv[0:nq, cols].unsqueeze(2).to_broadcast([nq, H, HD]), ALU.mult).then_inc(free(("att", t)), 1)

            filled(dve, "slogit")
            link(nc.vector.tensor_reduce(smx[0:64, :], ps("slogit")[0:64, 0:SK], AX.X, ALU.max))
            TS(snm[0:64, :], smx[0:64, :], -(HD ** -0.5), None, ALU.mult).then_inc(sem("sample_max"), 1)
            emptied(dve, "slogit")
            link(nc.vector.reciprocal(sri[0:64, :], srs[0:64, :]))
            link(TS(sprob[0:64, :], sprob[0:64, :], sri[0:64, :], None, ALU.mult))
            TS(dself[0:64, :], const("m24")[0:64, :], sprob[0:64, PAST:SK], None, ALU.mult).then_inc(sem("sample_probs"), 1)
            filled(dve, "satt")
            sv = ps("satt")[:, 0:64].rearrange("p (b c w) -> p c b w", b=NB, c=4)
            nc.vector.tensor_copy(ycat[0:HD, 4:8, NP_:T], sv[0:HD, :, :, 0])
            nc.vector.tensor_copy(ycat[HD:P, 4:8, NP_:T], sv[HD:P, :, :, 1]).then_inc(free("satt"), 1)

            def add_residual(name, c):
                filled(dve, (name, c))
                TT(x3[:, c, :], x3[:, c, :], ps((name, c))[:, 0:T], ALU.add).then_inc(free((name, c)), 1)

            def ff_low(n):
                f, k = n // 2, n % 2
                dve.wait_ge(sem("ff_high_ready"), n + 1)
                high, low_ = [place[:, n % FF_PLACES, half, :].rearrange("p (c m) -> p c m", c=C) for half in range(2)]
                TT(low_, unit(f"ffn{f // 2}", 256)[:, k * C:(k + 1) * C, (f % 2) * P:(f % 2) * P + P],
                   high.bitcast(F32), ALU.subtract).then_inc(sem("ff_low_ready"), 1)

            for n in range(FF_AHEAD):
                ff_low(n)
            for c in range(C):
                add_residual("wout", c)
            norm(1, param("g_ffn0"))
            for c in range(C):
                dve.wait_ge(sem("xs_high"), c + 1)
                TT(xs[:, 1, c, :], h3[:, c, :], xs[:, 0, c, :].bitcast(F32), ALU.subtract).then_inc(sem("xs_low"), 1)
            dve.wait_ge(sem("kv_out"), 16 * 2 * TC)
            for f in range(FT):
                for n in (2 * f + FF_AHEAD, 2 * f + FF_AHEAD + 1):
                    if n < FF_BLOCKS:
                        ff_low(n)
                filled(dve, ("up", f))
                emptied(dve, ("gate", f))
                TT(hff[:, f, :], ffa[:, f % 2, :], ps(("up", f))[:, 0:T], ALU.mult).then_inc(free(("up", f)), 1)
            for c in range(C):
                add_residual("down", c)

            norm(2, param("g_mix1"))
            dve.wait_ge(sem("normed"), 3 * C)
            nc.vector.tensor_copy(win_a[:, :, 0:1], h3[:, :, 0:1])
            link(TT(win_a[:, :, 1:NP_], h3[:, :, 1:NP_], h3[:, :, 0:NP_ - 1], ALU.add))
            nc.vector.tensor_copy(win_b[:, 2:8, 0:2], win_a[:, 2:8, 0:2])
            link(TT(win_b[:, 2:8, 2:NP_], win_a[:, 2:8, 2:NP_], win_a[:, 2:8, 0:NP_ - 2], ALU.add))
            nc.vector.tensor_copy(win_a[:, 4:8, 0:4], win_b[:, 4:8, 0:4])
            link(TT(win_a[:, 4:8, 4:NP_], win_b[:, 4:8, 4:NP_], win_b[:, 4:8, 0:NP_ - 4], ALU.add))
            nc.vector.tensor_copy(win_b[:, 6:8, 0:8], win_a[:, 6:8, 0:8])
            link(TT(win_b[:, 6:8, 8:NP_], win_a[:, 6:8, 8:NP_], win_a[:, 6:8, 0:NP_ - 8], ALU.add))
            dve.wait_ge(sem("hist_in"), 16)
            nc.vector.tensor_copy(ext[:, :, :, 0:15], hist)
            link(nc.vector.tensor_copy(ext[:, :, :, 15:16], h3[:, :, NP_:T].unsqueeze(3)))
            for g, w in enumerate(WINDOWS):
                cs = slice(2 * g, 2 * g + 2)
                win = (win_a, win_b)[g % 2]
                link(STT(pl[:, cs, 0:NP_], win[:, cs, :], 1.0 / w, h3[:, cs, 0:NP_], ALU.mult, ALU.subtract))
                few = const("rw")[:, g * 16:g * 16 + w - 1].unsqueeze(1).to_broadcast([P, 2, w - 1])
                link(TT(pl[:, cs, 0:w - 1], win[:, cs, 0:w - 1], few, ALU.mult))
                link(TT(pl[:, cs, 0:w - 1], pl[:, cs, 0:w - 1], h3[:, cs, 0:w - 1], ALU.subtract))
                link(nc.vector.tensor_reduce(pl[:, cs, NP_:T], ext[:, cs, :, 16 - w:16], AX.X, ALU.add))
                STT(pl[:, cs, NP_:T], pl[:, cs, NP_:T], 1.0 / w, h3[:, cs, NP_:T], ALU.mult,
                    ALU.subtract).then_inc(sem("pooled"), 1)
            for c in range(C):
                filled(dve, ("pool", c))
                STT(x3[:, c, :], ps(("pool", c))[:, 0:T], param("pool_scale")[:, c:c + 1], x3[:, c, :], ALU.mult,
                    ALU.add).then_inc(free(("pool", c)), 1)
            norm(3, param("g_ffn1"))

            link(nc.vector.memset(lgt, 0.0))
            filled(dve, "router")
            rl = ps("router")[:, 0:TC * NE].rearrange("p (t e) -> p t e", t=TC)
            nc.vector.tensor_copy(lgt[:, 0:2, :], rl[:, 0:2, :])
            nc.vector.tensor_copy(lgt[0:24, 2, :], rl[0:24, 2, :]).then_inc(free("router"), 1)
            emptied(dve, "router")
            iu = idx_u.rearrange("p (t e) -> p t e", t=TC)
            for t in range(TC):
                last = nc.vector.max(m8r[:, t, :], lgt[:, t, :])
            link(last)
            for t in range(TC):
                last = nc.vector.max_index(iu[:, t, :], m8r[:, t, :], lgt[:, t, :])
            link(last)
            TT(g12[:, 0, :], m8r[:, :, 1], m8r[:, :, 0], ALU.subtract).then_inc(sem("router_gap"), 1)
            link(nc.vector.tensor_copy(idxf, iu))
            e8 = iota[:, 0:NE].unsqueeze(1).to_broadcast([P, TC, NE])
            TT(oh1, e8, idxf[:, :, 0:1].to_broadcast([P, TC, NE]), ALU.is_equal)
            link(TT(oh2, e8, idxf[:, :, 1:2].to_broadcast([P, TC, NE]), ALU.is_equal))
            link(TT(sel, oh1, oh2, ALU.add))
            TT(sel, sel, const("valid")[:, 0:TC].unsqueeze(2).to_broadcast([P, TC, NE]), ALU.mult).then_inc(sem("picked"), 1)
            dve.wait_ge(sem("picked"), 1)
            dve.wait_ge(sem("router_exp"), 1)
            link(TS(g12[:, 2, :], g12[:, 1, :], 1.0, None, ALU.add))
            link(nc.vector.reciprocal(g12[:, 2, :], g12[:, 2, :]))
            link(TT(g12[:, 3, :], g12[:, 1, :], g12[:, 2, :], ALU.mult))
            link(TT(oh1, oh1, g12[:, 2, :].unsqueeze(2).to_broadcast([P, TC, NE]), ALU.mult))
            link(TT(oh2, oh2, g12[:, 3, :].unsqueeze(2).to_broadcast([P, TC, NE]), ALU.mult))
            link(TT(gate, oh1, oh2, ALU.add))
            filled(dve, "rank")
            rp = ps("rank")[:, 0:4 * NE].rearrange("p (t e) -> p t e", t=4)
            link(TT(slot_v, sel, rp[:, 0:TC, :], ALU.mult))
            link(TS(slot_v, slot_v, -1.0, None, ALU.add))
            ov2 = over.rearrange("p (b e) -> p b e", b=2)
            for b in range(2):
                link(TS(ov2[:, b, :], rp[:, TC, :], 128.0 * (b + 1), None, ALU.is_gt))
            nc.vector.tensor_tensor_scan(ranko, ones[:, 0:16], over, 0.0, ALU.mult, ALU.add).then_inc(free("rank"), 1)
            emptied(dve, "rank")
            for k in range(4):
                link(STT(oh[:, k, :], ranko, float(k + 1), over, ALU.is_equal, ALU.mult))
            for b in range(2):
                link(TS(cand[:, :, b, :], slot_v, -128.0 * (b + 1), None, ALU.add))
                link(nc.vector.tensor_copy(gcand[:, :, b, :], gate))
            ohb = oh.unsqueeze(1).to_broadcast([P, TC, 4, 16])
            for dst, src, first in ((pslot, cand, slot_v), (pgate, gcand, gate)):
                for t in range(TC):
                    sv_ = src[:, t, :, :].rearrange("p b e -> p (b e)").unsqueeze(1).to_broadcast([P, 4, 16])
                    link(TT(prod[:, t, :, :], sv_, oh, ALU.mult))
                link(nc.vector.tensor_reduce(dst[:, NE:PASSES, :].rearrange("p i t -> p t i"), prod, AX.X, ALU.add))
                link(nc.vector.tensor_copy(dst[:, 0:NE, :].rearrange("p e t -> p t e"), first))
            link(TT(prod[:, 0, :, :], const("ecol").unsqueeze(1).to_broadcast([P, 4, 16]), oh, ALU.mult))
            link(nc.vector.tensor_copy(pexp[:, 0:NE], iota[:, 0:NE]))
            link(nc.vector.tensor_reduce(pexp[:, NE:PASSES], prod[:, 0, :, :], AX.X, ALU.add))
            link(nc.vector.tensor_copy(exp_i[:, 0:PASSES], pexp))
            link(TS(over[:, 0:1], ranko[:, 15:16], float(NE), None, ALU.add))
            nc.vector.tensor_copy(exp_i[:, PASSES:PASSES + 1], over[:, 0:1]).then_inc(sem("passes_ready"), 1)
            for i in range(2):
                emptied(dve, ("xn", 2, i))

            dve.wait_ge(sem("passes_ready"), 1)
            n_pass = dve.value_load(exp_i[0:1, PASSES:PASSES + 1], min_val=NE, max_val=PASSES)
            with dve.Fori(0, n_pass) as i:
                nc.vector.tensor_copy(cur[:, 0:TC].unsqueeze(1), pslot[:, bass.ds(i, 1), :])
                nc.vector.tensor_copy(cur[:, TC:2 * TC].unsqueeze(1), pgate[:, bass.ds(i, 1), :]).then_inc(sem("pass_cols"), 1)
                dve.wait_ge(sem("pass_cols"), i + 1)
                for t in range(TC):
                    last = TS(pick[:, t, :], iota, cur[:, t:t + 1], None, ALU.is_equal)
                last.then_inc(sem("pick_ready"), 1)
                def low_part(n):
                    s, h = n % PLACES, n // 2
                    at = (h % PLACES) * 2 * BLOCK + (n % 2) * BLOCK
                    dve.wait_ge(sem("high_ready"), NBLK * i + n + 1)
                    TT(place[:, s, 1, :], raw_w[:, at:at + BLOCK], place[:, s, 0, :].bitcast(F32),
                       ALU.subtract).then_inc(sem("low_ready"), 1)

                def low_copy(k, name, dst, src, high):
                    dve.wait_ge(sem("high_copied"), (FC + 2) * i + k + 1)
                    TT(dst, src, high.bitcast(F32), ALU.subtract).then_inc(bank_free[PASS_BANK[name]], 1)

                def hidden_low(j):
                    low_copy(2 + j, ("hT", j), hb5[:, j % 2, 1, :, :],
                             bank[PASS_BANK[("hT", 0)]][:, :].rearrange("p (f s) -> p f s", f=4), hb5[:, j % 2, 0, :, :])

                for n in range(AHEAD):
                    low_part(n)
                for half in range(2):
                    cs = slice(4 * half, 4 * half + 4)
                    low_copy(half, ("gather", half), xg4[:, 1, cs, :],
                             bank[PASS_BANK[("gather", half)]][:, :].rearrange("p (c s) -> p c s", c=4), xg4[:, 0, cs, :])
                for n, (kind, j, q) in enumerate(PASS_BLOCKS):
                    if n + AHEAD < NBLK:
                        low_part(n + AHEAD)
                    if kind == "gate" and q == 3 and j > 0:
                        hidden_low(j - 1)
                    if kind == "up" and q == 3:
                        pass_emptied(dve, ("gate", j), i)
                        pass_filled(dve, ("up", j), i)
                        if j >= 2:
                            pass_filled(dve, ("hT", j - 2), i)
                        b = PASS_BANK[("up", j)]
                        TT(hb[:, j % 2, :], th[:, j % 2, :], bank[b][:, :], ALU.mult).then_inc(bank_free[b], 1)
                    if (kind, j, q) == ("down", FC - 2, 2):
                        hidden_low(FC - 1)
                for k in range(2 * TC):
                    t, half = k // 2, k % 2
                    n, b = TCN[t], PASS_BANK[("scatter", k)]
                    pass_filled(dve, ("scatter", k), i)
                    dst = acc[0:n, t, half * 512:(half + 1) * 512]
                    STT(dst, bank[b][0:n, :], cur[0:n, TC + t:TC + t + 1], dst, ALU.mult, ALU.add).then_inc(bank_free[b], 1)
                for k in (2 * TC - 2, 2 * TC - 1):
                    pass_emptied(dve, ("scatter", k), i)


def pack_inputs(i):
    f = np.float32

    def per_channel(v):
        return v.reshape(-1, P).T

    x = np.concatenate([i["meta_tokens"], i["x_prompt"][0], i["x_sample"][:, 0]], axis=0)
    p = np.zeros((P, PARAM_N), f)

    def put(name, v):
        at, n = PARAM_AT[name]
        p[:, at:at + n] = v.reshape(-1, n)

    for name, key in (("g_mix0", "norm_mix0"), ("g_ffn0", "norm_ffn0"), ("g_mix1", "norm_mix1"),
                      ("g_ffn1", "norm_ffn1"), ("pool_scale", "pool_scale"), ("d_skip", "ssm_d")):
        put(name, per_channel(i[key][0]))
    put("lam_re", per_channel(i["ssm_lambda_re"][0].reshape(-1)))
    put("lam_im", per_channel(i["ssm_lambda_im"][0].reshape(-1)))
    put("log_dt", per_channel(np.repeat(i["ssm_log_dt"][0], 64)))
    put("qg", i["q_norm"])
    put("kg", i["k_norm"])
    put("router", i["router_w"][0].reshape(C, P, NE).transpose(1, 0, 2))
    for name, key in (("h0r", "state_ssm_re"), ("h0i", "state_ssm_im")):
        put(name, i[key][0].reshape(NB, NJ, P).transpose(2, 1, 0))
    b = np.zeros((4, 2, 16, 4, 2, 2, 64), f)
    c = np.zeros((2, 64, NJ, 2, 2, 16), f)
    for r, (kb_, kc_) in enumerate((("ssm_b_re", "ssm_c_re"), ("ssm_b_im", "ssm_c_im"))):
        bv = i[kb_][0].reshape(4, 4, 2, 64, 16)
        cv = i[kc_][0].reshape(NJ, 2, 16, 64)
        for g in range(2):
            b[:, g, :, :, r, g, :] = bv[:, :, g].transpose(1, 3, 0, 2)
            c[g, :, :, r, g, :] = cv[:, g].transpose(2, 0, 1)
    put("b", b.reshape(P, -1))
    put("c", c.reshape(P, -1))
    return {
        "x": x.T.reshape(C, P, T).transpose(1, 0, 2).reshape(P, C * T),
        "consts": shape_constants(), "params": p,
        "w_in": i["w_in0"][0], "w_glu": i["ssm_w_glu"][0], "w_out": i["w_out0"][0],
        "w_gate": i["ffn_w_gate"][0], "w_up": i["ffn_w_up"][0], "w_down": i["ffn_w_down"][0],
        "pool_w": i["pool_w"][0].reshape(D, 256), "moe_gate": i["moe_w_gate"][0],
        "moe_up": i["moe_w_up"][0], "moe_down": i["moe_w_down"][0],
        "page_table": i["page_table"].reshape(1, 2 * NB),
        "cache_k": i["cache_k"][0].reshape(-1, P, H * HD), "cache_v": i["cache_v"][0].reshape(-1, P, H * HD),
        "cache_kidx": i["cache_kidx"][0], "state_pool": i["state_pool"][0],
        "hist": i["state_pool"][0].reshape(NB, 15, C, P).transpose(3, 2, 0, 1).reshape(P, -1),
    }


OUTS = {"y": (T, D), "k": (T, 512), "v": (T, 512), "kidx": (T, HD), "hs": (P, NJ * 2 * NB), "hl": (P, 2 * NJ),
        "pool_p": (15, D), "pool_s": (NB, 15, D)}


def kernel(**inputs):
    import concourse.bacc as bacc
    from concourse.bass_utils import run_bass_kernel_spmd

    nc = bacc.Bacc("TRN2", target_bir_lowering=False, num_devices=1)
    arrays = {k: np.ascontiguousarray(v) for k, v in pack_inputs({k: np.asarray(v) for k, v in inputs.items()}).items()}
    a = {k: nc.dram_tensor("in_" + k, v.shape, mybir.dt.from_np(v.dtype), kind="ExternalInput").ap()
         for k, v in arrays.items()}
    a["n_pool"] = arrays["cache_k"].shape[0]
    o = {k: nc.dram_tensor("out_" + k, shape, F32, kind="ExternalOutput").ap() for k, shape in OUTS.items()}
    hybrid_step(nc, a, o)
    r = run_bass_kernel_spmd(nc, [{"in_" + k: v for k, v in arrays.items()}], core_ids=[0]).results[0]
    g = {k: r["out_" + k] for k in OUTS}
    k_, v_ = [g[n].reshape(T, H, HD) for n in ("k", "v")]
    hs = g["hs"].reshape(P, NJ, 2, NB).transpose(2, 3, 1, 0).reshape(2, 1, NB, 32, 64)
    hl = g["hl"].reshape(P, 2, NJ).transpose(1, 2, 0).reshape(2, 1, 1, 32, 64)
    return (g["y"][16:NP_][None], g["y"][NP_:][:, None], k_[None, None, :NP_], v_[None, None, :NP_],
            g["kidx"][None, None, :NP_], hl[0], hl[1], g["pool_p"][None, None],
            k_[NP_:][None, :, None], v_[NP_:][None, :, None], g["kidx"][NP_:][None, :, None],
            hs[0], hs[1], g["pool_s"][None])
```
